# Optimizing a Trainium2 kernel written in Bass

```python
import jax
import jax.numpy as jnp
from jax import lax
import numpy as np
import math
import jax, jax.numpy as jnp

D_MODEL = 1024
BATCH = 1
SEQ = 512
DEPTH = 1

GRID_W = 64
CTX_LEN = 256
N_MOD = 6
EPS = 1e-6
ROPE_BASE = 10000.0
Q_BLOCK = 128
RET_CHUNK = 128

MLA_HEADS = 8
MLA_NOPE = 64
MLA_ROPE = 32
MLA_QK = MLA_NOPE + MLA_ROPE
MLA_V = 64
Q_LORA = 256
KV_LORA = 128
RET_HEADS = 4
RET_DK = 64
RET_DV = 128
MIX_WIDTH = MLA_HEADS * MLA_V + RET_HEADS * RET_DV

OFF_Q = 0
OFF_KV = OFF_Q + Q_LORA
OFF_PE = OFF_KV + KV_LORA
OFF_RQ = OFF_PE + MLA_ROPE
OFF_RK = OFF_RQ + RET_HEADS * RET_DK
OFF_RV = OFF_RK + RET_HEADS * RET_DK
OFF_RG = OFF_RV + RET_HEADS * RET_DV
D_IN = OFF_RG + RET_HEADS * RET_DV

N_EXPERTS = 32
TOP_K = 4
D_FF = D_MODEL
SWIGLU_LIMIT = 7.0
SWIGLU_ALPHA = 1.702
MOE_BLOCK = 128


def rms_norm(x, w):
    xf = x.astype(jnp.float32)
    y = xf * lax.rsqrt(jnp.mean(xf * xf, axis=-1, keepdims=True) + EPS)
    return (y * w.astype(jnp.float32)).astype(x.dtype)

def modulate(h, shift, scale):
    return h * (1 + scale) + shift

def axial_rope_tables(L, dim):
    rows = L // GRID_W
    nf = dim // 4
    inv = jnp.power(ROPE_BASE, -jnp.arange(nf, dtype=jnp.float32) / nf)
    row = jnp.repeat(jnp.arange(rows, dtype=jnp.float32), GRID_W)
    col = jnp.tile(jnp.arange(GRID_W, dtype=jnp.float32), rows)
    pos = jnp.stack([row, col], axis=-1)
    ang = pos[:, :, None] * inv
    ang = jnp.broadcast_to(ang[:, :, None, :], (L, 2, 2, nf)).reshape(L, dim)
    return jnp.cos(ang), jnp.sin(ang)

def apply_axial_rope(x, cos, sin):
    d = x.shape[-1]
    xa = x.reshape(x.shape[:-1] + (2, 2, d // 4))
    rot = jnp.stack([-xa[..., 1, :], xa[..., 0, :]], axis=-2).reshape(x.shape)
    return (x.astype(jnp.float32) * cos + rot.astype(jnp.float32) * sin).astype(x.dtype)

def merge_heads(o):
    B, H, L, dv = o.shape
    return o.transpose(0, 2, 1, 3).reshape(B, L, H * dv)

def mla_q(p, g_q_lora, w_q_up, g_q_head, rope):
    B, L, _ = p.shape
    c_q = rms_norm(p[..., OFF_Q:OFF_Q + Q_LORA], g_q_lora)
    q = (c_q @ w_q_up).reshape(B, L, MLA_HEADS, MLA_QK)
    q = rms_norm(q, g_q_head).transpose(0, 2, 1, 3)
    if rope is not None:
        q = jnp.concatenate([q[..., :MLA_NOPE], apply_axial_rope(q[..., MLA_NOPE:], *rope)], axis=-1)
    return q

def mla_kv(p, g_kv_lora, w_kv_up, g_k_head, rope):
    B, L, _ = p.shape
    c_kv = rms_norm(p[..., OFF_KV:OFF_KV + KV_LORA], g_kv_lora)
    k_pe = p[..., OFF_PE:OFF_PE + MLA_ROPE]
    kv = (c_kv @ w_kv_up).reshape(B, L, MLA_HEADS, MLA_NOPE + MLA_V)
    k_nope, v = kv[..., :MLA_NOPE], kv[..., MLA_NOPE:]
    k_pe = jnp.broadcast_to(k_pe[:, :, None, :], (B, L, MLA_HEADS, MLA_ROPE))
    k = rms_norm(jnp.concatenate([k_nope, k_pe], axis=-1), g_k_head).transpose(0, 2, 1, 3)
    if rope is not None:
        k = jnp.concatenate([k[..., :MLA_NOPE], apply_axial_rope(k[..., MLA_NOPE:], *rope)], axis=-1)
    return k, v.transpose(0, 2, 1, 3)

def attend_blocks(q, k, v):
    B, H, Lq, dq = q.shape
    nb = Lq // Q_BLOCK
    scale = dq ** -0.5
    qb = q.reshape(B, H, nb, Q_BLOCK, dq).transpose(2, 0, 1, 3, 4)

    def one_block(qi):
        s = jnp.einsum('bhqd,bhkd->bhqk', qi, k).astype(jnp.float32) * scale
        pr = jax.nn.softmax(s, axis=-1).astype(v.dtype)
        return jnp.einsum('bhqk,bhkd->bhqd', pr, v)

    o = lax.map(one_block, qb)
    return o.transpose(1, 2, 0, 3, 4).reshape(B, H, Lq, v.shape[-1])

def ret_q(p, rope):
    B, L, _ = p.shape
    q = p[..., OFF_RQ:OFF_RK].reshape(B, L, RET_HEADS, RET_DK).transpose(0, 2, 1, 3)
    return q if rope is None else apply_axial_rope(q, *rope)

def ret_kv(p, rope):
    B, L, _ = p.shape
    k = p[..., OFF_RK:OFF_RV].reshape(B, L, RET_HEADS, RET_DK).transpose(0, 2, 1, 3) * (RET_DK ** -0.5)
    v = p[..., OFF_RV:OFF_RG].reshape(B, L, RET_HEADS, RET_DV).transpose(0, 2, 1, 3)
    if rope is not None:
        k = apply_axial_rope(k, *rope)
    return k, v

def retention_state(k, v, log_gamma, reverse):
    L = k.shape[2]
    j = jnp.arange(L, dtype=jnp.float32)
    expo = j if reverse else (L - 1) - j
    w = jnp.exp(expo[None, :] * log_gamma[:, None])
    return jnp.einsum('bhld,bhle->bhde', k.astype(jnp.float32) * w[None, :, :, None],
                      v.astype(jnp.float32))

def retention_scan(q, k, v, log_gamma, s0):
    B, H, L, DK = q.shape
    DV = v.shape[-1]
    C = RET_CHUNK
    n = L // C
    to_chunks = lambda t: t.astype(jnp.float32).reshape(B, H, n, C, t.shape[-1]).transpose(2, 0, 1, 3, 4)
    i = jnp.arange(C, dtype=jnp.float32)
    diff = i[:, None] - i[None, :]
    causal = diff >= 0
    decay_mask = jnp.where(causal, jnp.exp(jnp.where(causal, diff, 0.0)[None] * log_gamma[:, None, None]), 0.0)
    q_decay = jnp.exp((i + 1.0)[None, :] * log_gamma[:, None])[..., None]
    k_decay = jnp.exp(((C - 1.0) - i)[None, :] * log_gamma[:, None])[..., None]
    chunk_decay = jnp.exp(C * log_gamma)[:, None, None]

    def step(s, inp):
        qc, kc, vc = inp
        inner = jnp.einsum('bhid,bhjd->bhij', qc, kc) * decay_mask
        o = jnp.einsum('bhij,bhje->bhie', inner, vc) + jnp.einsum('bhid,bhde->bhie', qc * q_decay, s)
        s_new = s * chunk_decay + jnp.einsum('bhjd,bhje->bhde', kc * k_decay, vc)
        return s_new, o

    _, o = lax.scan(step, s0.astype(jnp.float32), (to_chunks(q), to_chunks(k), to_chunks(v)))
    return o.transpose(1, 2, 0, 3, 4).reshape(B, H, L, DV)

def retention_bidir(q, k, v, log_gamma, s0_f, s0_b):
    flip = lambda t: jnp.flip(t, axis=2)
    o_f = retention_scan(q, k, v, log_gamma[0], s0_f)
    o_b = flip(retention_scan(flip(q), flip(k), flip(v), log_gamma[1], s0_b))
    return o_f + o_b

def ret_output(o, p, g_ret_out):
    B, H, L, DV = o.shape
    o = rms_norm(o.transpose(0, 2, 1, 3), g_ret_out.reshape(H, DV)).reshape(B, L, H * DV)
    gate = p[..., OFF_RG:D_IN].astype(jnp.float32)
    return (o * jax.nn.silu(gate)).astype(p.dtype)

def moe_ffn(h, w_router, b_router, w1, b1, w2, b2):
    T, D = h.shape
    N = T * TOP_K
    logits = (h @ w_router).astype(jnp.float32) + b_router.astype(jnp.float32)
    top_val, top_idx = lax.top_k(logits, TOP_K)
    gates = jax.nn.softmax(top_val, axis=-1)
    flat_e = top_idx.reshape(N).astype(jnp.int32)
    flat_g = gates.reshape(N)
    ar = jnp.arange(N, dtype=jnp.int32)
    flat_tok = ar // TOP_K
    order = jnp.argsort(flat_e)
    sorted_e = flat_e[order]
    counts = jax.ops.segment_sum(jnp.ones((N,), jnp.int32), flat_e, num_segments=N_EXPERTS)
    padded = ((counts + MOE_BLOCK - 1) // MOE_BLOCK) * MOE_BLOCK
    pad_end = jnp.cumsum(padded)
    pad_start = pad_end - padded
    start = jnp.cumsum(counts) - counts
    dest = pad_start[sorted_e] + (ar - start[sorted_e])
    n_blocks = -(-N // MOE_BLOCK) + N_EXPERTS
    n_pad = n_blocks * MOE_BLOCK
    buf_tok = jnp.full((n_pad,), T, jnp.int32).at[dest].set(flat_tok[order])
    buf_g = jnp.zeros((n_pad,), jnp.float32).at[dest].set(flat_g[order])
    block_e = jnp.minimum(jnp.searchsorted(pad_end, jnp.arange(n_blocks, dtype=jnp.int32) * MOE_BLOCK,
                                           side='right'), N_EXPERTS - 1).astype(jnp.int32)
    h_pad = jnp.concatenate([h, jnp.zeros((1, D), h.dtype)], axis=0)

    def expert_block(args):
        tok, g, e = args
        xb = h_pad[tok]
        u = (xb @ w1[e] + b1[e]).astype(jnp.float32)
        glu = jnp.minimum(u[:, 0::2], SWIGLU_LIMIT)
        lin = jnp.clip(u[:, 1::2], -SWIGLU_LIMIT, SWIGLU_LIMIT)
        act = glu * jax.nn.sigmoid(SWIGLU_ALPHA * glu) * (lin + 1.0)
        y = act.astype(xb.dtype) @ w2[e] + b2[e]
        return y.astype(jnp.float32) * g[:, None]

    ys = lax.map(expert_block, (buf_tok.reshape(n_blocks, MOE_BLOCK),
                                buf_g.reshape(n_blocks, MOE_BLOCK), block_e))
    out = jnp.zeros((T + 1, D), jnp.float32).at[buf_tok].add(ys.reshape(n_pad, D))[:T]
    return out.astype(h.dtype)

def first_inputs(seed: int = 0) -> dict:
    key = jax.random.key(seed)
    ks = jax.random.split(key, 24)
    f32 = jnp.float32

    def nrm(k, shape, scale):
        return jax.random.normal(k, shape, f32) * scale

    def gain(k, shape):
        return 1.0 + 0.1 * jax.random.normal(k, shape, f32)

    dec0 = jnp.log(jnp.power(2.0, 5.0 + jnp.arange(RET_HEADS, dtype=f32)) - 1.0)
    return {
        'x': nrm(ks[0], (BATCH, SEQ, D_MODEL), 1.0),
        'c': nrm(ks[1], (BATCH, D_MODEL), 1.0),
        'ctx': nrm(ks[2], (BATCH, CTX_LEN, D_MODEL), 1.0),
        'c_ctx': nrm(ks[3], (D_MODEL,), 1.0),
        'g_attn': gain(ks[4], (DEPTH, D_MODEL)),
        'g_ffn': gain(ks[5], (DEPTH, D_MODEL)),
        'w_ada': nrm(ks[6], (DEPTH, D_MODEL, N_MOD * D_MODEL), 0.5 * D_MODEL ** -0.5),
        'b_ada': nrm(ks[7], (DEPTH, N_MOD * D_MODEL), 0.02),
        'w_in': nrm(ks[8], (DEPTH, D_MODEL, D_IN), D_MODEL ** -0.5),
        'g_q_lora': gain(ks[9], (DEPTH, Q_LORA)),
        'w_q_up': nrm(ks[10], (DEPTH, Q_LORA, MLA_HEADS * MLA_QK), Q_LORA ** -0.5),
        'g_q_head': gain(ks[11], (DEPTH, MLA_QK)),
        'g_kv_lora': gain(ks[12], (DEPTH, KV_LORA)),
        'w_kv_up': nrm(ks[13], (DEPTH, KV_LORA, MLA_HEADS * (MLA_NOPE + MLA_V)), KV_LORA ** -0.5),
        'g_k_head': gain(ks[14], (DEPTH, MLA_QK)),
        'ret_decay_logit': dec0 + nrm(ks[15], (DEPTH, 2, RET_HEADS), 0.1),
        'g_ret_out': gain(ks[16], (DEPTH, RET_HEADS * RET_DV)),
        'w_out': nrm(ks[17], (DEPTH, MIX_WIDTH, D_MODEL), MIX_WIDTH ** -0.5),
        'w_router': nrm(ks[18], (DEPTH, D_MODEL, N_EXPERTS), D_MODEL ** -0.5),
        'b_router': nrm(ks[19], (DEPTH, N_EXPERTS), 0.01),
        'w_mlp1': nrm(ks[20], (DEPTH, N_EXPERTS, D_MODEL, 2 * D_FF), D_MODEL ** -0.5),
        'b_mlp1': nrm(ks[21], (DEPTH, N_EXPERTS, 2 * D_FF), 0.02),
        'w_mlp2': nrm(ks[22], (DEPTH, N_EXPERTS, D_FF, D_MODEL), D_FF ** -0.5),
        'b_mlp2': nrm(ks[23], (DEPTH, N_EXPERTS, D_MODEL), 0.02),
    }

def first_block(x, c, ctx, c_ctx, g_attn, g_ffn, w_ada, b_ada, w_in, g_q_lora, w_q_up, g_q_head,
              g_kv_lora, w_kv_up, g_k_head, ret_decay_logit, g_ret_out, w_out,
              w_router, b_router, w_mlp1, b_mlp1, w_mlp2, b_mlp2):
    B, L, D = x.shape
    Lc = ctx.shape[1]
    rope_mla = axial_rope_tables(L, MLA_ROPE)
    rope_ret = axial_rope_tables(L, RET_DK)
    for l in range(DEPTH):
        last = l == DEPTH - 1
        mod = (jax.nn.silu(c) @ w_ada[l] + b_ada[l]).reshape(B, N_MOD, 1, D)
        mod_c = (jax.nn.silu(c_ctx) @ w_ada[l] + b_ada[l]).reshape(N_MOD, 1, D)

        h = modulate(rms_norm(x, g_attn[l]), mod[:, 0], mod[:, 1])
        hc = modulate(rms_norm(ctx, g_attn[l]), mod_c[0], mod_c[1])
        p = h @ w_in[l]
        pc = hc @ w_in[l]

        k_c, v_c = mla_kv(pc, g_kv_lora[l], w_kv_up[l], g_k_head[l], None)
        k_x, v_x = mla_kv(p, g_kv_lora[l], w_kv_up[l], g_k_head[l], rope_mla)
        q_x = mla_q(p, g_q_lora[l], w_q_up[l], g_q_head[l], rope_mla)
        o_mla = attend_blocks(q_x, jnp.concatenate([k_c, k_x], axis=2), jnp.concatenate([v_c, v_x], axis=2))

        log_gamma = jax.nn.log_sigmoid(ret_decay_logit[l].astype(jnp.float32))
        kr_c, vr_c = ret_kv(pc, None)
        s0_f = retention_state(kr_c, vr_c, log_gamma[0], reverse=False)
        s0_b = retention_state(kr_c, vr_c, log_gamma[1], reverse=True)
        kr_x, vr_x = ret_kv(p, rope_ret)
        o_ret = retention_bidir(ret_q(p, rope_ret), kr_x, vr_x, log_gamma, s0_f, s0_b)

        mix = jnp.concatenate([merge_heads(o_mla), ret_output(o_ret, p, g_ret_out[l])], axis=-1)
        x = x + mod[:, 2] * (mix @ w_out[l])
        if not last:
            o_mla_c = attend_blocks(mla_q(pc, g_q_lora[l], w_q_up[l], g_q_head[l], None), k_c, v_c)
            s_zero = jnp.zeros((B, RET_HEADS, RET_DK, RET_DV), jnp.float32)
            o_ret_c = retention_bidir(ret_q(pc, None), kr_c, vr_c, log_gamma, s_zero, s_zero)
            mix_c = jnp.concatenate([merge_heads(o_mla_c), ret_output(o_ret_c, pc, g_ret_out[l])], axis=-1)
            ctx = ctx + mod_c[2] * (mix_c @ w_out[l])

        hf = modulate(rms_norm(x, g_ffn[l]), mod[:, 3], mod[:, 4]).reshape(B * L, D)
        moe_w = (w_router[l], b_router[l], w_mlp1[l], b_mlp1[l], w_mlp2[l], b_mlp2[l])
        if last:
            x = x + mod[:, 5] * moe_ffn(hf, *moe_w).reshape(B, L, D)
        else:
            hcf = modulate(rms_norm(ctx, g_ffn[l]), mod_c[3], mod_c[4]).reshape(B * Lc, D)
            y = moe_ffn(jnp.concatenate([hf, hcf], axis=0), *moe_w)
            x = x + mod[:, 5] * y[:B * L].reshape(B, L, D)
            ctx = ctx + mod_c[5] * y[B * L:].reshape(B, Lc, D)
    return x


SSD_HEADS = 16
SSD_HEAD_DIM = 64
D_SSD = SSD_HEADS * SSD_HEAD_DIM
SSD_GROUPS = 2
SSD_HEADS_PER_GROUP = SSD_HEADS // SSD_GROUPS
D_STATE = 128
CONV_W = 5
CHUNK = 128
D_XBC = D_SSD + 2 * SSD_GROUPS * D_STATE

ATTN_Q_HEADS = 16
ATTN_KV_HEADS = 4
HEAD_DIM = 64
GQA_GROUP = ATTN_Q_HEADS // ATTN_KV_HEADS
D_ATTN = ATTN_Q_HEADS * HEAD_DIM
ROPE_THETA = 10000.0

D_MIX = D_SSD + D_ATTN

OFF_Z = 0
OFF_Q_2 = OFF_Z + D_SSD
OFF_XBC = OFF_Q_2 + D_ATTN
OFF_DT = OFF_XBC + D_XBC
OFF_K = OFF_DT + 2 * SSD_HEADS
OFF_V = OFF_K + ATTN_KV_HEADS * HEAD_DIM
D_IN_PROJ = OFF_V + ATTN_KV_HEADS * HEAD_DIM

MOE_GROUPS = 4
EXPERTS_PER_GROUP = 4
N_EXPERTS_2 = MOE_GROUPS * EXPERTS_PER_GROUP
TOP_K_IN_GROUP = 2
D_EXPERT = 256


F32 = jnp.float32

def layer_norm(x, g, b, eps=1e-5):
    xf = x.astype(F32)
    mu = jnp.mean(xf, -1, keepdims=True)
    var = jnp.mean(jnp.square(xf - mu), -1, keepdims=True)
    return ((xf - mu) * lax.rsqrt(var + eps) * g + b).astype(x.dtype)

def rms_norm_2(x, g, eps=1e-6):
    xf = x.astype(F32)
    return (xf * lax.rsqrt(jnp.mean(xf * xf, -1, keepdims=True) + eps) * g).astype(x.dtype)

def dwconv_silu(u, w, b):
    y = lax.conv_general_dilated(u, w[:, None, :], (1,), [(CONV_W // 2, CONV_W // 2)],
                                 dimension_numbers=('NWC', 'WIO', 'NWC'),
                                 feature_group_count=u.shape[-1])
    return jax.nn.silu(y + b)

def axial_rope_tables_2(n_rows):
    rows = jnp.broadcast_to(jnp.arange(n_rows, dtype=F32)[:, None], (n_rows, GRID_W)).reshape(-1)
    cols = jnp.broadcast_to(jnp.arange(GRID_W, dtype=F32)[None, :], (n_rows, GRID_W)).reshape(-1)
    axis_dim = HEAD_DIM // 2
    inv_freq = jnp.power(ROPE_THETA, -jnp.arange(0, axis_dim, 2, dtype=F32) / axis_dim)
    ang = jnp.concatenate([rows[:, None] * inv_freq, cols[:, None] * inv_freq], -1)
    return jnp.cos(ang), jnp.sin(ang)

def apply_rope(x, cos, sin):
    xf = x.astype(F32).reshape(*x.shape[:-1], HEAD_DIM // 2, 2)
    x0, x1 = xf[..., 0], xf[..., 1]
    c = cos[None, :, None, :]
    s = sin[None, :, None, :]
    out = jnp.stack([x0 * c - x1 * s, x0 * s + x1 * c], -1)
    return out.reshape(x.shape).astype(x.dtype)

def ssd_scan(xs, dt, A, Bm, Cm, h0, with_output):
    b, L = xs.shape[:2]
    nc = L // CHUNK
    G, R, P, N = SSD_GROUPS, SSD_HEADS_PER_GROUP, SSD_HEAD_DIM, D_STATE
    xdt = (xs.astype(F32) * dt[..., None]).reshape(b, nc, CHUNK, G, R, P)
    a_cs = jnp.cumsum((dt * A).reshape(b, nc, CHUNK, G, R), axis=2)
    Bc = Bm.astype(F32).reshape(b, nc, CHUNK, G, N)
    w_state = jnp.exp(a_cs[:, :, -1:] - a_cs)
    chunk_states = jnp.einsum('bcsgn,bcsgr,bcsgrp->bcgrpn', Bc, w_state, xdt)
    chunk_decay = jnp.exp(a_cs[:, :, -1])

    def carry_state(h, inp):
        s_c, d_c = inp
        return h * d_c[..., None, None] + s_c, h

    h_final, h_in = lax.scan(carry_state, h0,
                             (jnp.moveaxis(chunk_states, 1, 0), jnp.moveaxis(chunk_decay, 1, 0)))
    if not with_output:
        return h_final
    Cc = Cm.astype(F32).reshape(b, nc, CHUNK, G, N)
    diff = a_cs[:, :, :, None] - a_cs[:, :, None]
    lower = jnp.tril(jnp.ones((CHUNK, CHUNK), bool))[:, :, None, None]
    decay = jnp.where(lower, jnp.exp(jnp.where(lower, diff, 0.0)), 0.0)
    cb = jnp.einsum('bcqgn,bcsgn->bcqsg', Cc, Bc)
    y_diag = jnp.einsum('bcqsgr,bcsgrp->bcqgrp', cb[..., None] * decay, xdt)
    y_off = jnp.einsum('bcqgn,bcgrpn,bcqgr->bcqgrp', Cc, jnp.moveaxis(h_in, 0, 1), jnp.exp(a_cs))
    return (y_diag + y_off).reshape(b, L, G, R, P), h_final

def ssd_bidirectional(xs, Bm, Cm, dt, A, h0_f, h0_b, with_output):
    fl = lambda u: jnp.flip(u, axis=1)
    out_f = ssd_scan(xs, dt[:, :, 0], A[0], Bm, Cm, h0_f, with_output)
    out_b = ssd_scan(fl(xs), fl(dt[:, :, 1]), A[1], fl(Bm), fl(Cm), h0_b, with_output)
    return out_f, out_b

def ssd_prepare(xbc_raw, dt_raw, p):
    b, L, _ = xbc_raw.shape
    xbc = dwconv_silu(xbc_raw, p['conv_w'], p['conv_b'])
    gn = SSD_GROUPS * D_STATE
    xs = xbc[..., :D_SSD].reshape(b, L, SSD_GROUPS, SSD_HEADS_PER_GROUP, SSD_HEAD_DIM)
    Bm = xbc[..., D_SSD:D_SSD + gn].reshape(b, L, SSD_GROUPS, D_STATE)
    Cm = xbc[..., D_SSD + gn:].reshape(b, L, SSD_GROUPS, D_STATE)
    dt = jax.nn.softplus(dt_raw.astype(F32).reshape(b, L, 2, SSD_HEADS) + p['dt_bias'].astype(F32))
    dt = dt.reshape(b, L, 2, SSD_GROUPS, SSD_HEADS_PER_GROUP)
    A = -jnp.exp(p['a_log'].astype(F32)).reshape(2, SSD_GROUPS, SSD_HEADS_PER_GROUP)
    return xs, Bm, Cm, dt, A

def ssd_output(y_f, y_b, xs, z, p):
    b, L = z.shape[:2]
    skip = p['d_skip'].astype(F32).reshape(SSD_GROUPS, SSD_HEADS_PER_GROUP)[..., None]
    y = y_f + jnp.flip(y_b, axis=1) + xs.astype(F32) * skip
    y = y.reshape(b, L, D_SSD) * jax.nn.silu(z.astype(F32))
    yg = y.reshape(b, L, SSD_GROUPS, D_SSD // SSD_GROUPS)
    yg = yg * lax.rsqrt(jnp.mean(yg * yg, -1, keepdims=True) + 1e-6)
    return (yg.reshape(b, L, D_SSD) * p['ssd_norm_g']).astype(z.dtype)

def gqa_block_attention(q, k, v):
    b, L = q.shape[:2]
    nblk = L // Q_BLOCK
    qb = q.reshape(b, nblk, Q_BLOCK, ATTN_KV_HEADS, GQA_GROUP, HEAD_DIM).swapaxes(0, 1)
    scale = HEAD_DIM ** -0.5

    def one_block(q_blk):
        s = jnp.einsum('bqhgd,bkhd->bhgqk', q_blk, k, preferred_element_type=F32) * scale
        pr = jax.nn.softmax(s, axis=-1).astype(v.dtype)
        return jnp.einsum('bhgqk,bkhd->bqhgd', pr, v)

    o = lax.map(one_block, qb)
    return o.swapaxes(0, 1).reshape(b, L, D_ATTN)

def context_mixer(hc, p, with_output):
    b, S, _ = hc.shape
    side = hc @ p['w_in'][:, OFF_XBC:]
    xbc_raw = side[..., :OFF_DT - OFF_XBC]
    dt_raw = side[..., OFF_DT - OFF_XBC:OFF_K - OFF_XBC]
    k = rms_norm_2(side[..., OFF_K - OFF_XBC:OFF_V - OFF_XBC].reshape(b, S, ATTN_KV_HEADS, HEAD_DIM), p['k_norm_g'])
    v = side[..., OFF_V - OFF_XBC:].reshape(b, S, ATTN_KV_HEADS, HEAD_DIM)
    xs, Bm, Cm, dt, A = ssd_prepare(xbc_raw, dt_raw, p)
    h0 = jnp.zeros((b, SSD_GROUPS, SSD_HEADS_PER_GROUP, SSD_HEAD_DIM, D_STATE), F32)
    if not with_output:
        hf, hb = ssd_bidirectional(xs, Bm, Cm, dt, A, h0, h0, False)
        return (k, v, hf, hb), None
    (y_f, hf), (y_b, hb) = ssd_bidirectional(xs, Bm, Cm, dt, A, h0, h0, True)
    zq = hc @ p['w_in'][:, :OFF_XBC]
    z = zq[..., OFF_Z:OFF_Q_2]
    q = rms_norm_2(zq[..., OFF_Q_2:].reshape(b, S, ATTN_Q_HEADS, HEAD_DIM), p['q_norm_g'])
    y_ssd = ssd_output(y_f, y_b, xs, z, p)
    o = gqa_block_attention(q, k, v)
    return (k, v, hf, hb), jnp.concatenate([y_ssd, o], -1) @ p['w_out']

def latent_mixer(hx, ctx_side, p, cos, sin):
    b, L, _ = hx.shape
    k_ctx, v_ctx, hf_ctx, hb_ctx = ctx_side
    proj = hx @ p['w_in']
    z = proj[..., OFF_Z:OFF_Q_2]
    q = proj[..., OFF_Q_2:OFF_XBC].reshape(b, L, ATTN_Q_HEADS, HEAD_DIM)
    xbc_raw = proj[..., OFF_XBC:OFF_DT]
    dt_raw = proj[..., OFF_DT:OFF_K]
    k = proj[..., OFF_K:OFF_V].reshape(b, L, ATTN_KV_HEADS, HEAD_DIM)
    v = proj[..., OFF_V:].reshape(b, L, ATTN_KV_HEADS, HEAD_DIM)
    xs, Bm, Cm, dt, A = ssd_prepare(xbc_raw, dt_raw, p)
    (y_f, _), (y_b, _) = ssd_bidirectional(xs, Bm, Cm, dt, A, hf_ctx, hb_ctx, True)
    y_ssd = ssd_output(y_f, y_b, xs, z, p)
    q = apply_rope(rms_norm_2(q, p['q_norm_g']), cos, sin)
    k = apply_rope(rms_norm_2(k, p['k_norm_g']), cos, sin)
    o = gqa_block_attention(q, jnp.concatenate([k_ctx, k], axis=1), jnp.concatenate([v_ctx, v], axis=1))
    return jnp.concatenate([y_ssd, o], -1) @ p['w_out']

def hier_moe(h, p):
    b, L, d = h.shape
    t = h.reshape(-1, d)
    g_prob = jax.nn.softmax((t @ p['w_rg'] + p['b_rg']).astype(F32), axis=-1)
    g_val, g_idx = lax.top_k(g_prob, 1)
    e_logits = (t @ p['w_re'] + p['b_re']).astype(F32).reshape(-1, MOE_GROUPS, EXPERTS_PER_GROUP)
    e_sel = jnp.take_along_axis(e_logits, g_idx[:, :, None], axis=1)[:, 0]
    e_val, e_idx = lax.top_k(jax.nn.softmax(e_sel, axis=-1), TOP_K_IN_GROUP)
    e_val = e_val / jnp.sum(e_val, -1, keepdims=True)
    w_group = jnp.sum(jax.nn.one_hot(e_idx, EXPERTS_PER_GROUP, dtype=F32) * e_val[..., None], axis=1)
    combine = jax.nn.one_hot(g_idx[:, 0], MOE_GROUPS, dtype=F32)[:, :, None] * g_val[:, :, None] * w_group[:, None, :]
    combine = combine.reshape(-1, N_EXPERTS_2).astype(t.dtype)
    gate = jnp.einsum('td,edf->tef', t, p['w_gate'])
    up = jnp.einsum('td,edf->tef', t, p['w_up'])
    hid = jax.nn.silu(gate) * up * combine[..., None]
    return jnp.einsum('tef,efd->td', hid, p['w_down']).reshape(b, L, d)

def second_inputs(seed: int = 0) -> dict:
    key = jax.random.key(seed)
    ks = jax.random.split(key, 28)
    nrm = lambda k, shape, scale: jax.random.normal(k, shape, F32) * scale
    beta = (8.0 * DEPTH) ** -0.25
    dt0 = jnp.exp(jax.random.uniform(ks[9], (DEPTH, 2, SSD_HEADS), F32, math.log(1e-3), math.log(1e-1)))
    dt_bias = dt0 + jnp.log(-jnp.expm1(-dt0))
    a_log = jnp.log(jax.random.uniform(ks[10], (DEPTH, 2, SSD_HEADS), F32, 1.0, 16.0))
    return {
        'x': nrm(ks[0], (BATCH, SEQ, D_MODEL), 1.0),
        'c': nrm(ks[1], (BATCH, D_MODEL), 1.0),
        'ctx': nrm(ks[2], (BATCH, CTX_LEN, D_MODEL), 1.0),
        'c_ctx': nrm(ks[3], (D_MODEL,), 1.0),
        'w_mod': nrm(ks[4], (DEPTH, D_MODEL, 6 * D_MODEL), 0.5 * D_MODEL ** -0.5),
        'b_mod': nrm(ks[5], (DEPTH, 6 * D_MODEL), 0.02),
        'w_in': nrm(ks[6], (DEPTH, D_MODEL, D_IN_PROJ), D_MODEL ** -0.5),
        'conv_w': nrm(ks[7], (DEPTH, CONV_W, D_XBC), CONV_W ** -0.5),
        'conv_b': nrm(ks[8], (DEPTH, D_XBC), 0.02),
        'dt_bias': dt_bias,
        'a_log': a_log,
        'd_skip': 1.0 + nrm(ks[11], (DEPTH, SSD_HEADS), 0.05),
        'ssd_norm_g': 1.0 + nrm(ks[12], (DEPTH, D_SSD), 0.05),
        'q_norm_g': 1.0 + nrm(ks[13], (DEPTH, HEAD_DIM), 0.05),
        'k_norm_g': 1.0 + nrm(ks[14], (DEPTH, HEAD_DIM), 0.05),
        'w_out': nrm(ks[15], (DEPTH, D_MIX, D_MODEL), beta * D_MIX ** -0.5),
        'ln1_g': 1.0 + nrm(ks[16], (DEPTH, D_MODEL), 0.05),
        'ln1_b': nrm(ks[17], (DEPTH, D_MODEL), 0.02),
        'w_rg': nrm(ks[18], (DEPTH, D_MODEL, MOE_GROUPS), D_MODEL ** -0.5),
        'b_rg': nrm(ks[19], (DEPTH, MOE_GROUPS), 0.01),
        'w_re': nrm(ks[20], (DEPTH, D_MODEL, N_EXPERTS_2), D_MODEL ** -0.5),
        'b_re': nrm(ks[21], (DEPTH, N_EXPERTS_2), 0.01),
        'w_gate': nrm(ks[22], (DEPTH, N_EXPERTS_2, D_MODEL, D_EXPERT), D_MODEL ** -0.5),
        'w_up': nrm(ks[23], (DEPTH, N_EXPERTS_2, D_MODEL, D_EXPERT), D_MODEL ** -0.5),
        'w_down': nrm(ks[24], (DEPTH, N_EXPERTS_2, D_EXPERT, D_MODEL), beta * D_EXPERT ** -0.5),
        'ln2_g': 1.0 + nrm(ks[25], (DEPTH, D_MODEL), 0.05),
        'ln2_b': nrm(ks[26], (DEPTH, D_MODEL), 0.02),
    }

def second_block(x, c, ctx, c_ctx, w_mod, b_mod, w_in, conv_w, conv_b, dt_bias, a_log, d_skip, ssd_norm_g,
              q_norm_g, k_norm_g, w_out, ln1_g, ln1_b, w_rg, b_rg, w_re, b_re, w_gate, w_up, w_down,
              ln2_g, ln2_b):
    n_rows = x.shape[1] // GRID_W
    cos, sin = axial_rope_tables_2(n_rows)
    alpha = (2.0 * DEPTH) ** 0.25
    silu_c = jax.nn.silu(c)
    silu_cc = jax.nn.silu(c_ctx)
    for l in range(DEPTH):
        last = l == DEPTH - 1
        p = {'w_in': w_in[l], 'conv_w': conv_w[l], 'conv_b': conv_b[l], 'dt_bias': dt_bias[l],
             'a_log': a_log[l], 'd_skip': d_skip[l], 'ssd_norm_g': ssd_norm_g[l], 'q_norm_g': q_norm_g[l],
             'k_norm_g': k_norm_g[l], 'w_out': w_out[l], 'w_rg': w_rg[l], 'b_rg': b_rg[l], 'w_re': w_re[l],
             'b_re': b_re[l], 'w_gate': w_gate[l], 'w_up': w_up[l], 'w_down': w_down[l]}
        sh_a, sc_a, g_a, sh_f, sc_f, g_f = [m[:, None, :] for m in jnp.split(silu_c @ w_mod[l] + b_mod[l], 6, axis=-1)]
        n_mod = 3 if last else 6
        mod_c = jnp.split(silu_cc @ w_mod[l][:, :n_mod * D_MODEL] + b_mod[l][:n_mod * D_MODEL], n_mod, axis=-1)
        hc = ctx * (1.0 + mod_c[1]) + mod_c[0]
        ctx_side, ctx_out = context_mixer(hc, p, not last)
        hx = x * (1.0 + sc_a) + sh_a
        x = layer_norm(alpha * x + g_a * latent_mixer(hx, ctx_side, p, cos, sin), ln1_g[l], ln1_b[l])
        x = layer_norm(alpha * x + g_f * hier_moe(x * (1.0 + sc_f) + sh_f, p), ln2_g[l], ln2_b[l])
        if not last:
            ctx = layer_norm(alpha * ctx + mod_c[2] * ctx_out, ln1_g[l], ln1_b[l])
            ctx = layer_norm(alpha * ctx + mod_c[5] * hier_moe(ctx * (1.0 + mod_c[4]) + mod_c[3], p),
                             ln2_g[l], ln2_b[l])
    return x


def setup_inputs(seed=0):
    out = dict(first_inputs(seed))
    for name, value in second_inputs(seed + 1).items():
        if name != "x":
            out[name + "_2"] = value
    return out


def reference(
    x, c, ctx, c_ctx, g_attn, g_ffn, w_ada, b_ada, w_in, g_q_lora, w_q_up, g_q_head, g_kv_lora,
    w_kv_up, g_k_head, ret_decay_logit, g_ret_out, w_out, w_router, b_router, w_mlp1, b_mlp1,
    w_mlp2, b_mlp2, c_2, ctx_2, c_ctx_2, w_mod_2, b_mod_2, w_in_2, conv_w_2, conv_b_2,
    dt_bias_2, a_log_2, d_skip_2, ssd_norm_g_2, q_norm_g_2, k_norm_g_2, w_out_2, ln1_g_2,
    ln1_b_2, w_rg_2, b_rg_2, w_re_2, b_re_2, w_gate_2, w_up_2, w_down_2, ln2_g_2, ln2_b_2,
):
    x = first_block(
        x, c, ctx, c_ctx, g_attn, g_ffn, w_ada, b_ada, w_in, g_q_lora, w_q_up, g_q_head,
        g_kv_lora, w_kv_up, g_k_head, ret_decay_logit, g_ret_out, w_out, w_router, b_router,
        w_mlp1, b_mlp1, w_mlp2, b_mlp2,
    )
    return second_block(
        x, c_2, ctx_2, c_ctx_2, w_mod_2, b_mod_2, w_in_2, conv_w_2, conv_b_2, dt_bias_2,
        a_log_2, d_skip_2, ssd_norm_g_2, q_norm_g_2, k_norm_g_2, w_out_2, ln1_g_2, ln1_b_2,
        w_rg_2, b_rg_2, w_re_2, b_re_2, w_gate_2, w_up_2, w_down_2, ln2_g_2, ln2_b_2,
    )


_drawn_inputs = setup_inputs


def setup_inputs(seed=0):
    import zlib

    import numpy as np

    out = dict(_drawn_inputs(seed))
    spreads = {}
    factors = {'g_q_lora': 8.0,
     'g_q_head': 7.46,
     'g_kv_lora': 5.157,
     'g_k_head': 8.0,
     'b_router': 3.604,
     'b_mlp1': 8.0,
     'b_mlp2': 8.0,
     'ctx_2': 8.0,
     'c_ctx_2': 4.855,
     'b_mod_2': 5.42,
     'conv_b_2': 37.94,
     'd_skip_2': 64.0,
     'ssd_norm_g_2': 8.0,
     'q_norm_g_2': 8.0,
     'k_norm_g_2': 8.0,
     'ln1_b_2': 2.786,
     'b_rg_2': 36.543,
     'b_re_2': 64.0,
     'ln2_b_2': 2.76}
    for name, (base, spread) in spreads.items():
        noise = np.random.default_rng([zlib.crc32(name.encode()), seed]).standard_normal(out[name].shape)
        drawn = base * np.exp(spread * noise) if base else spread * noise
        out[name] = jnp.asarray(drawn.astype(out[name].dtype))
    for name, factor in factors.items():
        out[name] = (out[name] * factor).astype(out[name].dtype)
    return out
```

```python
from collections import namedtuple
from contextlib import ExitStack, contextmanager

import numpy as np

import concourse.bass as bass
from concourse import mybir

F32 = mybir.dt.float32
I32 = mybir.dt.int32
U32 = mybir.dt.uint32
ALU = mybir.AluOpType
ACT = mybir.ActivationFunctionType
AX = mybir.AxisListType.X
ds = bass.ds

P = 128
D = 1024
DC = D // P
L = 512
LC = 256
TX = L // P
TC = LC // P
TK = TX + TC
GRID_W = 64
EPS = 1e-6
BANK = 512
SLOTS = 3
BIG = 3.0e38

H1, NOPE, ROPE, VD = 8, 64, 32, 64
QK = NOPE + ROPE
QL, KVL = 256, 128
RH, RDK, RDV = 4, 64, 128
O_KV = QL
O_PE = O_KV + KVL
O_RQ = O_PE + ROPE
O_RK = O_RQ + RH * RDK
O_RV = O_RK + RH * RDK
O_RG = O_RV + RH * RDV
DIN1 = O_RG + RH * RDV
MIX1 = H1 * VD + RH * RDV
E1, K1, FF1 = 32, 4, 1024
LIMIT, ALPHA = 7.0, 1.702

SH, SP_, SG, SN = 16, 64, 2, 128
SR = SH // SG
DS = SH * SP_
TAPS = 5
DXBC = DS + 2 * SG * SN
AH, AKV, AD = 16, 4, 64
O_Q2 = DS
O_XBC = O_Q2 + AH * AD
O_DT = O_XBC + DXBC
O_K2 = O_DT + 2 * SH
O_V2 = O_K2 + AKV * AD
DIN2 = O_V2 + AKV * AD
MIX2 = DS + AH * AD
MG, ME = 4, 4
E2, K2, FF2 = MG * ME, 2, 256
ALPHA2 = 2.0 ** 0.25


def most_blocks(tokens, top, experts):
    return (tokens * top) // P + experts


def record(**fields):
    return namedtuple("Record", list(fields))(**fields)


class Steps:

    def __init__(self, engine, semaphore):
        self.engine, self.semaphore, self.count = engine, semaphore, 0

    def __call__(self, instruction):
        self.count += 1
        instruction.then_inc(self.semaphore, 1)
        self.engine.wait_ge(self.semaphore, self.count)

    def restart(self):
        self.engine.sem_clear(self.semaphore)
        self.count = 0

    def reach(self, instruction, semaphore, value):
        instruction.then_inc(semaphore, 1)
        self.engine.wait_ge(semaphore, value)


class Ring:

    def __init__(self, slots, loaded):
        self.slots, self.loaded = slots, loaded
        self.count = [0] * SLOTS
        self.ahead = 0

    def load(self, engine, slot, source):
        _, k, n = source.shape
        engine.dma_start(self.slots[:, slot, 0:k, 0:n], source).then_inc(self.loaded[slot], 16)
        self.count[slot] += 16


class Core:

    def __init__(self, nc, stack, halves, psum, ring):
        self.nc, self.stack, self.halves, self.psum, self.ring = nc, stack, halves, psum, ring
        self.stages = 0


def core_state(nc, stack):
    free = sorted(nc.free_semaphores)
    halves = [free[-48:-24], free[-24:]]
    psum = stack.enter_context(nc.psum_tensor("psum", [P, 8, BANK], F32))
    slots = stack.enter_context(nc.sbuf_tensor("weight_slots", [P, SLOTS, DC, BANK], F32))
    loaded = [stack.enter_context(nc.semaphore(f"weights_loaded{i}")) for i in range(SLOTS)]
    return Core(nc, stack, halves, psum, Ring(slots, loaded))


@contextmanager
def stage(core, name, *signals, pool_dma=(), from_one=()):
    nc = core.nc
    mine, other = core.halves[core.stages % 2], core.halves[1 - core.stages % 2]
    first = core.stages == 0
    core.stages += 1
    assert len(signals) <= len(mine)
    with ExitStack() as stack:
        found = {s: stack.enter_context(nc.semaphore(f"{name}_{s}", num=n)) for s, n in zip(signals, mine)}
        found.update({s: core.stack.enter_context(nc.semaphore(f"{name}_{s}")) for s in pool_dma})
        block = stack.enter_context(nc.Block(no_gpsimd_drain=True))
        if not first:
            @block.sync
            def _(sync):
                sync.sem_clear(range(other[0], other[-1] + 1))
        if from_one:
            @block.sync
            def _(sync):
                for signal in from_one:
                    sync.sem_inc(found[signal], 1)
        yield block, record(**found)


@contextmanager
def buffers(core, others=None, **shapes):
    with ExitStack() as stack:
        made = dict(others or {})
        for name, shape in shapes.items():
            kind = F32
            if not isinstance(shape[-1], int):
                *shape, kind = shape
            made[name] = stack.enter_context(core.nc.sbuf_tensor(f"{name}_{core.nc.next_id()}", list(shape), kind))
        yield record(**made)


def spread(ap, axis, count):
    ap = ap.unsqueeze(axis)
    shape = list(ap.shape)
    shape[axis] = count
    return ap.to_broadcast(shape)


def by_column(vector):
    return vector.rearrange("(m p) -> p m", p=P)


def on_all(row, parts=P):
    return row.to_broadcast([parts, row.shape[1]])




def setup(core, k, args):
    nc = core.nc
    with stage(core, "setup", "filled", "selected", "rows_loaded", "zeroed") as (block, s):
        @block.sync
        def _(sync):
            sync.dma_start(k.x[:], args.x[0].rearrange("(t p) d -> p t d", p=P)).then_inc(s.rows_loaded, 16)
            sync.wait_ge(s.rows_loaded, 16)
            sync.wait_ge(s.zeroed, 1)
            for dram in (k.slot_rows1, k.slot_rows2):
                view = dram.rearrange("(p b) d -> p (b d)", p=P).rearrange("p (n d) -> p n d", d=D // 4)
                sync.dma_start(view, spread(k.zeros[:], 1, view.shape[1])).then_inc(k.slots_cleared, 16)

        @block.gpsimd
        def _(pool):
            pool.memset(k.zeros[:], 0.0).then_inc(s.zeroed, 1)
            pool.memset(k.ident[:], 0.0).then_inc(s.filled, 1)
            pool.memset(k.ones[:], 1.0).then_inc(s.filled, 1)
            pool.memset(k.eps[:], EPS).then_inc(s.filled, 1)
            pool.memset(k.one[:], 1.0).then_inc(s.filled, 1)
            pool.iota(k.numbers[:], [[1, 64]], base=0, channel_multiplier=0,
                      allow_small_or_imprecise_dtypes=True).then_inc(s.filled, 1)
            pool.wait_ge(s.filled, 5)
            pool.affine_select(out=k.ident[:], in_=k.ident[:], compare_op=ALU.not_equal, fill=1.0, base=0,
                               pattern=[[-1, P]], channel_multiplier=1).then_inc(s.selected, 1)
            pool.affine_select(out=k.upto[:], in_=k.ones[:], compare_op=ALU.is_ge, fill=0.0, base=0,
                               pattern=[[1, P]], channel_multiplier=-1).then_inc(s.selected, 1)
            pool.affine_select(out=k.after[:], in_=k.ones[:], compare_op=ALU.is_ge, fill=0.0, base=0,
                               pattern=[[-1, P]], channel_multiplier=1).then_inc(s.selected, 1)
            pool.affine_select(out=k.before[:], in_=k.ones[:], compare_op=ALU.is_gt, fill=0.0, base=0,
                               pattern=[[1, P]], channel_multiplier=-1).then_inc(s.selected, 1)
            pool.wait_ge(s.selected, 4)


def modulation(core, k, name, c, c_ctx, weights, bias, columns, rows_dram):
    nc, ring, psum = core.nc, core.ring, core.psum
    n = 6 * D
    chunks = n // BANK
    per = 2 * SLOTS
    turns = chunks // per
    w = weights.rearrange("(p k) n -> p k n", k=DC)
    with buffers(core, cin=[P, 2, DC], act=[P, 2, DC], brow=[2, n], row=[2, n]) as b, \
            stage(core, name, "c_loaded", "c_ready", "b_loaded", "summed", "added", "turned", "kept", "stored",
                  from_one=("summed", "added")) \
            as (block, s):
        @block.sync
        def _(sync):
            sync.dma_start(b.cin[:, 0], c.rearrange("o (p k) -> (o p) k", k=DC)).then_inc(s.c_loaded, 16)
            sync.dma_start(b.cin[:, 1], c_ctx.rearrange("(p k) -> p k", k=DC)).then_inc(s.c_loaded, 16)
            for j in range(SLOTS):
                ring.load(sync, j, w[:, :, j * BANK:(j + 1) * BANK])
            sync.dma_start(b.brow[:], on_all(bias.rearrange("(a n) -> a n", a=1), 2)).then_inc(s.b_loaded, 16)
            for j in range(SLOTS, 2 * SLOTS):
                sync.wait_ge(s.summed, j - SLOTS + 2)
                ring.load(sync, j % SLOTS, w[:, :, j * BANK:(j + 1) * BANK])
            with sync.Fori(1, turns) as i:
                for j in range(per):
                    sync.wait_ge(s.summed, i * per + (j - SLOTS + 2))
                    sync.dma_start(ring.slots[:, j % SLOTS], w[:, :, ds((i * per + j) * BANK, BANK)])\
                        .then_inc(ring.loaded[j % SLOTS], 16)
            sync.wait_ge(s.added, chunks + 1)
            sync.dma_start(rows_dram, b.row[:]).then_inc(s.stored, 16)
            sync.wait_ge(s.stored, 16)

        base = [x - 16 * 2 for x in ring.count]

        @block.scalar
        def _(act):
            act.wait_ge(s.c_loaded, 32)
            act.activation(b.act[:], b.cin[:], ACT.Silu).then_inc(s.c_ready, 1)

        @block.tensor
        def _(pe):
            pe.wait_ge(s.c_ready, 1)
            with pe.Fori(0, turns) as i:
                for j in range(per):
                    pe.wait_ge(ring.loaded[j % SLOTS], i * 32 + (base[j % SLOTS] + 16 * (j // SLOTS + 1)))
                    if j >= 2:
                        pe.wait_ge(s.added, i * per + j)
                    else:
                        pe.wait_ge(s.added, i * per + 1)
                    for kc in range(DC):
                        mm = pe.matmul(psum[0:2, j % 2, :], b.act[:, :, kc], ring.slots[:, j % SLOTS, kc, :],
                                       start=kc == 0, stop=kc == DC - 1)
                    mm.then_inc(s.summed, 1)
            pe.wait_ge(s.added, chunks + 1)
            for m in range(n // P):
                mm = pe.transpose(psum[:, 2, 2 * m:2 * m + 2], b.row[:, m * P:(m + 1) * P], k.ident[0:2, 0:2])
            mm.then_inc(s.turned, 1)

        @block.vector
        def _(dve):
            dve.wait_ge(s.b_loaded, 16)
            with dve.Fori(0, turns) as i:
                for j in range(per):
                    dve.wait_ge(s.summed, i * per + (j + 2))
                    at = ds((i * per + j) * BANK, BANK)
                    dve.tensor_tensor(b.row[:, at], psum[0:2, j % 2, :], b.brow[:, at], ALU.add).then_inc(s.added, 1)
            dve.wait_ge(s.turned, 1)
            dve.tensor_copy(columns[:], psum[:, 2, 0:2 * (n // P)].rearrange("p (m c) -> p m c", c=2))\
                .then_inc(s.kept, 1)
            dve.wait_ge(s.kept, 1)

        for j in range(SLOTS):
            ring.count[j] += 32 * (turns - 1)


def scale_columns(core, k, name, pairs):
    with ExitStack() as stack:
        gains = [None if p[1] is None else stack.enter_context(
            core.nc.sbuf_tensor(f"gain_{core.nc.next_id()}", [P, DC], F32)) for p in pairs]
        with stage(core, name, "gains_loaded", "vector_step") as (block, s):
            @block.sync
            def _(sync):
                for gain, p in zip(gains, pairs):
                    if gain is not None:
                        sync.dma_start(gain[:], by_column(p[1]), allow_slow_non_contiguous=True).then_inc(s.gains_loaded, 16)

            @block.vector
            def _(dve):
                step = Steps(dve, s.vector_step)
                n = sum(g is not None for g in gains)
                if n:
                    dve.wait_ge(s.gains_loaded, 16 * n)
                for gain, (out, _, column) in zip(gains, pairs):
                    if gain is None:
                        step(dve.tensor_scalar(out, column, 1.0, None, ALU.add))
                    else:
                        step(dve.scalar_tensor_tensor(out=out, in0=column, scalar=1.0, in1=gain[:], op0=ALU.add,
                                                      op1=ALU.mult))


def norm_rows(core, k, name, sources, scratch):
    n = len(sources)
    with buffers(core, sums=[P, n], roots=[P, n], rates=[P, n]) as b, \
            stage(core, name, "scalar_step", "rooted", "vector_step") as (block, s):
        @block.scalar
        def _(act):
            step = Steps(act, s.scalar_step)
            for t, (src, _) in enumerate(sources):
                step(act.activation(scratch, src, ACT.Square, accum_out=b.sums[:, t:t + 1]))
            act.activation(b.roots[:], b.sums[:], ACT.Sqrt, scale=1.0 / D, bias=k.eps[:, 0:1]).then_inc(s.rooted, 1)

        @block.vector
        def _(dve):
            step = Steps(dve, s.vector_step)
            dve.wait_ge(s.rooted, 1)
            step(dve.reciprocal(b.rates[:], b.roots[:]))
            for t, (src, out) in enumerate(sources):
                step(dve.tensor_scalar(out, src, b.rates[:, t:t + 1], None, ALU.mult))


def to_features(core, k, name, groups, prefetch=None):
    nc, psum = core.nc, core.psum
    work = [(tiles, m, out, scale, bias) for tiles, chunks, out, scale, bias in groups for m in range(chunks)]
    with stage(core, name, "turned", "kept_by_scalar", "kept_by_vector") as (block, s):
        if prefetch:
            @block.sync
            def _(sync):
                prefetch(sync)

        @block.tensor
        def _(pe):
            for w, (tiles, m, *_) in enumerate(work):
                if w >= 8:
                    pe.wait_ge(s.kept_by_vector if w % 2 else s.kept_by_scalar, (w - 8) // 2 + 1)
                for t, tile in enumerate(tiles):
                    mm = pe.transpose(psum[:, w % 8, t * P:(t + 1) * P], tile(m), k.ident[:])
                mm.then_inc(s.turned, 1)

        def keep(engine, w, vector):
            tiles, m, out, scale, bias = work[w]
            engine.wait_ge(s.turned, w + 1)
            src = psum[:, w % 8, 0:len(tiles) * P]
            if vector and bias is not None:
                ins = engine.tensor_scalar(out(m), src, scale(m), bias(m), ALU.mult, ALU.add)
            elif vector and scale is not None:
                ins = engine.tensor_scalar(out(m), src, scale(m), None, ALU.mult)
            elif vector:
                ins = engine.tensor_copy(out(m), src)
            elif scale is not None:
                ins = engine.activation(out(m), src, ACT.Identity, scale=scale(m),
                                        **({} if bias is None else {"bias": bias(m)}))
            else:
                ins = engine.copy(out(m), src)
            ins.then_inc(s.kept_by_vector if vector else s.kept_by_scalar, 1)

        @block.scalar
        def _(act):
            for w in range(0, len(work), 2):
                keep(act, w, False)
            act.wait_ge(s.kept_by_scalar, (len(work) + 1) // 2)

        @block.vector
        def _(dve):
            for w in range(1, len(work), 2):
                keep(dve, w, True)
            if len(work) > 1:
                dve.wait_ge(s.kept_by_vector, len(work) // 2)


def load_first(core, chunks):
    core.ring.ahead = min(SLOTS, len(chunks))

    def go(engine):
        for j in range(core.ring.ahead):
            core.ring.load(engine, j, chunks[j].source)
    return go


def project(core, k, name, chunks, evacuate, extra=(), vector_only=False, loads=None):
    nc, ring, psum = core.nc, core.ring, core.psum
    ahead, ring.ahead = ring.ahead, 0
    passes = [(j, p) for j, c in enumerate(chunks) for p in c.passes]
    last_group = max(p.group for _, p in passes)
    sharers = 1 if vector_only else 2
    start = list(ring.count)
    for j in range(ahead):
        start[j] -= 16
    done, n = [], 0
    for c in chunks:
        n += len(c.passes)
        done.append(n)
    finish = {p.group: i + 1 for i, (_, p) in enumerate(passes) if p.last}
    with stage(core, name, "summed", "out_by_scalar", "out_by_vector", "scalar_step", "vector_step", *extra) \
            as (block, s):
        @block.sync
        def _(sync):
            if loads:
                loads(sync, s)
            for j in range(ahead, len(chunks)):
                if j >= SLOTS:
                    sync.wait_ge(s.summed, done[j - SLOTS])
                ring.load(sync, j % SLOTS, chunks[j].source)

        @block.tensor
        def _(pe):
            for j, c in enumerate(chunks):
                pe.wait_ge(ring.loaded[j % SLOTS], start[j % SLOTS] + 16 * (j // SLOTS + 1))
                _, ks, width = c.source.shape
                for p in c.passes:
                    if p.first and p.group >= 8:
                        by_vector = vector_only or p.group % 2
                        pe.wait_ge(s.out_by_vector if by_vector else s.out_by_scalar, (p.group - 8) // sharers + 1)
                    for kc in range(ks):
                        mm = pe.matmul(psum[:, p.group % 8, 0:p.width], p.lhs(kc, ring.slots[:, j % SLOTS]),
                                       p.rhs(kc, ring.slots[:, j % SLOTS]),
                                       start=p.first and kc == 0, stop=p.last and kc == ks - 1)
                    mm.then_inc(s.summed, 1)

        def out(engine, which, finished, step):
            for group in range(0 if vector_only else which, last_group + 1, sharers):
                engine.wait_ge(s.summed, finish[group])
                step.reach(evacuate(engine, s, group, psum[:, group % 8, :], step), finished, group // sharers + 1)

        if not vector_only:
            @block.scalar
            def _(act):
                out(act, 0, s.out_by_scalar, Steps(act, s.scalar_step))

        @block.vector
        def _(dve):
            out(dve, 1, s.out_by_vector, Steps(dve, s.vector_step))


def token_chunk(source, tiles, first_group, lhs, first=True, last=True):
    width = source.shape[2]
    return record(source=source, passes=[
        record(group=first_group + i, width=width, first=first, last=last,
                        lhs=lambda kc, slot, t=t: lhs(kc, t),
                        rhs=lambda kc, slot, width=width: slot[:, kc, 0:width])
        for i, t in enumerate(tiles)])


def copy_out(engine, out, bank):
    if engine.engine == mybir.EngineType.Activation:
        return engine.copy(out, bank)
    return engine.tensor_copy(out, bank)


def rotate(step, dve, x, cos, sin, turned, sums, halves):
    for i in range(2):
        step(dve.tensor_tensor(halves(turned, i), halves(x, 1 - i), halves(sin, i), ALU.mult))
    step(dve.tensor_tensor(sums, x, cos, ALU.mult))
    step(dve.tensor_tensor(x, sums, turned, ALU.add))


def blocked_halves(width):
    q = width // 4

    def halves(view, i):
        return view.rearrange("p h (a b) -> p h a b", a=2)[:, :, :, i * q:(i + 1) * q]
    return halves


def pair_halves(view, i):
    return view.rearrange("p h (m b) -> p h m b", b=2)[:, :, :, i]


def latent_norms(core, k, px, pc):
    with buffers(core, sums=[P, TX + TK], roots=[P, TX + TK], rates=[P, TX + TK], junk=[P, QL]) as b, \
            stage(core, "latents", "scalar_step", "rooted", "vector_step") as (block, s):
        q = [px[:, t, 0:QL] for t in range(TX)]
        kv = [px[:, t, O_KV:O_PE] for t in range(TX)] + [pc[:, t, 0:KVL] for t in range(TC)]

        @block.scalar
        def _(act):
            step = Steps(act, s.scalar_step)
            for i, src in enumerate(q + kv):
                step(act.activation(b.junk[:, 0:src.shape[1]], src, ACT.Square, accum_out=b.sums[:, i:i + 1]))
            act.activation(b.roots[:, 0:TX], b.sums[:, 0:TX], ACT.Sqrt, scale=1.0 / QL,
                           bias=k.eps[:, 0:1]).then_inc(s.rooted, 1)
            act.activation(b.roots[:, TX:], b.sums[:, TX:], ACT.Sqrt, scale=1.0 / KVL,
                           bias=k.eps[:, 0:1]).then_inc(s.rooted, 1)

        @block.vector
        def _(dve):
            step = Steps(dve, s.vector_step)
            dve.wait_ge(s.rooted, 2)
            step(dve.reciprocal(b.rates[:], b.roots[:]))
            for i, src in enumerate(q + kv):
                step(dve.tensor_scalar(src, src, b.rates[:, i:i + 1], None, ALU.mult))


def head_norms(core, k, name, jobs, width, rope, loads):
    off, rw, halves = rope
    most = max(x.shape[1] for x, *_ in jobs)
    base, n = [], 0
    for x, *_ in jobs:
        base.append(n)
        n += x.shape[1]
    with buffers(core, squares=[P, 2, most * width], sums=[P, n], roots=[P, n], rates=[P, n],
                 turned=[P, most, rw], products=[P, most, rw]) as b, \
            stage(core, name, "tables_loaded", "squared", "reduced", "rooted", "vector_step") as (block, s):
        @block.sync
        def _(sync):
            for out, src in loads:
                sync.dma_start(out, src).then_inc(s.tables_loaded, 16)

        def sq(i):
            h = jobs[i][0].shape[1]
            return b.squares[:, i % 2, 0:h * width].rearrange("p (h w) -> p h w", w=width)

        @block.scalar
        def _(act):
            for i, (x, *_) in enumerate(jobs):
                if i >= 2:
                    act.wait_ge(s.reduced, i - 1)
                act.activation(sq(i), x, ACT.Square).then_inc(s.squared, 1)
            act.wait_ge(s.reduced, len(jobs))
            act.activation(b.roots[:], b.sums[:], ACT.Sqrt, scale=1.0 / width,
                           bias=k.eps[:, 0:1]).then_inc(s.rooted, 1)

        @block.vector
        def _(dve):
            step = Steps(dve, s.vector_step)
            for i, (x, *_) in enumerate(jobs):
                dve.wait_ge(s.squared, i + 1)
                dve.tensor_reduce(b.sums[:, base[i]:base[i] + x.shape[1]], sq(i), AX, ALU.add).then_inc(s.reduced, 1)
            dve.wait_ge(s.rooted, 1)
            step(dve.reciprocal(b.rates[:], b.roots[:]))
            dve.wait_ge(s.tables_loaded, 16 * len(loads))
            for i, (x, gain, table) in enumerate(jobs):
                h = x.shape[1]
                step(dve.tensor_tensor(x, x, spread(b.rates[:, base[i]:base[i] + h], 2, width), ALU.mult))
                step(dve.tensor_tensor(x, x, spread(gain, 1, h), ALU.mult))
                if table is not None:
                    cos, sin = (spread(v, 1, h) for v in table)
                    rotate(step, dve, x[:, :, off:off + rw], cos, sin, b.turned[:, 0:h], b.products[:, 0:h], halves)


def attention(core, k, name, q, kv_groups, rep, dim, keys, values, out, vdim, prefetch=None):
    nc, psum = core.nc, core.psum
    n_keys = TK * P
    turns = TX * rep
    scale = float(dim) ** -0.5
    flat = psum[:, :, :].rearrange("p b n -> p (b n)")
    scores = [flat[:, 0:n_keys], flat[:, 2 * BANK:2 * BANK + n_keys]]
    turn_ps, o_ps, q_ps = flat[:, 4 * BANK:4 * BANK + n_keys], psum[:, 6, 0:vdim], psum[:, 7, :]
    with buffers(core, q_head=[P, TX, rep * dim], k_head=[P, TK, dim], q_turned=[dim, rep, L], k_turned=[dim, n_keys],
                 probs=[P, 2, n_keys], probs_turned=[P, n_keys], peaks=[P, turns], shifts=[P, turns],
                 sums=[P, turns], shares=[P, turns]) as b, \
            stage(core, name, "staged", "k_turned", "k_kept", "q_turned", "q_kept", "scored", "shifted", "exped",
                  "p_turned", "p_kept", "weighted", "put", "vector_step", "begun",
                  from_one=("staged", "k_turned", "k_kept", "q_turned", "q_kept", "scored", "shifted", "exped", "p_turned", "p_kept", "weighted", "put")) as (block, s):
        if prefetch:
            @block.sync
            def _(sync):
                prefetch(sync)

        @block.tensor
        def _(pe):
            with pe.Fori(0, kv_groups) as g:
                pe.wait_ge(s.staged, g * 2 + 3)
                pe.wait_ge(s.p_kept, g * turns + 1)
                pe.sem_inc(s.begun, 1)
                for t in range(TK):
                    mm = pe.transpose(turn_ps[0:dim, t * P:(t + 1) * P], b.k_head[:, t, :], k.ident[:])
                mm.then_inc(s.k_turned, 1)
                for r in range(rep):
                    pe.wait_ge(s.q_kept, g * rep + r + 1)
                    pe.sem_inc(s.begun, 1)
                    for t in range(TX):
                        mm = pe.transpose(q_ps[0:dim, t * P:(t + 1) * P], b.q_head[:, t, r * dim:(r + 1) * dim],
                                          k.ident[:])
                    mm.then_inc(s.q_turned, 1)

                def score(n):
                    r, t = divmod(n, TX)
                    if n == 0:
                        pe.wait_ge(s.k_kept, g + 2)
                    pe.wait_ge(s.q_kept, g * rep + (r + 2))
                    pe.wait_ge(s.exped, g * turns + max(n - 1, 0) + 1)
                    for c in range(0, n_keys, BANK):
                        e = min(c + BANK, n_keys)
                        mm = pe.matmul(scores[n % 2][:, c:e], b.q_turned[:, r, t * P:(t + 1) * P],
                                       b.k_turned[:, c:e], start=True, stop=True)
                    mm.then_inc(s.scored, 1)

                score(0)
                for n in range(turns):
                    if n + 1 < turns:
                        score(n + 1)
                    pe.wait_ge(s.exped, g * turns + (n + 2))
                    pe.wait_ge(s.p_kept, g * turns + n + 1)
                    for t in range(TK):
                        mm = pe.transpose(turn_ps[:, t * P:(t + 1) * P], b.probs[:, n % 2, t * P:(t + 1) * P],
                                          k.ident[:])
                    mm.then_inc(s.p_turned, 1)
                    pe.wait_ge(s.p_kept, g * turns + (n + 2))
                    pe.wait_ge(s.put, g * turns + n + 1)
                    for t in range(TK):
                        mm = pe.matmul(o_ps, b.probs_turned[:, t * P:(t + 1) * P], values(t, g),
                                       start=t == 0, stop=t == TK - 1)
                    mm.then_inc(s.weighted, 1)

        @block.scalar
        def _(act):
            with act.Fori(0, kv_groups) as g:
                act.wait_ge(s.k_turned, g + 1)
                act.wait_ge(s.q_turned, g * rep + 1)
                act.copy(b.k_head[:], keys[:, :, ds(g * dim, dim)]).then_inc(s.staged, 1)
                act.copy(b.q_head[:], q[:, :, ds(g * (rep * dim), rep * dim)]).then_inc(s.staged, 1)
                act.wait_ge(s.scored, g * turns + 1)
                for r in range(rep):
                    act.wait_ge(s.q_turned, g * rep + (r + 2))
                    act.copy(b.q_turned[:, r, :], q_ps[0:dim, :]).then_inc(s.q_kept, 1)
                for n in range(turns):
                    act.wait_ge(s.shifted, g * turns + (n + 2))
                    act.wait_ge(s.p_turned, g * turns + max(n - 1, 0) + 1)
                    act.activation(b.probs[:, n % 2, :], scores[n % 2], ACT.Exp, bias=b.shifts[:, n:n + 1],
                                   scale=scale, accum_out=b.sums[:, n:n + 1]).then_inc(s.exped, 1)
            act.wait_ge(s.exped, kv_groups * turns + 1)

        @block.vector
        def _(dve):
            step = Steps(dve, s.vector_step)
            with dve.Fori(0, kv_groups) as g:
                step.restart()
                dve.wait_ge(s.k_turned, g + 2)
                dve.wait_ge(s.scored, g * turns + 1)
                dve.tensor_copy(b.k_turned[:], turn_ps[0:dim, :]).then_inc(s.k_kept, 1)

                def peak(n):
                    dve.wait_ge(s.scored, g * turns + (n + 2))
                    step(dve.tensor_reduce(b.peaks[:, n:n + 1], scores[n % 2], AX, ALU.max))
                    dve.tensor_scalar(b.shifts[:, n:n + 1], b.peaks[:, n:n + 1], -scale, None, ALU.mult)\
                        .then_inc(s.shifted, 1)

                peak(0)
                for n in range(turns):
                    if n + 1 < turns:
                        peak(n + 1)
                    dve.wait_ge(s.p_turned, g * turns + (n + 2))
                    dve.wait_ge(s.weighted, g * turns + n + 1)
                    dve.tensor_copy(b.probs_turned[:], turn_ps).then_inc(s.p_kept, 1)
                    step(dve.reciprocal(b.shares[:, n:n + 1], b.sums[:, n:n + 1]))
                    dve.wait_ge(s.weighted, g * turns + (n + 2))
                    dve.tensor_scalar(out(n % TX, g * rep + n // TX), o_ps, b.shares[:, n:n + 1], None, ALU.mult)\
                        .then_inc(s.put, 1)
            dve.wait_ge(s.put, kv_groups * turns + 1)


def retention(core, k, px, pc, mix, decay):
    nc, psum = core.nc, core.psum
    W, WC = 2 * L - P, L + P
    flat = psum[:, :, :].rearrange("p b n -> p (b n)")
    k_ps, q_ps, o_ps = flat[:, 4 * BANK:4 * BANK + TK * P], psum[:, 7, :], psum[:, 6, :]
    with ExitStack() as inner:
        b = inner.enter_context(buffers(
            core, lg_in=[P, 2 * RH], lg=[P, 2 * RH], t0=[P, 2 * RH], gap=[P, W], dist=[P, W], fwd=[P, W], bwd=[P, W],
            gap_cf=[P, WC], gap_cb=[P, WC], pw=[P, 2, W], pwc=[P, 2, WC], both=[P, W], both_c=[P, WC],
            q_head=[P, TX, RDK], k_head=[P, TK, RDK], q_turned=[RDK, L], k_turned=[RDK, TK * P], weights=[P, TK, L],
            cos=[P, TX, RDK], sin=[P, TX, RDK], turned=[P, 2 * RH, RDK], products=[P, 2 * RH, RDK]))
        with stage(core, "ret_prep", "loaded", "patterned", "logs", "vector_step", "scalar_step") as (block, s):
            @block.sync
            def _(sync):
                sync.dma_start(b.lg_in[:], on_all(decay.rearrange("a d h -> a (d h)"))).then_inc(s.loaded, 16)
                sync.dma_start(b.cos[:], k.args.cos_ret.rearrange("(t p) w -> p t w", p=P)).then_inc(s.loaded, 16)
                sync.dma_start(b.sin[:], k.args.sin_ret.rearrange("(t p) w -> p t w", p=P)).then_inc(s.loaded, 16)

            @block.gpsimd
            def _(pool):
                pool.iota(b.gap[:], [[1, W]], base=-(L - P), channel_multiplier=-1,
                          allow_small_or_imprecise_dtypes=True).then_inc(s.patterned, 1)
                pool.iota(b.gap_cf[:], [[1, WC]], base=LC - P, channel_multiplier=-1,
                          allow_small_or_imprecise_dtypes=True).then_inc(s.patterned, 1)
                pool.iota(b.gap_cb[:], [[-1, WC]], base=L + P, channel_multiplier=1,
                          allow_small_or_imprecise_dtypes=True).then_inc(s.patterned, 1)

            @block.scalar
            def _(act):
                step = Steps(act, s.scalar_step)
                act.wait_ge(s.loaded, 48)
                step(act.activation(b.t0[:], b.lg_in[:], ACT.Abs))
                step(act.activation(b.t0[:], b.t0[:], ACT.Exp, scale=-1.0))
                act.activation(b.t0[:], b.t0[:], ACT.Ln, bias=k.one[:, 0:1]).then_inc(s.logs, 1)

            @block.vector
            def _(dve):
                step = Steps(dve, s.vector_step)
                dve.wait_ge(s.patterned, 3)
                step(dve.scalar_tensor_tensor(out=b.dist[:], in0=b.gap[:], scalar=-1.0, in1=b.gap[:], op0=ALU.mult,
                                              op1=ALU.max))
                step(dve.tensor_scalar(b.fwd[:], b.gap[:], 0.0, None, ALU.is_ge))
                step(dve.tensor_scalar(b.bwd[:], b.gap[:], 0.0, None, ALU.is_le))
                dve.wait_ge(s.logs, 1)
                step(dve.scalar_tensor_tensor(out=b.lg[:], in0=b.lg_in[:], scalar=0.0, in1=b.t0[:], op0=ALU.min,
                                              op1=ALU.subtract))
                halves = blocked_halves(RDK)
                for t in range(TX):
                    x = px[:, t, O_RQ:O_RV].rearrange("p (h w) -> p h w", w=RDK)
                    cos, sin = spread(b.cos[:, t], 1, 2 * RH), spread(b.sin[:, t], 1, 2 * RH)
                    rotate(step, dve, x, cos, sin, b.turned[:], b.products[:], halves)

        rk_c = O_PE + ROPE - O_KV
        with stage(core, "retention", "staged", "powered", "mixed", "k_turned", "k_kept", "q_turned", "q_kept",
                   "scored", "weighed", "summed", "put", "vector_step", "begun",
                  from_one=("staged", "powered", "mixed", "k_turned", "k_kept", "q_turned", "q_kept", "scored", "weighed", "summed", "put")) as (block, s):
            @block.scalar
            def _(act):
                with act.Fori(0, RH) as h:
                    act.wait_ge(s.k_turned, h + 1)
                    act.wait_ge(s.q_turned, h + 1)
                    act.copy(b.k_head[:, 0:TX], px[:, :, ds(h * RDK + O_RK, RDK)]).then_inc(s.staged, 1)
                    act.copy(b.k_head[:, TX:], pc[:, :, ds(h * RDK + rk_c, RDK)]).then_inc(s.staged, 1)
                    act.copy(b.q_head[:], px[:, :, ds(h * RDK + O_RQ, RDK)]).then_inc(s.staged, 1)
                    act.wait_ge(s.mixed, h + 1)
                    for d in range(2):
                        lg = b.lg[:, ds(h + d * RH, 1)]
                        act.activation(b.pw[:, d], b.dist[:], ACT.Exp, scale=lg).then_inc(s.powered, 1)
                        act.activation(b.pwc[:, d], b.gap_cb[:] if d else b.gap_cf[:], ACT.Exp, scale=lg)\
                            .then_inc(s.powered, 1)
                    act.wait_ge(s.scored, h * TK + 1)
                    act.wait_ge(s.q_turned, h + 2)
                    act.copy(b.q_turned[:], q_ps[0:RDK, :]).then_inc(s.q_kept, 1)
                    act.wait_ge(s.summed, h + 2)
                    act.copy(mix[:, :, ds(h * RDV + H1 * VD, RDV)], o_ps.rearrange("p (t w) -> p t w", t=TX))\
                        .then_inc(s.put, 1)
                act.wait_ge(s.put, RH + 1)

            @block.tensor
            def _(pe):
                with pe.Fori(0, RH) as h:
                    pe.wait_ge(s.staged, h * 3 + 4)
                    pe.wait_ge(s.k_kept, h + 1)
                    pe.sem_inc(s.begun, 1)
                    for t in range(TK):
                        mm = pe.transpose(k_ps[0:RDK, t * P:(t + 1) * P], b.k_head[:, t, :], k.ident[:])
                    mm.then_inc(s.k_turned, 1)
                    pe.wait_ge(s.q_kept, h + 1)
                    pe.sem_inc(s.begun, 1)
                    for t in range(TX):
                        mm = pe.transpose(q_ps[0:RDK, t * P:(t + 1) * P], b.q_head[:, t, :], k.ident[:])
                    mm.then_inc(s.q_turned, 1)
                    pe.wait_ge(s.k_kept, h + 2)
                    pe.wait_ge(s.q_kept, h + 2)
                    for t in range(TK):
                        pe.wait_ge(s.weighed, h * TK + max(t - 1, 0) + 1)
                        pe.matmul(psum[:, t % 2, :], b.k_turned[:, t * P:(t + 1) * P], b.q_turned[:],
                                  start=True, stop=True).then_inc(s.scored, 1)
                    pe.wait_ge(s.weighed, h * TK + TK + 1)
                    pe.wait_ge(s.put, h + 1)
                    for t in range(TX):
                        for j in range(TK):
                            src = px[:, j, ds(h * RDV + O_RV, RDV)] if j < TX else \
                                pc[:, j - TX, ds(h * RDV + rk_c + RH * RDK, RDV)]
                            mm = pe.matmul(o_ps[:, t * P:(t + 1) * P], b.weights[:, j, t * P:(t + 1) * P], src,
                                           start=j == 0, stop=j == TK - 1)
                    mm.then_inc(s.summed, 1)

            @block.vector
            def _(dve):
                step = Steps(dve, s.vector_step)
                with dve.Fori(0, RH) as h:
                    step.restart()
                    dve.wait_ge(s.powered, h * 4 + 5)
                    step(dve.tensor_tensor(b.pw[:, 0], b.pw[:, 0], b.fwd[:], ALU.mult))
                    step(dve.tensor_tensor(b.pw[:, 1], b.pw[:, 1], b.bwd[:], ALU.mult))
                    step(dve.tensor_tensor(b.both[:], b.pw[:, 0], b.pw[:, 1], ALU.add))
                    step.reach(dve.tensor_tensor(b.both_c[:], b.pwc[:, 0], b.pwc[:, 1], ALU.add), s.mixed, h + 2)
                    dve.wait_ge(s.k_turned, h + 2)
                    dve.wait_ge(s.scored, h * TK + 1)
                    dve.tensor_copy(b.k_turned[:], k_ps[0:RDK, :]).then_inc(s.k_kept, 1)
                    dve.wait_ge(s.summed, h + 1)
                    for t in range(TK):
                        dve.wait_ge(s.scored, h * TK + (t + 2))
                        m = b.both[:, L - P - t * P:2 * L - P - t * P] if t < TX else \
                            b.both_c[:, P - (t - TX) * P:P - (t - TX) * P + L]
                        dve.scalar_tensor_tensor(out=b.weights[:, t], in0=psum[:, t % 2, :], scalar=RDK ** -0.5,
                                                 in1=m, op0=ALU.mult, op1=ALU.mult).then_inc(s.weighed, 1)
                dve.wait_ge(s.weighed, RH * TK + 1)

    with buffers(core, squares=[P, TX, RH * RDV], sums=[P, TX * RH], roots=[P, TX * RH], rates=[P, TX * RH],
                 gain=[P, RH * RDV], gate=[P, TX, RH * RDV]) as b, \
            stage(core, "ret_out", "loaded", "squared", "reduced", "rooted", "gated", "vector_step") as (block, s):
        o = mix[:, :, H1 * VD:]
        by_head = [v.rearrange("p t (h w) -> p t h w", w=RDV) for v in (o, b.squares[:])]
        sums, rates = (v[:].rearrange("p (t h) -> p t h", t=TX) for v in (b.sums, b.rates))

        @block.sync
        def _(sync):
            sync.dma_start(b.gain[:], on_all(k.args.g_ret_out)).then_inc(s.loaded, 16)

        @block.scalar
        def _(act):
            act.activation(b.squares[:], o, ACT.Square).then_inc(s.squared, 1)
            act.activation(b.gate[:], px[:, :, O_RG:], ACT.Silu).then_inc(s.gated, 1)
            act.wait_ge(s.reduced, 1)
            act.activation(b.roots[:], b.sums[:], ACT.Sqrt, scale=1.0 / RDV, bias=k.eps[:, 0:1]).then_inc(s.rooted, 1)

        @block.vector
        def _(dve):
            step = Steps(dve, s.vector_step)
            dve.wait_ge(s.squared, 1)
            dve.tensor_reduce(sums, by_head[1], AX, ALU.add).then_inc(s.reduced, 1)
            dve.wait_ge(s.rooted, 1)
            step(dve.reciprocal(b.rates[:], b.roots[:]))
            step(dve.tensor_tensor(by_head[0], by_head[0], spread(rates, 3, RDV), ALU.mult))
            dve.wait_ge(s.loaded, 16)
            step(dve.tensor_tensor(o, o, spread(b.gain[:], 1, TX), ALU.mult))
            dve.wait_ge(s.gated, 1)
            step(dve.tensor_tensor(o, o, b.gate[:], ALU.mult))


def first_mixer(core, k, args):
    nc = core.nc
    w_in = args.w_in[0].rearrange("(k p) n -> p k n", p=P)
    with buffers(core, mix=[P, TX, MIX1], px=[P, TX, DIN1], pc=[P, TC, O_PE + ROPE - O_KV + O_RG - O_RK]) as m:
        with buffers(core, turned=[P, DC, TK * P]) as h:
            with buffers(core, ctx=[P, TC, D], xn=[P, TX, D], junk=[P, D]) as b:
                with stage(core, "load_ctx", "loaded") as (block, s):
                    @block.sync
                    def _(sync):
                        sync.dma_start(b.ctx[:], args.ctx[0].rearrange("(t p) d -> p t d", p=P)).then_inc(s.loaded, 16)
                        sync.wait_ge(s.loaded, 16)
                norm_rows(core, k, "norm1", [(k.x[:, t], b.xn[:, t]) for t in range(TX)] +
                          [(b.ctx[:, t], b.ctx[:, t]) for t in range(TC)], b.junk[:])
                cols = [(0, QL, False), (O_KV, O_PE + ROPE, True), (O_RQ, O_RK, False),
                        (O_RK, O_RK + BANK, True), (O_RK + BANK, O_RG, True), (O_RG, DIN1, False)]
                chunks, outs, g = [], [], 0
                for lo, hi, ctx_too in cols:
                    tiles = range(TK if ctx_too else TX)
                    chunks.append(token_chunk(w_in[:, :, lo:hi], tiles, g,
                                              lambda kc, t: h.turned[:, kc, t * P:(t + 1) * P]))
                    at = lo - O_KV if lo < O_RQ else lo - O_KV - RH * RDK
                    outs += [m.px[:, t, lo:hi] if t < TX else m.pc[:, t - TX, at:at + hi - lo] for t in tiles]
                    g += len(tiles)
                to_features(core, k, "turn1", [
                    ([lambda i, t=t: b.xn[:, t, i * P:(i + 1) * P] for t in range(TX)], DC,
                     lambda i: h.turned[:, i, 0:L], lambda i: k.scale1[:, i:i + 1],
                     lambda i: k.cols1[:, i, 0:1]),
                    ([lambda i, t=t: b.ctx[:, t, i * P:(i + 1) * P] for t in range(TC)], DC,
                     lambda i: h.turned[:, i, L:L + LC], lambda i: k.scale1c[:, i:i + 1],
                     lambda i: k.cols1[:, i, 1:2])], prefetch=load_first(core, chunks))
            project(core, k, "in1", chunks,
                    lambda e, s, g, bank, step: copy_out(e, outs[g], bank[:, 0:outs[g].shape[1]]))
        retention(core, k, m.px[:], m.pc[:], m.mix[:], args.ret_decay_logit)
        with buffers(core, q=[P, TX, H1 * QK], kv=[P, TK, H1 * (NOPE + VD)], keys=[P, TK, H1 * QK]) as a:
            with buffers(core, cq=[P, QL // P, L], ckv=[P, 1, TK * P], gq=[P, 2], gkv=[P, 1]) as b:
                latent_norms(core, k, m.px[:], m.pc[:])
                with stage(core, "lora_gain", "loaded") as (block, s):
                    @block.sync
                    def _(sync):
                        sync.dma_start(b.gq[:], by_column(args.g_q_lora[0]), allow_slow_non_contiguous=True)\
                            .then_inc(s.loaded, 16)
                        sync.dma_start(b.gkv[:], by_column(args.g_kv_lora[0]), allow_slow_non_contiguous=True)\
                            .then_inc(s.loaded, 16)
                        sync.wait_ge(s.loaded, 32)
                wq = args.w_q_up[0].rearrange("(k p) n -> p k n", p=P)
                wkv = args.w_kv_up[0].rearrange("(k p) n -> p k n", p=P)
                chunks, outs, g = [], [], 0
                for w, lo, hi, src, tiles, out in (
                        (wq, 0, BANK, b.cq, TX, a.q), (wq, BANK, H1 * QK, b.cq, TX, a.q),
                        (wkv, 0, BANK, b.ckv, TK, a.kv), (wkv, BANK, 2 * BANK, b.ckv, TK, a.kv)):
                    chunks.append(token_chunk(w[:, :, lo:hi], range(tiles), g,
                                              lambda kc, t, src=src: src[:, kc, t * P:(t + 1) * P]))
                    outs += [out[:, t, lo:hi] for t in range(tiles)]
                    g += tiles
                to_features(core, k, "turn_latents", [
                    ([lambda i, t=t: m.px[:, t, i * P:(i + 1) * P] for t in range(TX)], QL // P,
                     lambda i: b.cq[:, i, :], lambda i: b.gq[:, i:i + 1], None),
                    ([lambda i, t=t: m.px[:, t, O_KV:O_PE] for t in range(TX)], 1,
                     lambda i: b.ckv[:, 0, 0:L], lambda i: b.gkv[:, 0:1], None),
                    ([lambda i, t=t: m.pc[:, t, 0:KVL] for t in range(TC)], 1,
                     lambda i: b.ckv[:, 0, L:], lambda i: b.gkv[:, 0:1], None)],
                    prefetch=load_first(core, chunks))
                project(core, k, "up1", chunks,
                        lambda e, s, g, bank, step: copy_out(e, outs[g], bank[:, 0:outs[g].shape[1]]))
            with stage(core, "join_keys", "joined") as (block, s):
                @block.gpsimd
                def _(pool):
                    for t in range(TK):
                        pe_src = m.px[:, t, O_PE:O_RQ] if t < TX else m.pc[:, t - TX, KVL:KVL + ROPE]
                        pool.tensor_copy(a.keys[:, t].rearrange("p (h w) -> p h w", w=QK)[:, :, NOPE:],
                                         spread(pe_src, 1, H1)).then_inc(s.joined, 1)
                    pool.wait_ge(s.joined, TK)

                @block.scalar
                def _(act):
                    for t in range(TK):
                        act.copy(a.keys[:, t].rearrange("p (h w) -> p h w", w=QK)[:, :, 0:NOPE],
                                 a.kv[:, t].rearrange("p (h w) -> p h w", w=NOPE + VD)[:, :, 0:NOPE])
            with buffers(core, cos=[P, TX, ROPE], sin=[P, TX, ROPE], gq=[P, QK], gk=[P, QK]) as b:
                table = [(b.cos[:, t], b.sin[:, t]) for t in range(TX)] + [None] * TC
                view = lambda x, t: x[:, t].rearrange("p (h w) -> p h w", w=QK)
                head_norms(core, k, "heads1",
                           [(view(a.q, t), b.gq[:], table[t]) for t in range(TX)] +
                           [(view(a.keys, t), b.gk[:], table[t]) for t in range(TK)],
                           QK, (NOPE, ROPE, blocked_halves(ROPE)),
                           [(b.cos[:], k.args.cos_mla.rearrange("(t p) w -> p t w", p=P)),
                            (b.sin[:], k.args.sin_mla.rearrange("(t p) w -> p t w", p=P)),
                            (b.gq[:], on_all(args.g_q_head)), (b.gk[:], on_all(args.g_k_head))])
            attention(core, k, "attn1", a.q[:], H1, 1, QK, a.keys[:],
                      lambda t, g: a.kv[:, t, ds(g * (NOPE + VD) + NOPE, VD)],
                      lambda t, h: m.mix[:, t, ds(h * VD, VD)], VD)
        project_out(core, k, "out1", lambda t, i: m.mix[:, t, i * P:(i + 1) * P], MIX1, args.w_out[0], k.rows1, 1.0)


def project_out(core, k, name, mix, width, w_out, rows, alpha):
    kc = width // P
    parts = kc // DC
    w = w_out.rearrange("(q k p) n -> p q k n", p=P, k=DC)
    with buffers(core, turned=[P, kc, L], gate=[P, D], prod=[P, BANK]) as b:
        chunks = []
        for n in range(2):
            for q in range(parts):
                chunks.append(token_chunk(w[:, q, :, n * BANK:(n + 1) * BANK], range(TX), n * TX,
                                          lambda i, t, q=q: b.turned[:, q * DC + i, t * P:(t + 1) * P],
                                          first=q == 0, last=q == parts - 1))
        to_features(core, k, name + "_turn", [
            ([lambda i, t=t: mix(t, i) for t in range(TX)], kc,
             lambda i: b.turned[:, i, :], None, None)], prefetch=load_first(core, chunks))

        def add(dve, s, g, bank, step):
            n, t = divmod(g, TX)
            cols = slice(n * BANK, (n + 1) * BANK)
            if g == 0:
                dve.wait_ge(s.gate_loaded, 16)
            step(dve.tensor_tensor(b.prod[:], bank, b.gate[:, cols], ALU.mult))
            return dve.scalar_tensor_tensor(out=k.x[:, t, cols], in0=k.x[:, t, cols], scalar=alpha, in1=b.prod[:],
                                            op0=ALU.mult, op1=ALU.add)

        project(core, k, name, chunks, add, extra=("gate_loaded",), vector_only=True,
                loads=lambda sync, s: sync.dma_start(b.gate[:], on_all(rows[0:1, 2 * D:3 * D]))
                .then_inc(s.gate_loaded, 16))




def places(core, k, name, r, oneh, mask, experts, top, n_blocks):
    nc, psum = core.nc, core.psum
    with buffers(core, pos=[P, TX, experts], full=[experts, 4], wide=[experts, P], count=[experts, 1],
                 ends=[experts, 1], passed=[experts, n_blocks], prod=[P, TX, experts], dest=[P, TX, top],
                 zeros=[P, n_blocks + 1, I32], ids=[P, TX, I32]) as b, \
            stage(core, name, "counted", "rounded", "summed", "compared", "listed", "placed", "ids_made", "cleared",
                  "vector_step", pool_dma=("scattered",)) as (block, s):
        ps_pos, ps_count, ps_start, ps_end, ps_total, ps_blocks = (psum[:, i, :] for i in range(6))

        @block.tensor
        def _(pe):
            for t in range(TX):
                for u in range(t + 1):
                    pe.matmul(ps_pos[:, t * experts:(t + 1) * experts], k.before[:] if u == t else k.ones[:],
                              mask[:, u, :], start=u == 0, stop=u == t)
            for t in range(TX):
                mm = pe.matmul(ps_count[0:experts, 0:1], mask[:, t, :], k.ones[:, 0:1], start=t == 0, stop=t == TX - 1)
            mm.then_inc(s.counted, 1)
            pe.wait_ge(s.rounded, 2)
            pe.matmul(ps_start[:, 0:experts], b.wide[:], k.before[0:experts, 0:experts], start=True, stop=True)
            pe.matmul(ps_end[0:experts, 0:1], k.upto[0:experts, 0:experts], b.count[:], start=True, stop=True)
            pe.matmul(ps_total[0:1, 0:1], b.count[:], k.ones[0:experts, 0:1], start=True, stop=True)\
                .then_inc(s.summed, 1)
            pe.wait_ge(s.compared, 1)
            pe.matmul(ps_blocks[0:1, 0:n_blocks], k.ones[0:experts, 0:1], b.passed[:], start=True, stop=True)\
                .then_inc(s.listed, 1)

        @block.vector
        def _(dve):
            step = Steps(dve, s.vector_step)
            step(dve.memset(b.zeros[:], 0))
            dve.engine_nop().then_inc(s.cleared, 1)
            dve.wait_ge(s.counted, 1)
            step(dve.tensor_copy(b.pos[:], ps_pos[:, 0:TX * experts].rearrange("p (t e) -> p t e", t=TX)))
            for i in range(4):
                step(dve.tensor_scalar(b.full[:, i:i + 1], ps_count[0:experts, 0:1], float(P * i), None, ALU.is_gt))
            dve.tensor_reduce(b.count[:], b.full[:], AX, ALU.add).then_inc(s.rounded, 1)
            dve.wait_ge(s.rounded, 1)
            dve.tensor_scalar(b.wide[:], k.ones[0:experts, :], b.count[:, 0:1], None, ALU.mult).then_inc(s.rounded, 1)
            dve.wait_ge(s.summed, 1)
            step(dve.tensor_copy(b.ends[:], ps_end[0:experts, 0:1]))
            dve.tensor_scalar(b.passed[:], k.numbers[0:experts, 0:n_blocks], b.ends[:, 0:1], None, ALU.is_ge)\
                .then_inc(s.compared, 1)
            step(dve.tensor_copy(r.blocks[0:1, n_blocks:n_blocks + 1], ps_total[0:1, 0:1]))
            for t in range(TX):
                step(dve.scalar_tensor_tensor(out=b.pos[:, t], in0=ps_start[:, 0:experts], scalar=float(P),
                                              in1=b.pos[:, t], op0=ALU.mult, op1=ALU.add))
            for j in range(top):
                step(dve.tensor_tensor(b.prod[:], oneh[:, j], b.pos[:], ALU.mult))
                step(dve.tensor_reduce(b.dest[:, :, j], b.prod[:], AX, ALU.add))
            dve.tensor_copy(r.dest[:], b.dest[:].rearrange("p t j -> p (t j)")).then_inc(s.placed, 1)
            dve.wait_ge(s.listed, 1)
            step(dve.tensor_scalar(r.blocks[0:1, 0:n_blocks], ps_blocks[0:1, 0:n_blocks], float(experts - 1), None,
                                   ALU.min))

        @block.gpsimd
        def _(pool):
            pool.iota(b.ids[:], [[P, TX]], base=0, channel_multiplier=1).then_inc(s.ids_made, 1)
            pool.wait_ge(s.ids_made, 1)
            pool.wait_ge(s.cleared, 1)
            pool.dma_start(r.slot_token.rearrange("(p b) o -> p (b o)", p=P), b.zeros[:]).then_inc(s.scattered, 16)
            pool.wait_ge(s.scattered, 16)
            pool.wait_ge(s.placed, 1)
            for t in range(TX):
                for j in range(top):
                    i = t * top + j
                    pool.indirect_dma_start(r.slot_token, bass.IndirectOffsetOnAxis(ap=r.dest[:, i:i + 1], axis=0),
                                            b.ids[:, t:t + 1], None).then_inc(s.scattered, 16)
            pool.wait_ge(s.scattered, 16 * (1 + TX * top))


def logits_of(core, k, name, turned, r, weights, biases, width):
    psum = core.psum
    with buffers(core, w=[P, DC, width], bias=[P, width]) as b, \
            stage(core, name, "loaded", "summed", "vector_step", "stored") as (block, s):
        @block.sync
        def _(sync):
            at = 0
            for w, bias in zip(weights, biases):
                n = w.shape[1]
                sync.dma_start(b.w[:, :, at:at + n], w.rearrange("(k p) n -> p k n", p=P)).then_inc(s.loaded, 16)
                sync.dma_start(b.bias[:, at:at + n], on_all(bias)).then_inc(s.loaded, 16)
                at += n

        @block.tensor
        def _(pe):
            pe.wait_ge(s.loaded, 32 * len(weights))
            for t in range(TX):
                for kc in range(DC):
                    mm = pe.matmul(psum[:, 0, t * width:(t + 1) * width], turned[:, kc, t * P:(t + 1) * P],
                                   b.w[:, kc, :], start=kc == 0, stop=kc == DC - 1)
            mm.then_inc(s.summed, 1)

        @block.vector
        def _(dve):
            step = Steps(dve, s.vector_step)
            dve.wait_ge(s.summed, 1)
            dve.wait_ge(s.loaded, 32 * len(weights))
            step(dve.tensor_tensor(r.logits[:], psum[:, 0, 0:TX * width].rearrange("p (t e) -> p t e", t=TX),
                                   spread(b.bias[:], 1, TX), ALU.add))


def choose_first(core, k, r, oneh, mask):
    with buffers(core, top=[P, TX, 8], index=[P, TX, 8, U32], indexf=[P, TX, 8], less=[P, TX, K1], sums=[P, TX],
                 e=[P, TX, K1]) as b, \
            stage(core, "choose1", "shifted", "exped", "vector_step") as (block, s):
        @block.scalar
        def _(act):
            act.wait_ge(s.shifted, 1)
            act.activation(b.e[:], b.less[:], ACT.Exp).then_inc(s.exped, 1)

        @block.vector
        def _(dve):
            step = Steps(dve, s.vector_step)
            for t in range(TX):
                step(dve.max(b.top[:, t], r.logits[:, t]))
                step(dve.max_index(b.index[:, t], b.top[:, t], r.logits[:, t]))
            dve.tensor_tensor(b.less[:], b.top[:, :, 0:K1], b.top[:, :, 0:1].to_broadcast([P, TX, K1]),
                              ALU.subtract).then_inc(s.shifted, 1)
            step(dve.tensor_copy(b.indexf[:], b.index[:]))
            one_hot(step, dve, k, oneh, mask, b.indexf, E1, K1)
            dve.wait_ge(s.exped, 1)
            step(dve.tensor_reduce(b.sums[:], b.e[:], AX, ALU.add))
            step(dve.reciprocal(b.sums[:], b.sums[:]))
            step(dve.tensor_tensor(r.gates[:], b.e[:], spread(b.sums[:], 2, K1), ALU.mult))


def one_hot(step, dve, k, oneh, mask, index, experts, top):
    for j in range(top):
        step(dve.tensor_tensor(oneh[:, j], spread(k.numbers[:, 0:experts], 1, TX),
                               index[:, :, j:j + 1].to_broadcast([P, TX, experts]), ALU.is_equal))
        if j == 1:
            step(dve.tensor_tensor(mask[:], oneh[:, 0], oneh[:, 1], ALU.add))
        elif j > 1:
            step(dve.tensor_tensor(mask[:], mask[:], oneh[:, j], ALU.add))


def choose_second(core, k, r, oneh, mask):
    with buffers(core, padded=[P, TX, 8], top=[P, TX, 8], index=[P, TX, 8, U32], indexf=[P, TX, 8],
                 less=[P, TX, MG], e=[P, TX, MG], sums=[P, TX], group=[P, TX, MG], penalty=[P, TX, MG],
                 inside=[P, TX, E2], gap=[P, TX], ratio=[P, TX], share=[P, TX]) as b, \
            stage(core, "choose2", "shifted", "exped", "vector_step") as (block, s):
        @block.scalar
        def _(act):
            act.wait_ge(s.shifted, 1)
            act.activation(b.e[:], b.less[:], ACT.Exp).then_inc(s.exped, 1)
            act.wait_ge(s.shifted, 2)
            act.activation(b.ratio[:], b.gap[:], ACT.Exp).then_inc(s.exped, 1)

        @block.vector
        def _(dve):
            step = Steps(dve, s.vector_step)
            step(dve.memset(b.padded[:], -BIG))
            step(dve.tensor_copy(b.padded[:, :, 0:MG], r.logits[:, :, 0:MG]))
            for t in range(TX):
                step(dve.max(b.top[:, t], b.padded[:, t]))
                step(dve.max_index(b.index[:, t], b.top[:, t], b.padded[:, t]))
            dve.tensor_tensor(b.less[:], r.logits[:, :, 0:MG], b.top[:, :, 0:1].to_broadcast([P, TX, MG]),
                              ALU.subtract).then_inc(s.shifted, 1)
            step(dve.tensor_copy(b.indexf[:], b.index[:]))
            step(dve.tensor_tensor(b.group[:], spread(k.numbers[:, 0:MG], 1, TX),
                                   b.indexf[:, :, 0:1].to_broadcast([P, TX, MG]), ALU.is_equal))
            step(dve.tensor_scalar(b.penalty[:], b.group[:], -1.0, BIG, ALU.add, ALU.mult))
            for t in range(TX):
                inside = b.inside[:, t].rearrange("p (g e) -> p g e", e=ME)
                step(dve.tensor_tensor(inside, r.logits[:, t, MG:].rearrange("p (g e) -> p g e", e=ME),
                                       spread(b.group[:, t], 2, ME), ALU.mult))
                step(dve.tensor_tensor(inside, inside, spread(b.penalty[:, t], 2, ME), ALU.add))
                step(dve.max(b.top[:, t], b.inside[:, t]))
                step(dve.max_index(b.index[:, t], b.top[:, t], b.inside[:, t]))
            dve.tensor_tensor(b.gap[:], b.top[:, :, 1], b.top[:, :, 0], ALU.subtract).then_inc(s.shifted, 1)
            step(dve.tensor_copy(b.indexf[:], b.index[:]))
            one_hot(step, dve, k, oneh, mask, b.indexf, E2, K2)
            dve.wait_ge(s.exped, 2)
            step(dve.tensor_reduce(b.sums[:], b.e[:], AX, ALU.add))
            step(dve.scalar_tensor_tensor(out=b.share[:], in0=b.ratio[:], scalar=1.0, in1=b.sums[:], op0=ALU.add,
                                          op1=ALU.mult))
            step(dve.reciprocal(r.gates[:, :, 0], b.share[:]))
            step(dve.tensor_tensor(r.gates[:, :, 1], r.gates[:, :, 0], b.ratio[:], ALU.mult))


def store_rows(core, name, rows, dram, cleared):
    with stage(core, name, "stored") as (block, s):
        @block.sync
        def _(sync):
            sync.dma_start(dram.rearrange("(t p) d -> p t d", p=P), rows).then_inc(s.stored, 16)
            sync.wait_ge(s.stored, 16)
            sync.wait_ge(cleared, 32)


def gather_tokens(pool, s, b, r, rows, block_no, value):
    pool.dma_start(b.slot_ids[:], r.slot_token[ds(block_no * P, P), :] if not isinstance(block_no, int) else
                   r.slot_token[block_no * P:(block_no + 1) * P, :]).then_inc(s.gathered, 16)
    pool.wait_ge(s.gathered, value + 16)
    pool.sem_inc(s.taken, 1)
    pool.indirect_dma_start(b.rows[:], None, rows, bass.IndirectOffsetOnAxis(ap=b.slot_ids[:, 0:1], axis=0))\
        .then_inc(s.gathered, 16)


def block_count(engine, r, n_blocks):
    return engine.value_load(r.blocks[0:1, n_blocks:n_blocks + 1], min_val=1, max_val=n_blocks)


def first_expert_blocks(core, k, r, rows, y_rows, args, n_blocks):
    nc, psum, ring = core.nc, core.psum, core.ring
    UC, YC = 2 * FF1 // BANK, D // BANK
    per = UC + YC
    half = BANK // 2
    with buffers(core, more=[P, per - SLOTS, DC, BANK], slot_ids=[P, 1, I32], rows=[P, D], turned=[P, DC, P],
                 bias_row=[1, 2 * FF1 + D], bias=[P, 2 * FF1 + D], u=[P, BANK], glu=[P, half], lin=[P, half],
                 sig=[P, half], act=[P, FF1], act_turned=[P, FF1 // P, P], y=[P, D]) as b, \
            stage(core, "experts1", *[f"chunk{c}_loaded" for c in range(per)], "chunk_done", "bias_loaded",
                  "bias_spread", "x_turned", "x_kept", "biased", "clipped", "squashed", "activated",
                  "act_turned", "act_kept", "y_added", "y_stored", "vector_step", "taken", pool_dma=("gathered",),
                  from_one=("chunk_done", "bias_spread", "x_turned", "x_kept", "biased", "clipped", "squashed", "activated", "act_turned", "act_kept", "y_added", "y_stored")) as (block, s):
        slots = [ring.slots[:, i] for i in range(SLOTS)] + [b.more[:, i] for i in range(per - SLOTS)]
        loaded = [s.chunk0_loaded, s.chunk1_loaded, s.chunk2_loaded, s.chunk3_loaded, s.chunk4_loaded,
                  s.chunk5_loaded]

        @block.sync
        def _(sync):
            n = block_count(sync, r, n_blocks)
            with sync.Fori(0, n) as i:
                e = sync.value_load(r.blocks[0:1, ds(i, 1)], min_val=0, max_val=E1 - 1)
                sync.wait_ge(s.bias_spread, i * 2 + 1)
                sync.dma_start(b.bias_row[:, 0:2 * FF1], args.b_mlp1[0][ds(e, 1), :]).then_inc(s.bias_loaded, 16)
                sync.dma_start(b.bias_row[:, 2 * FF1:], args.b_mlp2[0][ds(e, 1), :]).then_inc(s.bias_loaded, 16)
                for c in range(per):
                    sync.wait_ge(s.chunk_done, i * per + c + 1)
                    w, at = (args.w_mlp1, c) if c < UC else (args.w_mlp2, c - UC)
                    src = w[0][ds(e, 1)].rearrange("a (k p) n -> p (a k) n", p=P)
                    sync.dma_start(slots[c], src[:, :, at * BANK:(at + 1) * BANK]).then_inc(loaded[c], 16)

        @block.gpsimd
        def _(pool):
            n = block_count(pool, r, n_blocks)
            gather_tokens(pool, s, b, r, rows, 0, 0)
            with pool.Fori(0, n) as i:
                pool.wait_ge(s.bias_loaded, i * 32 + 32)
                pool.wait_ge(s.y_added, i * 2 + 1)
                pool.sem_inc(s.taken, 1)
                pool.partition_broadcast(b.bias[:, 0:2 * FF1], b.bias_row[:, 0:2 * FF1]).then_inc(s.bias_spread, 1)
                pool.partition_broadcast(b.bias[:, 2 * FF1:], b.bias_row[:, 2 * FF1:]).then_inc(s.bias_spread, 1)
                pool.wait_ge(s.x_turned, i + 2)
                pool.wait_ge(s.gathered, i * 32 + 32)
                gather_tokens(pool, s, b, r, rows, i + 1, i * 32 + 32)
            pool.wait_ge(s.gathered, n * 32 + 32)

        @block.tensor
        def _(pe):
            n = block_count(pe, r, n_blocks)

            def turn_rows():
                for m in range(DC):
                    mm = pe.transpose(psum[:, 4 + m // 4, (m % 4) * P:(m % 4 + 1) * P], b.rows[:, m * P:(m + 1) * P],
                                      k.ident[:])
                mm.then_inc(s.x_turned, 1)

            pe.sem_inc(s.chunk_done, per - 1)
            pe.wait_ge(s.gathered, 32)
            turn_rows()
            with pe.Fori(0, n) as i:
                pe.wait_ge(s.x_kept, i * 2 + 3)
                pe.wait_ge(s.y_added, i * 2 + 1)
                for c in range(UC):
                    pe.wait_ge(loaded[c], i * 16 + 16)
                    for kc in range(DC):
                        mm = pe.matmul(psum[:, c, :], b.turned[:, kc, :], slots[c][:, kc, :], start=kc == 0,
                                       stop=kc == DC - 1)
                    mm.then_inc(s.chunk_done, 1)
                pe.wait_ge(s.gathered, i * 32 + 64)
                turn_rows()
                for c in range(UC):
                    pe.wait_ge(s.activated, i * UC + (c + 2))
                    for m in range(2 * c, 2 * c + 2):
                        mm = pe.transpose(psum[:, 6 + m // 4, (m % 4) * P:(m % 4 + 1) * P],
                                          b.act[:, m * P:(m + 1) * P], k.ident[:])
                    if c % 2:
                        mm.then_inc(s.act_turned, 1)
                for c in range(YC):
                    pe.wait_ge(loaded[UC + c], i * 16 + 16)
                    pe.wait_ge(s.act_kept, i * 2 + 3)
                    for kc in range(DC):
                        mm = pe.matmul(psum[:, c, :], b.act_turned[:, kc, :], slots[UC + c][:, kc, :], start=kc == 0,
                                       stop=kc == DC - 1)
                    mm.then_inc(s.chunk_done, 1)

        @block.scalar
        def _(act):
            n = block_count(act, r, n_blocks)

            def keep_rows(value):
                act.wait_ge(s.x_turned, value + 1)
                for m in range(DC):
                    ins = act.activation(b.turned[:, m, :], psum[:, 4 + m // 4, (m % 4) * P:(m % 4 + 1) * P],
                                         ACT.Identity, scale=k.scale1f[:, m:m + 1],
                                         bias=k.cols1[:, 3 * DC + m, 0:1])
                    if m >= DC - 2:
                        ins.then_inc(s.x_kept, 1)

            keep_rows(1)
            with act.Fori(0, n) as i:
                for c in range(UC):
                    act.wait_ge(s.clipped, i * UC + (c + 2))
                    act.activation(b.sig[:], b.glu[:], ACT.Sigmoid, scale=ALPHA).then_inc(s.squashed, 1)
                keep_rows(i + 2)
                for c in range(2):
                    act.wait_ge(s.act_turned, i * 2 + (c + 2))
                    act.copy(b.act_turned[:, 4 * c:4 * c + 4, :], psum[:, 6 + c, :].rearrange("p (m q) -> p m q", q=P))\
                        .then_inc(s.act_kept, 1)
                act.wait_ge(s.y_added, i * 2 + 3)
                act.dma_start(y_rows[ds(i * P, P), :], b.y[:]).then_inc(s.y_stored, 16)
            act.wait_ge(s.y_stored, n * 16 + 1)
            act.sem_inc(s.taken, 1)

        @block.vector
        def _(dve):
            n = block_count(dve, r, n_blocks)
            step = Steps(dve, s.vector_step)
            with dve.Fori(0, n) as i:
                step.restart()
                dve.wait_ge(s.act_turned, i * 2 + 1)
                dve.wait_ge(s.bias_spread, i * 2 + 3)
                for c in range(UC):
                    dve.wait_ge(s.chunk_done, i * per + (c + per + 1))
                    step(dve.tensor_tensor(b.u[:], psum[:, c, :], b.bias[:, c * BANK:(c + 1) * BANK], ALU.add))
                    step.reach(dve.tensor_scalar(b.glu[:], b.u[:, 0::2], LIMIT, None, ALU.min), s.clipped,
                                i * UC + (c + 2))
                    step(dve.tensor_scalar(b.lin[:], b.u[:, 1::2], LIMIT, -LIMIT, ALU.min, ALU.max))
                    step(dve.scalar_tensor_tensor(out=b.lin[:], in0=b.lin[:], scalar=1.0, in1=b.glu[:], op0=ALU.add,
                                                  op1=ALU.mult))
                    dve.wait_ge(s.squashed, i * UC + (c + 2))
                    step.reach(dve.tensor_tensor(b.act[:, c * half:(c + 1) * half], b.lin[:], b.sig[:], ALU.mult),
                                s.activated, i * UC + (c + 2))
                dve.wait_ge(s.y_stored, i * 16 + 1)
                for c in range(YC):
                    dve.wait_ge(s.chunk_done, i * per + (UC + c + per + 1))
                    dve.tensor_tensor(b.y[:, c * BANK:(c + 1) * BANK], psum[:, c, :],
                                      b.bias[:, 2 * FF1 + c * BANK:2 * FF1 + (c + 1) * BANK], ALU.add)\
                        .then_inc(s.y_added, 1)


def second_expert_blocks(core, k, r, rows, y_rows, args, n_blocks):
    nc, psum, ring = core.nc, core.psum, core.ring
    hk = DC // 2
    fk = FF2 // P
    per = 3
    down = ring.slots[:, 2].rearrange("p k n -> p (k n)")[:, 0:fk * D].rearrange("p (k n) -> p k n", k=fk)
    with buffers(core, slot_ids=[P, 1, I32], rows=[P, D], turned=[P, DC, P], sil=[P, FF2], act=[P, FF2],
                 act_turned=[P, fk, P], y=[P, D]) as b, \
            stage(core, "experts2", "first_loaded", "second_loaded", "down_loaded", "chunk_done", "x_turned", "x_kept", "silued", "activated", "act_turned", "act_kept", "y_copied", "y_stored", "taken",
                  pool_dma=("gathered",),
                  from_one=("chunk_done", "x_turned", "x_kept", "silued", "activated", "act_turned", "act_kept", "y_copied", "y_stored")) \
            as (block, s):
        @block.sync
        def _(sync):
            n = block_count(sync, r, n_blocks)
            with sync.Fori(0, n) as i:
                e = sync.value_load(r.blocks[0:1, ds(i, 1)], min_val=0, max_val=E2 - 1)
                for c, loaded in enumerate((s.first_loaded, s.second_loaded)):
                    sync.wait_ge(s.chunk_done, i * per + c + 1)
                    for at, w in enumerate((args.w_gate_2, args.w_up_2)):
                        src = w[0][ds(e, 1)].rearrange("a (k p) n -> p (a k) n", p=P)
                        sync.dma_start(ring.slots[:, c, 0:hk, at * FF2:(at + 1) * FF2],
                                       src[:, c * hk:(c + 1) * hk, :]).then_inc(loaded, 16)
                sync.wait_ge(s.chunk_done, i * per + 3)
                sync.dma_start(down, args.w_down_2[0][ds(e, 1)].rearrange("a (k p) n -> p (a k) n", p=P))\
                    .then_inc(s.down_loaded, 16)

        @block.gpsimd
        def _(pool):
            n = block_count(pool, r, n_blocks)
            gather_tokens(pool, s, b, r, rows, 0, 0)
            with pool.Fori(0, n) as i:
                pool.wait_ge(s.x_turned, i + 2)
                pool.wait_ge(s.gathered, i * 32 + 32)
                gather_tokens(pool, s, b, r, rows, i + 1, i * 32 + 32)
            pool.wait_ge(s.gathered, n * 32 + 32)

        @block.tensor
        def _(pe):
            n = block_count(pe, r, n_blocks)

            def turn_rows():
                for m in range(DC):
                    mm = pe.transpose(psum[:, 4 + m // 4, (m % 4) * P:(m % 4 + 1) * P], b.rows[:, m * P:(m + 1) * P],
                                      k.ident[:])
                mm.then_inc(s.x_turned, 1)

            pe.sem_inc(s.chunk_done, per - 1)
            pe.wait_ge(s.gathered, 32)
            turn_rows()
            with pe.Fori(0, n) as i:
                pe.wait_ge(s.x_kept, i * 2 + 3)
                pe.wait_ge(s.activated, i + 1)
                for c, loaded in enumerate((s.first_loaded, s.second_loaded)):
                    pe.wait_ge(loaded, i * 32 + 32)
                    for kc in range(hk):
                        mm = pe.matmul(psum[:, 0, :], b.turned[:, c * hk + kc, :], ring.slots[:, c, kc, :],
                                       start=c == 0 and kc == 0, stop=c == 1 and kc == hk - 1)
                    mm.then_inc(s.chunk_done, 1)
                pe.wait_ge(s.gathered, i * 32 + 64)
                turn_rows()
                pe.wait_ge(s.activated, i + 2)
                for m in range(fk):
                    mm = pe.transpose(psum[:, 6, m * P:(m + 1) * P], b.act[:, m * P:(m + 1) * P], k.ident[:])
                mm.then_inc(s.act_turned, 1)
                pe.wait_ge(s.down_loaded, i * 16 + 16)
                pe.wait_ge(s.act_kept, i + 2)
                pe.wait_ge(s.y_copied, i * 2 + 1)
                for c in range(D // BANK):
                    for kc in range(fk):
                        mm = pe.matmul(psum[:, 1 + c, :], b.act_turned[:, kc, :],
                                       down[:, kc, c * BANK:(c + 1) * BANK], start=kc == 0, stop=kc == fk - 1)
                mm.then_inc(s.chunk_done, 1)

        @block.scalar
        def _(act):
            n = block_count(act, r, n_blocks)

            def keep_rows(value):
                act.wait_ge(s.x_turned, value + 1)
                for m in range(DC):
                    ins = act.activation(b.turned[:, m, :], psum[:, 4 + m // 4, (m % 4) * P:(m % 4 + 1) * P],
                                         ACT.Identity, scale=k.scale2f[:, m:m + 1],
                                         bias=k.cols2[:, 3 * DC + m, 0:1])
                    if m >= DC - 2:
                        ins.then_inc(s.x_kept, 1)

            keep_rows(1)
            with act.Fori(0, n) as i:
                act.wait_ge(s.chunk_done, i * per + 5)
                act.activation(b.sil[:], psum[:, 0, 0:FF2], ACT.Silu).then_inc(s.silued, 1)
                keep_rows(i + 2)
                act.wait_ge(s.y_copied, i * 2 + 3)
                act.dma_start(y_rows[ds(i * P, P), :], b.y[:]).then_inc(s.y_stored, 16)
            act.wait_ge(s.y_stored, n * 16 + 1)
            act.sem_inc(s.taken, 1)

        @block.vector
        def _(dve):
            n = block_count(dve, r, n_blocks)
            with dve.Fori(0, n) as i:
                dve.wait_ge(s.silued, i + 2)
                dve.wait_ge(s.act_turned, i + 1)
                dve.tensor_tensor(b.act[:], b.sil[:], psum[:, 0, FF2:2 * FF2], ALU.mult).then_inc(s.activated, 1)
                dve.wait_ge(s.act_turned, i + 2)
                dve.tensor_copy(b.act_turned[:], psum[:, 6, 0:FF2].rearrange("p (m q) -> p m q", q=P))\
                    .then_inc(s.act_kept, 1)
                dve.wait_ge(s.chunk_done, i * per + 6)
                dve.wait_ge(s.y_stored, i * 16 + 1)
                for c in range(D // BANK):
                    dve.tensor_copy(b.y[:, c * BANK:(c + 1) * BANK], psum[:, 1 + c, :]).then_inc(s.y_copied, 1)


def combine(core, k, name, r, y_rows, rows, top, alpha):
    ahead = 4
    with buffers(core, got=[P, ahead, D], total=[P, D], gate=[P, D]) as b, \
            stage(core, name, "gate_loaded", "added", "vector_step", pool_dma=("got0", "got1", "got2", "got3")) as (block, s):
        got = [s.got0, s.got1, s.got2, s.got3]
        work = [(t, j) for t in range(TX) for j in range(top)]

        @block.sync
        def _(sync):
            sync.dma_start(b.gate[:], on_all(rows[0:1, 5 * D:6 * D])).then_inc(s.gate_loaded, 16)

        @block.gpsimd
        def _(pool):
            for i, (t, j) in enumerate(work):
                if i >= ahead:
                    pool.wait_ge(s.added, i - ahead + 1)
                pool.indirect_dma_start(b.got[:, i % ahead], None, y_rows,
                                        bass.IndirectOffsetOnAxis(ap=r.dest[:, i:i + 1], axis=0))\
                    .then_inc(got[i % ahead], 16)

        @block.vector
        def _(dve):
            step = Steps(dve, s.vector_step)
            dve.wait_ge(s.gate_loaded, 16)
            for i, (t, j) in enumerate(work):
                dve.wait_ge(got[i % ahead], 16 * (i // ahead + 1))
                share = r.gates[:, t, j:j + 1]
                if j == 0:
                    ins = dve.tensor_scalar(b.total[:], b.got[:, i % ahead], share, None, ALU.mult)
                else:
                    ins = dve.scalar_tensor_tensor(out=b.total[:], in0=b.got[:, i % ahead], scalar=share,
                                                   in1=b.total[:], op0=ALU.mult, op1=ALU.add)
                step.reach(ins, s.added, i + 1)
                if j == top - 1:
                    step(dve.tensor_tensor(b.total[:], b.total[:], b.gate[:], ALU.mult))
                    step(dve.scalar_tensor_tensor(out=k.x[:, t], in0=k.x[:, t], scalar=alpha, in1=b.total[:],
                                                  op0=ALU.mult, op1=ALU.add))


def expert_layer(core, k, args, which):
    nc = core.nc
    first = which == 1
    experts, top = (E1, K1) if first else (E2, K2)
    width = E1 if first else MG + E2
    n_blocks = most_blocks(L, top, experts)
    rows = nc.dram_tensor(f"token_rows{which}", [L, D], F32).ap()
    y_rows = k.slot_rows1 if first else k.slot_rows2
    slot_token = nc.dram_tensor(f"slot_token{which}", [(n_blocks + 1) * P, 1], I32).ap()
    scale, cols = (k.scale1f, k.cols1) if first else (k.scale2f, k.cols2)
    with buffers(core, logits=[P, TX, width], gates=[P, TX, top], dest=[P, TX * top, I32],
                 blocks=[1, n_blocks + 1, I32], others={"slot_token": slot_token}) as r:
        with buffers(core, turned=[P, DC, L], xn=[P, TX, D], junk=[P, D]) as b:
            src = k.x
            if first:
                norm_rows(core, k, "norm_ffn", [(k.x[:, t], b.xn[:, t]) for t in range(TX)], b.junk[:])
                src = b.xn
            store_rows(core, f"store_rows{which}", src[:], rows, k.slots_cleared)
            to_features(core, k, f"turn_ffn{which}", [
                ([lambda i, t=t: src[:, t, i * P:(i + 1) * P] for t in range(TX)], DC,
                 lambda i: b.turned[:, i, :], lambda i: scale[:, i:i + 1], lambda i: cols[:, 3 * DC + i, 0:1])])
            if first:
                logits_of(core, k, "logits1", b.turned, r, [args.w_router[0]], [args.b_router], width)
            else:
                logits_of(core, k, "logits2", b.turned, r, [args.w_rg_2[0], args.w_re_2[0]],
                          [args.b_rg_2, args.b_re_2], width)
        with buffers(core, oneh=[P, top, TX, experts], mask=[P, TX, experts]) as b:
            (choose_first if first else choose_second)(core, k, r, b.oneh, b.mask)
            places(core, k, f"places{which}", r, b.oneh, b.mask, experts, top, n_blocks)
        (first_expert_blocks if first else second_expert_blocks)(core, k, r, rows, y_rows, args, n_blocks)
        combine(core, k, f"combine{which}", r, y_rows, k.rows1 if first else k.rows2, top, 1.0 if first else ALPHA2)


def first_experts(core, k, args):
    expert_layer(core, k, args, 1)


def second_experts(core, k, args):
    expert_layer(core, k, args, 2)
    layer_norm(core, k, "ln2", args.ln2_g_2, args.ln2_b_2)




CTX_AT, X_AT = 2, LC + 6
WIDE = LC + L + 8


def layer_norm(core, k, name, gain, bias):
    with buffers(core, sums=[P, TX], squares=[P, TX], roots=[P, TX], rates=[P, TX], eps=[P, 1], junk=[P, D],
                 gain=[P, D], bias=[P, D]) as b, \
            stage(core, name, "loaded", "summed", "centred", "rooted", "scalar_step", "vector_step", "eps_set") \
            as (block, s):
        @block.sync
        def _(sync):
            sync.dma_start(b.gain[:], on_all(gain)).then_inc(s.loaded, 16)
            sync.dma_start(b.bias[:], on_all(bias)).then_inc(s.loaded, 16)

        @block.gpsimd
        def _(pool):
            pool.memset(b.eps[:], 1e-5).then_inc(s.eps_set, 1)

        @block.scalar
        def _(act):
            step = Steps(act, s.scalar_step)
            for t in range(TX):
                step.reach(act.activation(b.junk[:], k.x[:, t], ACT.Copy, accum_out=b.sums[:, t:t + 1]),
                            s.summed, t + 1)
            for t in range(TX):
                act.wait_ge(s.centred, t + 1)
                step(act.activation(b.junk[:], k.x[:, t], ACT.Square, accum_out=b.squares[:, t:t + 1]))
            act.wait_ge(s.eps_set, 1)
            act.activation(b.roots[:], b.squares[:], ACT.Sqrt, scale=1.0 / D, bias=b.eps[:, 0:1])\
                .then_inc(s.rooted, 1)

        @block.vector
        def _(dve):
            step = Steps(dve, s.vector_step)
            for t in range(TX):
                dve.wait_ge(s.summed, t + 1)
                step(dve.tensor_scalar(b.sums[:, t:t + 1], b.sums[:, t:t + 1], 1.0 / D, None, ALU.mult))
                step.reach(dve.tensor_scalar(k.x[:, t], k.x[:, t], b.sums[:, t:t + 1], None, ALU.subtract),
                            s.centred, t + 1)
            dve.wait_ge(s.rooted, 1)
            step(dve.reciprocal(b.rates[:], b.roots[:]))
            dve.wait_ge(s.loaded, 32)
            for t in range(TX):
                step(dve.scalar_tensor_tensor(out=k.x[:, t], in0=k.x[:, t], scalar=b.rates[:, t:t + 1],
                                              in1=b.gain[:], op0=ALU.mult, op1=ALU.mult))
                step(dve.tensor_tensor(k.x[:, t], k.x[:, t], b.bias[:], ALU.add))


def convolve(core, k, raw, xs, b_rows, conv_w, conv_b):
    nc, psum = core.nc, core.psum
    chunks = DXBC // P
    n_xs = DS // P
    n_turned = n_xs + SG
    span = WIDE - TAPS + 1
    flat = psum[:, :, :].rearrange("p b n -> p (b n)")
    with buffers(core, taps=[P, chunks, TAPS], bias=[P, chunks], acc=[P, 2, span], sil=[P, 2, span]) as b, \
            stage(core, "convolve", "loaded", "first_tap", "last_tap", "silued", "turned", "kept", "vector_step") \
            as (block, s):
        @block.sync
        def _(sync):
            for j in range(TAPS):
                sync.dma_start(b.taps[:, :, j], by_column(conv_w[0, j]), allow_slow_non_contiguous=True)\
                    .then_inc(s.loaded, 16)
            sync.dma_start(b.bias[:], by_column(conv_b[0]), allow_slow_non_contiguous=True).then_inc(s.loaded, 16)

        @block.scalar
        def _(act):
            act.wait_ge(s.loaded, 16 * (TAPS + 1))

            def first(c):
                if c >= 2:
                    act.wait_ge(s.silued, c - 1)
                act.activation(b.acc[:, c % 2], raw[:, c, 0:span], ACT.Identity,
                               scale=b.taps[:, c, 0:1]).then_inc(s.first_tap, 1)

            first(0)
            for c in range(chunks):
                if c + 1 < chunks:
                    first(c + 1)
                act.wait_ge(s.last_tap, c + 1)
                if 2 <= c < n_turned:
                    act.wait_ge(s.turned, c - 1)
                out = b.sil[:, c % 2] if c < n_xs else raw[:, c, 0:span]
                act.activation(out, b.acc[:, c % 2], ACT.Silu, bias=b.bias[:, c:c + 1]).then_inc(s.silued, 1)
                if c < n_turned:
                    act.wait_ge(s.turned, c + 1)
                    dst = xs[:, :, c * P:(c + 1) * P] if c < n_xs else b_rows[:, :, c - n_xs]
                    act.copy(dst, flat[:, (c % 2) * 2 * BANK:(c % 2) * 2 * BANK + TK * P]
                             .rearrange("p (t n) -> p t n", t=TK)).then_inc(s.kept, 1)
            act.wait_ge(s.kept, n_turned)

        @block.vector
        def _(dve):
            step = Steps(dve, s.vector_step)
            for c in range(chunks):
                dve.wait_ge(s.first_tap, c + 1)
                for j in range(1, TAPS):
                    ins = dve.scalar_tensor_tensor(out=b.acc[:, c % 2], in0=raw[:, c, j:j + span],
                                                   scalar=b.taps[:, c, j:j + 1], in1=b.acc[:, c % 2],
                                                   op0=ALU.mult, op1=ALU.add)
                    if j < TAPS - 1:
                        step(ins)
                    else:
                        step.reach(ins, s.last_tap, c + 1)

        @block.tensor
        def _(pe):
            for c in range(n_turned):
                pe.wait_ge(s.silued, c + 1)
                if c >= 2:
                    pe.wait_ge(s.kept, c - 1)
                src = b.sil[:, c % 2] if c < n_xs else raw[:, c]
                for t in range(TK):
                    at = X_AT - CTX_AT + t * P if t < TX else (t - TX) * P
                    mm = pe.transpose(flat[:, (c % 2) * 2 * BANK + t * P:(c % 2) * 2 * BANK + (t + 1) * P],
                                      src[:, at:at + P], k.ident[:])
                mm.then_inc(s.turned, 1)


def step_sizes(core, k, w, args):
    nc, psum = core.nc, core.psum
    n = 2 * SH
    with buffers(core, bias=[P, n], a_row=[P, n], a_neg=[P, n], t0=[P, TK, n], t1=[P, TK, n], left=[P, TK, n]) as b, \
            stage(core, "step_sizes", "loaded", "a_exped", "biased", "logs", "scaled", "summed", "differed",
                  "exped", "scalar_step", "vector_step") as (block, s):
        @block.sync
        def _(sync):
            sync.dma_start(b.bias[:], on_all(args.dt_bias_2.rearrange("o d h -> o (d h)"))).then_inc(s.loaded, 16)
            sync.dma_start(b.a_row[:], on_all(args.a_log_2.rearrange("o d h -> o (d h)"))).then_inc(s.loaded, 16)

        @block.scalar
        def _(act):
            step = Steps(act, s.scalar_step)
            act.wait_ge(s.loaded, 32)
            act.activation(b.a_neg[:], b.a_row[:], ACT.Exp).then_inc(s.a_exped, 1)
            act.wait_ge(s.biased, 1)
            step(act.activation(b.t1[:], b.t0[:], ACT.Abs))
            step(act.activation(b.t1[:], b.t1[:], ACT.Exp, scale=-1.0))
            act.activation(b.t1[:], b.t1[:], ACT.Ln, bias=k.one[:, 0:1]).then_inc(s.logs, 1)
            act.wait_ge(s.differed, 1)
            step(act.activation(w.to_end[:], b.left[:], ACT.Exp))
            step(act.activation(w.whole[:], w.total[:], ACT.Exp))
            act.activation(w.grown[:], w.running[:, 0:TX], ACT.Exp).then_inc(s.exped, 1)

        @block.tensor
        def _(pe):
            pe.wait_ge(s.scaled, 1)
            half = lambda bank, d: psum[:, bank, 0:TK * SH].rearrange("p (t h) -> p t h", t=TK)
            pe.matmul(half(0, 0), k.upto[:], w.a[:, :, 0:SH], start=True, stop=True)
            pe.matmul(half(1, 1), k.after[:], w.a[:, :, SH:n], start=True, stop=True)
            pe.matmul(psum[:, 2, 0:TK * n].rearrange("p (t h) -> p t h", t=TK), k.ones[:], w.a[:],
                      start=True, stop=True).then_inc(s.summed, 1)

        @block.vector
        def _(dve):
            step = Steps(dve, s.vector_step)
            dve.wait_ge(s.loaded, 32)
            dve.tensor_tensor(b.t0[:], w.raw_dt[:], spread(b.bias[:], 1, TK), ALU.add).then_inc(s.biased, 1)
            dve.wait_ge(s.logs, 1)
            step(dve.scalar_tensor_tensor(out=w.dt[:], in0=b.t0[:], scalar=0.0, in1=b.t1[:], op0=ALU.max, op1=ALU.add))
            dve.wait_ge(s.a_exped, 1)
            dve.scalar_tensor_tensor(out=w.a[:], in0=w.dt[:], scalar=-1.0, in1=spread(b.a_neg[:], 1, TK),
                                     op0=ALU.mult, op1=ALU.mult).then_inc(s.scaled, 1)
            dve.wait_ge(s.summed, 1)
            for d in range(2):
                step(dve.tensor_copy(w.running[:, :, d * SH:(d + 1) * SH],
                                     psum[:, d, 0:TK * SH].rearrange("p (t h) -> p t h", t=TK)))
            step(dve.tensor_copy(w.total[:], psum[:, 2, 0:TK * n].rearrange("p (t h) -> p t h", t=TK)))
            step(dve.tensor_scalar(w.fallen[:], w.running[:], -1.0, None, ALU.mult))
            dve.tensor_tensor(b.left[:], w.total[:], w.running[:], ALU.subtract).then_inc(s.differed, 1)
            dve.wait_ge(s.exped, 1)
            step(dve.tensor_tensor(w.to_end[:], w.to_end[:], w.dt[:], ALU.mult))


def carry_states(core, k, w, raw, xs, b_rows, y):
    nc, psum = core.nc, core.psum
    work = [(d, i, t) for d, tiles in enumerate(([4, 5, 0, 1, 2, 3], [5, 4, 3, 2, 1, 0])) for i, t in enumerate(tiles)]
    states = [(d, i, t) for d, i, t in work if i < TK - 1]
    gw = SR * SP_
    with buffers(core, weighted=[P, 2, DS], h=[P, SG, gw], read=[P, gw]) as b, \
            stage(core, "carry", "weighted", "state_summed", "read_summed", "read_out", "updated", "vector_step") \
            as (block, s):
        per_head = lambda v, t, d, g: spread(v[:, t, d * SH + g * SR:d * SH + (g + 1) * SR], 2, SP_)
        heads = lambda v: v.rearrange("p (r e) -> p r e", e=SP_)

        @block.gpsimd
        def _(pool):
            for n, (d, i, t) in enumerate(states):
                if n >= 2:
                    pool.wait_ge(s.state_summed, n - 1)
                pool.tensor_tensor(heads(b.weighted[:, n % 2]), heads(xs[:, t]),
                                   spread(w.to_end[:, t, d * SH:(d + 1) * SH], 2, SP_), ALU.mult)\
                    .then_inc(s.weighted, 1)

        @block.tensor
        def _(pe):
            n = reads = 0
            for d, i, t in work:
                if t < TX:
                    pe.wait_ge(s.updated, n)
                    pe.wait_ge(s.read_out, reads)
                    for g in range(SG):
                        mm = pe.matmul(psum[:, 4 + g, :], raw[:, DS // P + SG + g, X_AT - CTX_AT + t * P:
                                                              X_AT - CTX_AT + (t + 1) * P], b.h[:, g, :],
                                       start=True, stop=True)
                    mm.then_inc(s.read_summed, 1)
                    reads += 1
                if i < TK - 1:
                    pe.wait_ge(s.weighted, n + 1)
                    if n >= 2:
                        pe.wait_ge(s.updated, n - 1)
                    for g in range(SG):
                        mm = pe.matmul(psum[:, 2 * (n % 2) + g, :], b_rows[:, t, g], b.weighted[:, n % 2,
                                       g * gw:(g + 1) * gw], start=True, stop=True)
                    mm.then_inc(s.state_summed, 1)
                    n += 1

        @block.vector
        def _(dve):
            step = Steps(dve, s.vector_step)
            n = reads = 0
            for d, i, t in work:
                if t < TX:
                    reads += 1
                    dve.wait_ge(s.read_summed, reads)
                    for g in range(SG):
                        into = y[:, t, g * gw:(g + 1) * gw] if d == 0 else b.read[:]
                        step(dve.tensor_tensor(heads(into), heads(psum[:, 4 + g, :]), per_head(w.grown, t, d, g),
                                               ALU.mult))
                        if d == 1:
                            out = y[:, t, g * gw:(g + 1) * gw]
                            step(dve.tensor_tensor(out, out, b.read[:], ALU.add))
                    dve.sem_inc(s.read_out, 1)
                if i < TK - 1:
                    dve.wait_ge(s.state_summed, n + 1)
                    for g in range(SG):
                        bank = psum[:, 2 * (n % 2) + g, :]
                        if i == 0:
                            ins = dve.tensor_copy(b.h[:, g], bank)
                        else:
                            step(dve.tensor_tensor(heads(b.h[:, g]), heads(b.h[:, g]), per_head(w.whole, t, d, g),
                                                   ALU.mult))
                            ins = dve.tensor_tensor(b.h[:, g], b.h[:, g], bank, ALU.add)
                        if g < SG - 1:
                            step(ins)
                        else:
                            step.reach(ins, s.updated, n + 1)
                    n += 1


def within_chunks(core, k, w, raw, xs, y):
    nc, psum = core.nc, core.psum
    flat = psum[:, :, :].rearrange("p b n -> p (b n)")
    work = [(t, g, d) for t in range(TX) for g in range(SG) for d in range(2)]
    gw = SR * SP_
    with buffers(core, decay=[P, 2, SR * P], xdt=[P, 2, DS], cb=[P, P], never=[P, 2, P]) as b, \
            stage(core, "within", "xdt_made", "never_made", "cb_summed", "cb_kept", "spread_out", "exped", "joined",
                  "summed", "added", "vector_step") as (block, s):
        @block.gpsimd
        def _(pool):
            for t in range(TX):
                for d in range(2):
                    if t:
                        pool.wait_ge(s.summed, 4 * t)
                    pool.tensor_tensor(b.xdt[:, d].rearrange("p (h e) -> p h e", e=SP_),
                                       xs[:, t].rearrange("p (h e) -> p h e", e=SP_),
                                       spread(w.dt[:, t, d * SH:(d + 1) * SH], 2, SP_), ALU.mult)\
                        .then_inc(s.xdt_made, 1)

        @block.tensor
        def _(pe):
            pe.wait_ge(s.never_made, 2)

            def decays(n):
                t, g, d = work[n]
                at = X_AT - CTX_AT + t * P
                if d == 0:
                    pe.wait_ge(s.cb_kept, n // 2)
                    pe.matmul(psum[:, 6, 0:P], raw[:, DS // P + g, at:at + P],
                              raw[:, DS // P + SG + g, at:at + P], start=True, stop=True).then_inc(s.cb_summed, 1)
                if n >= 2:
                    pe.wait_ge(s.exped, n - 1)
                for r in range(SR):
                    c = d * SH + g * SR + r
                    out = flat[:, (n % 2) * 2 * BANK + r * P:(n % 2) * 2 * BANK + (r + 1) * P]
                    pe.matmul(out, w.a[:, t, c:c + 1].to_broadcast([P, P]), k.after[:] if d else k.upto[:],
                              start=True, stop=False)
                    mm = pe.matmul(out, k.ident[:], b.never[:, d], start=False, stop=True)
                mm.then_inc(s.spread_out, 1)

            decays(0)
            for n, (t, g, d) in enumerate(work):
                if n + 1 < len(work):
                    decays(n + 1)
                pe.wait_ge(s.joined, n + 1)
                pe.wait_ge(s.xdt_made, 2 * t + 2)
                if n >= 2:
                    pe.wait_ge(s.added, n - 1)
                for r in range(SR):
                    mm = pe.matmul(psum[:, 4 + n % 2, r * SP_:(r + 1) * SP_], b.decay[:, n % 2, r * P:(r + 1) * P],
                                   b.xdt[:, d, (g * SR + r) * SP_:(g * SR + r + 1) * SP_], start=True, stop=True)
                mm.then_inc(s.summed, 1)

        @block.scalar
        def _(act):
            for n, (t, g, d) in enumerate(work):
                act.wait_ge(s.spread_out, n + 1)
                if n >= 2:
                    act.wait_ge(s.summed, n - 1)
                for r in range(SR):
                    c = d * SH + g * SR + r
                    ins = act.activation(b.decay[:, n % 2, r * P:(r + 1) * P],
                                         flat[:, (n % 2) * 2 * BANK + r * P:(n % 2) * 2 * BANK + (r + 1) * P],
                                         ACT.Exp, bias=w.fallen[:, t, c:c + 1])
                ins.then_inc(s.exped, 1)

        @block.vector
        def _(dve):
            step = Steps(dve, s.vector_step)
            for d in range(2):
                dve.tensor_scalar(b.never[:, d], k.after[:] if d else k.upto[:], -1.0, 1e30, ALU.add, ALU.mult)\
                    .then_inc(s.never_made, 1)

            def add(n):
                t, g, _ = work[n]
                out = y[:, t, g * gw:(g + 1) * gw]
                dve.wait_ge(s.summed, n + 1)
                step.reach(dve.tensor_tensor(out, out, psum[:, 4 + n % 2, :], ALU.add), s.added, n + 1)

            for n, (t, g, d) in enumerate(work):
                if d == 0:
                    dve.wait_ge(s.cb_summed, n // 2 + 1)
                    step.reach(dve.tensor_copy(b.cb[:], psum[:, 6, 0:P]), s.cb_kept, n // 2 + 1)
                dve.wait_ge(s.exped, n + 1)
                v = b.decay[:, n % 2].rearrange("p (r q) -> p r q", q=P)
                step.reach(dve.tensor_tensor(v, v, spread(b.cb[:], 1, SR), ALU.mult), s.joined, n + 1)
                if n >= 1:
                    add(n - 1)
            add(len(work) - 1)


def state_output(core, k, xs, y, z, args):
    gw = DS // SG
    with buffers(core, skip=[P, SH], gain=[P, DS], skipped=[P, DS], junk=[P, gw], sums=[P, TX * SG],
                 roots=[P, TX * SG], rates=[P, TX * SG]) as b, \
            stage(core, "state_out", "loaded", "gated", "multiplied", "rooted", "scalar_step", "vector_step") \
            as (block, s):
        @block.sync
        def _(sync):
            sync.dma_start(b.skip[:], on_all(args.d_skip_2)).then_inc(s.loaded, 16)
            sync.dma_start(b.gain[:], on_all(args.ssd_norm_g_2)).then_inc(s.loaded, 16)

        @block.scalar
        def _(act):
            step = Steps(act, s.scalar_step)
            act.activation(z, z, ACT.Silu).then_inc(s.gated, 1)
            for t in range(TX):
                act.wait_ge(s.multiplied, t + 1)
                for g in range(SG):
                    step(act.activation(b.junk[:], y[:, t, g * gw:(g + 1) * gw], ACT.Square,
                                        accum_out=b.sums[:, t * SG + g:t * SG + g + 1]))
            act.activation(b.roots[:], b.sums[:], ACT.Sqrt, scale=1.0 / gw, bias=k.eps[:, 0:1]).then_inc(s.rooted, 1)

        @block.vector
        def _(dve):
            step = Steps(dve, s.vector_step)
            dve.wait_ge(s.loaded, 32)
            heads = lambda v: v.rearrange("p (h e) -> p h e", e=SP_)
            for t in range(TX):
                step(dve.tensor_tensor(heads(b.skipped[:]), heads(xs[:, t]), spread(b.skip[:], 2, SP_), ALU.mult))
                step(dve.tensor_tensor(y[:, t], y[:, t], b.skipped[:], ALU.add))
                dve.wait_ge(s.gated, 1)
                step.reach(dve.tensor_tensor(y[:, t], y[:, t], z[:, t], ALU.mult), s.multiplied, t + 1)
            dve.wait_ge(s.rooted, 1)
            step(dve.reciprocal(b.rates[:], b.roots[:]))
            for t in range(TX):
                for g in range(SG):
                    v = y[:, t, g * gw:(g + 1) * gw]
                    step(dve.scalar_tensor_tensor(out=v, in0=v, scalar=b.rates[:, t * SG + g:t * SG + g + 1],
                                                  in1=b.gain[:, g * gw:(g + 1) * gw], op0=ALU.mult, op1=ALU.mult))


def second_mixer(core, k, args):
    w_in = args.w_in_2[0].rearrange("(k p) n -> p k n", p=P)
    with buffers(core, z=[P, TX, DS], q=[P, TX, AH * AD], raw=[P, DXBC // P, WIDE], raw_dt=[P, TK, 2 * SH]) as m:
        with buffers(core, keys=[P, TK, AKV * AD], values=[P, TK, AKV * AD]) as a:
            with buffers(core, turned=[P, DC, TK * P]) as h:
                chunks, outs = [], []

                def rows(lo, hi, tiles, out):
                    chunks.append(token_chunk(w_in[:, :, lo:hi], tiles, len(outs),
                                              lambda kc, t: h.turned[:, kc, t * P:(t + 1) * P]))
                    outs.extend((hi - lo, out(t)) for t in tiles)

                for i in range(2):
                    rows(i * BANK, (i + 1) * BANK, range(TX), lambda t: m.z[:, t, i * BANK:(i + 1) * BANK])
                for i in range(2):
                    rows(O_Q2 + i * BANK, O_Q2 + (i + 1) * BANK, range(TX),
                         lambda t: m.q[:, t, i * BANK:(i + 1) * BANK])
                for j in range(DXBC // BANK):
                    passes = []
                    for c in range(BANK // P):
                        ch = j * (BANK // P) + c
                        for lo, n, at in ((0, L, X_AT), (L, LC, CTX_AT)):
                            if lo and ch >= (DS + SG * SN) // P:
                                continue
                            passes.append(record(
                                group=len(outs), width=n, first=True, last=True,
                                lhs=lambda kc, slot, c=c: slot[:, kc, c * P:(c + 1) * P],
                                rhs=lambda kc, slot, lo=lo, n=n: h.turned[:, kc, lo:lo + n]))
                            outs.append((n, m.raw[:, ch, at:at + n]))
                    chunks.append(record(
                        source=w_in[:, :, O_XBC + j * BANK:O_XBC + (j + 1) * BANK], passes=passes))
                rows(O_DT, O_K2, range(TK), lambda t: m.raw_dt[:, t])
                rows(O_K2, O_V2, range(TK), lambda t: a.keys[:, t])
                rows(O_V2, DIN2, range(TK), lambda t: a.values[:, t])
                with buffers(core, ctx=[P, TC, D]) as b:
                    with stage(core, "load_ctx2", "loaded", "padded") as (block, s):
                        @block.sync
                        def _(sync):
                            sync.dma_start(b.ctx[:], args.ctx_2[0].rearrange("(t p) d -> p t d", p=P))\
                                .then_inc(s.loaded, 16)
                            sync.wait_ge(s.loaded, 16)

                        @block.gpsimd
                        def _(pool):
                            pool.memset(m.raw[:, :, 0:CTX_AT], 0.0).then_inc(s.padded, 1)
                            pool.memset(m.raw[:, :, CTX_AT + LC:X_AT], 0.0).then_inc(s.padded, 1)
                            pool.memset(m.raw[:, :, X_AT + L:WIDE], 0.0).then_inc(s.padded, 1)
                            pool.memset(m.raw[:, (DS + SG * SN) // P:, CTX_AT:CTX_AT + LC], 0.0)\
                                .then_inc(s.padded, 1)
                            pool.wait_ge(s.padded, 4)
                    to_features(core, k, "turn2", [
                        ([lambda i, t=t: k.x[:, t, i * P:(i + 1) * P] for t in range(TX)], DC,
                         lambda i: h.turned[:, i, 0:L], lambda i: k.scale2[:, i:i + 1],
                         lambda i: k.cols2[:, i, 0:1]),
                        ([lambda i, t=t: b.ctx[:, t, i * P:(i + 1) * P] for t in range(TC)], DC,
                         lambda i: h.turned[:, i, L:L + LC], lambda i: k.scale2c[:, i:i + 1],
                         lambda i: k.cols2[:, i, 1:2])], prefetch=load_first(core, chunks))
                project(core, k, "in2", chunks,
                        lambda e, s, g, bank, step: copy_out(e, outs[g][1], bank[:, 0:outs[g][0]]))
            with buffers(core, cos=[P, TX, AD], sin=[P, TX, AD], gq=[P, AD], gk=[P, AD]) as b:
                table = [(b.cos[:, t], b.sin[:, t]) for t in range(TX)] + [None] * TC
                view = lambda x, t: x[:, t].rearrange("p (h w) -> p h w", w=AD)
                head_norms(core, k, "heads2",
                           [(view(m.q, t), b.gq[:], table[t]) for t in range(TX)] +
                           [(view(a.keys, t), b.gk[:], table[t]) for t in range(TK)],
                           AD, (0, AD, pair_halves),
                           [(b.cos[:], args.cos_gqa.rearrange("(t p) w -> p t w", p=P)),
                            (b.sin[:], args.sin_gqa.rearrange("(t p) w -> p t w", p=P)),
                            (b.gq[:], on_all(args.q_norm_g_2)), (b.gk[:], on_all(args.k_norm_g_2))])
            attention(core, k, "attn2", m.q[:], AKV, AH // AKV, AD, a.keys[:],
                      lambda t, g: a.values[:, t, ds(g * AD, AD)], lambda t, h: m.q[:, t, ds(h * AD, AD)], AD)
        y = m.raw[:].rearrange("p c n -> p (c n)")[:, 0:TX * DS].rearrange("p (t n) -> p t n", t=TX)
        with buffers(core, xs=[P, TK, DS]) as c:
            n = 2 * SH
            with buffers(core, a=[P, TK, n], dt=[P, TK, n], running=[P, TK, n], fallen=[P, TK, n], total=[P, TK, n],
                         to_end=[P, TK, n], whole=[P, TK, n], grown=[P, TX, n],
                         others={"raw_dt": m.raw_dt}) as w:
                with buffers(core, b_rows=[P, TK, SG, SN]) as e:
                    convolve(core, k, m.raw[:], c.xs[:], e.b_rows[:], args.conv_w_2, args.conv_b_2)
                    step_sizes(core, k, w, args)
                    carry_states(core, k, w, m.raw[:], c.xs[:], e.b_rows[:], y)
                within_chunks(core, k, w, m.raw[:], c.xs[:], y)
            state_output(core, k, c.xs[:], y, m.z[:], args)
        project_out(core, k, "out2", lambda t, i: y[:, t, i * P:(i + 1) * P] if i < DS // P else
                    m.q[:, t, i * P - DS:(i + 1) * P - DS], MIX2, args.w_out_2[0], k.rows2, ALPHA2)
    layer_norm(core, k, "ln1", args.ln1_g_2, args.ln1_b_2)


def build(nc, **tensors):
    args = record(**tensors)
    with ExitStack() as stack:
        core = core_state(nc, stack)
        others = {
            "args": args,
            "slot_rows1": nc.dram_tensor("slot_rows1", [most_blocks(L, K1, E1) * P, D], F32).ap(),
            "slot_rows2": nc.dram_tensor("slot_rows2", [most_blocks(L, K2, E2) * P, D], F32).ap(),
            "slots_cleared": stack.enter_context(nc.semaphore("slots_cleared")),
            "rows1": nc.dram_tensor("rows1", [2, 6 * D], F32).ap(),
            "rows2": nc.dram_tensor("rows2", [2, 6 * D], F32).ap(),
        }
        k = stack.enter_context(buffers(
            core, others=others, x=[P, TX, D], ident=[P, P], ones=[P, P], upto=[P, P], after=[P, P], before=[P, P],
            zeros=[P, D // 4], eps=[P, 1], one=[P, 1], numbers=[P, 64], cols1=[P, 6 * DC, 2], cols2=[P, 6 * DC, 2],
            scale1=[P, DC], scale1c=[P, DC], scale1f=[P, DC], scale2=[P, DC], scale2c=[P, DC], scale2f=[P, DC]))
        setup(core, k, args)
        modulation(core, k, "mod1", args.c, args.c_ctx, args.w_ada[0], args.b_ada[0], k.cols1, k.rows1)
        modulation(core, k, "mod2", args.c_2, args.c_ctx_2, args.w_mod_2[0], args.b_mod_2[0], k.cols2, k.rows2)
        part = lambda cols, i, which: cols[:, i * DC:(i + 1) * DC, which]
        scale_columns(core, k, "scales", [
            (k.scale1[:], args.g_attn[0], part(k.cols1, 1, 0)), (k.scale1c[:], args.g_attn[0], part(k.cols1, 1, 1)),
            (k.scale1f[:], args.g_ffn[0], part(k.cols1, 4, 0)), (k.scale2[:], None, part(k.cols2, 1, 0)),
            (k.scale2c[:], None, part(k.cols2, 1, 1)), (k.scale2f[:], None, part(k.cols2, 4, 0))])
        first_mixer(core, k, args)
        first_experts(core, k, args)
        second_mixer(core, k, args)
        second_experts(core, k, args)
        finish(core, k, args)


def finish(core, k, args):
    with stage(core, "store", "stored") as (block, s):
        @block.sync
        def _(sync):
            sync.dma_start(args.out[0].rearrange("(t p) d -> p t d", p=P), k.x[:]).then_inc(s.stored, 16)
            sync.wait_ge(s.stored, 16)


def rotary_tables(width, paired):
    n = width // 4
    inv = np.power(np.float32(10000.0), -np.arange(n, dtype=np.float32) / np.float32(n)).astype(np.float32)
    at = np.arange(L)
    row = (at // GRID_W).astype(np.float32)[:, None] * inv
    col = (at % GRID_W).astype(np.float32)[:, None] * inv
    if paired:
        angle = np.repeat(np.concatenate([row, col], -1), 2, axis=-1)
        sign = np.tile(np.array([-1.0, 1.0]), width // 2)
    else:
        angle = np.concatenate([row, row, col, col], -1)
        sign = np.tile(np.repeat(np.array([-1.0, 1.0]), n), 2)
    return np.cos(angle).astype(np.float32), (np.sin(angle) * sign).astype(np.float32)


INPUTS = """x c ctx c_ctx g_attn g_ffn w_ada b_ada w_in g_q_lora w_q_up g_q_head g_kv_lora w_kv_up g_k_head
ret_decay_logit g_ret_out w_out w_router b_router w_mlp1 b_mlp1 w_mlp2 b_mlp2 c_2 ctx_2 c_ctx_2 w_mod_2 b_mod_2 w_in_2
conv_w_2 conv_b_2 dt_bias_2 a_log_2 d_skip_2 ssd_norm_g_2 q_norm_g_2 k_norm_g_2 w_out_2 ln1_g_2 ln1_b_2 w_rg_2 b_rg_2
w_re_2 b_re_2 w_gate_2 w_up_2 w_down_2 ln2_g_2 ln2_b_2""".split()


def kernel(**inputs):
    import concourse.bacc as bacc
    from concourse.bass_utils import run_bass_kernel_spmd

    nc = bacc.Bacc("TRN2", target_bir_lowering=False, num_devices=1)
    arrays = {name: np.ascontiguousarray(inputs[name]) for name in INPUTS}
    for name, width, paired in (("mla", ROPE, False), ("ret", RDK, False), ("gqa", AD, True)):
        arrays["cos_" + name], arrays["sin_" + name] = rotary_tables(width, paired)
    tensors = {name: nc.dram_tensor("in_" + name, a.shape, mybir.dt.from_np(a.dtype), kind="ExternalInput").ap()
               for name, a in arrays.items()}
    out = nc.dram_tensor("out_x", (1, L, D), F32, kind="ExternalOutput").ap()
    build(nc, out=out, **tensors)
    result = run_bass_kernel_spmd(nc, [{"in_" + name: a for name, a in arrays.items()}], core_ids=[0])
    return result.results[0]["out_x"]
```

```python
from collections import namedtuple
from contextlib import ExitStack, contextmanager

import numpy as np

import concourse.bass as bass
from concourse import mybir

F32 = mybir.dt.float32
F32R = mybir.dt.float32r
I32 = mybir.dt.int32
U32 = mybir.dt.uint32
ALU = mybir.AluOpType
ACT = mybir.ActivationFunctionType
AX = mybir.AxisListType.X
ds = bass.ds

P = 128
D = 1024
DC = D // P
L = 512
LC = 256
TX = L // P
TC = LC // P
TK = TX + TC
GRID_W = 64
EPS = 1e-6
BANK = 512
SLOTS = 3
BIG = 3.0e38
SK = DC // 2

H1, NOPE, ROPE, VD = 8, 64, 32, 64
QK = NOPE + ROPE
QL, KVL = 256, 128
RH, RDK, RDV = 4, 64, 128
O_KV = QL
O_PE = O_KV + KVL
O_RQ = O_PE + ROPE
O_RK = O_RQ + RH * RDK
O_RV = O_RK + RH * RDK
O_RG = O_RV + RH * RDV
DIN1 = O_RG + RH * RDV
MIX1 = H1 * VD + RH * RDV
E1, K1, FF1 = 32, 4, 1024
LIMIT, ALPHA = 7.0, 1.702

SH, SP_, SG, SN = 16, 64, 2, 128
SR = SH // SG
DS = SH * SP_
TAPS = 5
DXBC = DS + 2 * SG * SN
AH, AKV, AD = 16, 4, 64
O_Q2 = DS
O_XBC = O_Q2 + AH * AD
O_DT = O_XBC + DXBC
O_K2 = O_DT + 2 * SH
O_V2 = O_K2 + AKV * AD
DIN2 = O_V2 + AKV * AD
MIX2 = DS + AH * AD
MG, ME = 4, 4
E2, K2, FF2 = MG * ME, 2, 256
ALPHA2 = 2.0 ** 0.25


def most_blocks(tokens, top, experts):
    return (tokens * top) // P + experts


def record(**fields):
    return namedtuple("Record", list(fields))(**fields)


class Steps:

    def __init__(self, engine, semaphore):
        self.engine, self.semaphore, self.count = engine, semaphore, 0

    def __call__(self, instruction):
        self.count += 1
        instruction.then_inc(self.semaphore, 1)
        self.engine.wait_ge(self.semaphore, self.count)

    def restart(self):
        self.engine.sem_clear(self.semaphore)
        self.count = 0

    def reach(self, instruction, semaphore, value):
        instruction.then_inc(semaphore, 1)
        self.engine.wait_ge(semaphore, value)


class Ring:

    def __init__(self, slots, loaded):
        self.slots, self.loaded = slots, loaded
        self.count = [0] * SLOTS
        self.ahead = 0

    def load(self, engine, slot, source):
        _, k, n = source.shape
        engine.dma_start(self.slots[:, slot, 0:k, 0:n], source).then_inc(self.loaded[slot], 16)
        self.count[slot] += 16


class Core:

    def __init__(self, nc, stack, halves, psum, ring):
        self.nc, self.stack, self.halves, self.psum, self.ring = nc, stack, halves, psum, ring
        self.stages = 0


def core_state(nc, stack):
    free = sorted(nc.free_semaphores)
    halves = [free[-48:-24], free[-24:]]
    psum = stack.enter_context(nc.psum_tensor("psum", [P, 8, BANK], F32))
    slots = stack.enter_context(nc.sbuf_tensor("weight_slots", [P, SLOTS, DC, BANK], F32))
    loaded = [stack.enter_context(nc.semaphore(f"weights_loaded{i}")) for i in range(SLOTS)]
    return Core(nc, stack, halves, psum, Ring(slots, loaded))


@contextmanager
def stage(core, name, *signals, pool_dma=(), from_one=()):
    nc = core.nc
    mine, other = core.halves[core.stages % 2], core.halves[1 - core.stages % 2]
    first = core.stages == 0
    core.stages += 1
    assert len(signals) <= len(mine)
    with ExitStack() as stack:
        found = {s: stack.enter_context(nc.semaphore(f"{name}_{s}", num=n)) for s, n in zip(signals, mine)}
        found.update({s: core.stack.enter_context(nc.semaphore(f"{name}_{s}")) for s in pool_dma})
        block = stack.enter_context(nc.Block(no_gpsimd_drain=True))
        if not first:
            @block.sync
            def _(sync):
                sync.sem_clear(range(other[0], other[-1] + 1))
        if from_one:
            @block.sync
            def _(sync):
                for signal in from_one:
                    sync.sem_inc(found[signal], 1)
        yield block, record(**found)


@contextmanager
def buffers(core, others=None, **shapes):
    with ExitStack() as stack:
        made = dict(others or {})
        for name, shape in shapes.items():
            kind = F32
            if not isinstance(shape[-1], int):
                *shape, kind = shape
            made[name] = stack.enter_context(core.nc.sbuf_tensor(f"{name}_{core.nc.next_id()}", list(shape), kind))
        yield record(**made)


def spread(ap, axis, count):
    ap = ap.unsqueeze(axis)
    shape = list(ap.shape)
    shape[axis] = count
    return ap.to_broadcast(shape)


def by_column(vector):
    return vector.rearrange("(m p) -> p m", p=P)


def on_all(row, parts=P):
    return row.to_broadcast([parts, row.shape[1]])




def setup(core, k, args):
    nc = core.nc
    with stage(core, "setup", "filled", "selected", "rows_loaded", "zeroed") as (block, s):
        @block.sync
        def _(sync):
            sync.dma_start(k.x[:], args.x[0].rearrange("(t p) d -> p t d", p=P)).then_inc(s.rows_loaded, 16)
            sync.wait_ge(s.rows_loaded, 16)
            sync.wait_ge(s.zeroed, 1)

        @block.gpsimd
        def _(pool):
            pool.memset(k.zeros[:], 0.0).then_inc(s.zeroed, 1)
            pool.memset(k.ident[:], 0.0).then_inc(s.filled, 1)
            pool.memset(k.ones[:], 1.0).then_inc(s.filled, 1)
            pool.memset(k.eps[:], EPS).then_inc(s.filled, 1)
            pool.memset(k.one[:], 1.0).then_inc(s.filled, 1)
            pool.iota(k.numbers[:], [[1, 64]], base=0, channel_multiplier=0,
                      allow_small_or_imprecise_dtypes=True).then_inc(s.filled, 1)
            pool.wait_ge(s.filled, 5)
            pool.affine_select(out=k.ident[:], in_=k.ident[:], compare_op=ALU.not_equal, fill=1.0, base=0,
                               pattern=[[-1, P]], channel_multiplier=1).then_inc(s.selected, 1)
            pool.affine_select(out=k.upto[:], in_=k.ones[:], compare_op=ALU.is_ge, fill=0.0, base=0,
                               pattern=[[1, P]], channel_multiplier=-1).then_inc(s.selected, 1)
            pool.affine_select(out=k.after[:], in_=k.ones[:], compare_op=ALU.is_ge, fill=0.0, base=0,
                               pattern=[[-1, P]], channel_multiplier=1).then_inc(s.selected, 1)
            pool.affine_select(out=k.before[:], in_=k.ones[:], compare_op=ALU.is_gt, fill=0.0, base=0,
                               pattern=[[1, P]], channel_multiplier=-1).then_inc(s.selected, 1)
            pool.wait_ge(s.selected, 4)


def clear_slots(k):
    def go(engine):
        view = k.slot_rows.rearrange("(p b) d -> p (b d)", p=P).rearrange("p (n d) -> p n d", d=D // 4)
        engine.dma_start(view, spread(k.zeros[:], 1, view.shape[1])).then_inc(k.slots_cleared, 16)
    return go


def modulation(core, k, name, c, c_ctx, weights, bias, columns, rows_dram, following=None):
    nc, ring, psum = core.nc, core.ring, core.psum
    WHOLE = 3
    SK = DC - WHOLE
    n = 6 * D
    chunks = n // BANK
    per = 2 * SLOTS
    turns = chunks // per
    by_chunk = lambda v: v.rearrange("(p k) n -> p k n", k=DC)
    w = by_chunk(weights)
    ahead, ring.ahead = ring.ahead, 0
    base = list(ring.count)
    for j in range(ahead):
        base[j] -= 16
    with buffers(core, cin=[P, 2, DC], act=[P, 2, DC], high=[P, 2, DC, F32R], low=[P, 2, DC, F32R], brow=[2, n],
                 row=[2, n], w_high=[P, SLOTS, SK, BANK, F32R], w_low=[P, SLOTS, SK, BANK, F32R]) as b, \
            stage(core, name, "c_loaded", "c_ready", "c_high", "c_split", "b_loaded", "high_made", "low_made", "summed",
                  "added", "turned", "kept", "stored", from_one=("summed", "added", "high_made", "low_made")) \
            as (block, s):
        @block.sync
        def _(sync):
            sync.dma_start(b.cin[:, 0], c.rearrange("o (p k) -> (o p) k", k=DC)).then_inc(s.c_loaded, 16)
            sync.dma_start(b.cin[:, 1], c_ctx.rearrange("(p k) -> p k", k=DC)).then_inc(s.c_loaded, 16)
            for j in range(ahead, SLOTS):
                ring.load(sync, j, w[:, :, j * BANK:(j + 1) * BANK])
            sync.dma_start(b.brow[:], on_all(bias.rearrange("(a n) -> a n", a=1), 2)).then_inc(s.b_loaded, 16)
            for j in range(SLOTS, 2 * SLOTS):
                sync.wait_ge(s.summed, j - SLOTS + 2)
                ring.load(sync, j % SLOTS, w[:, :, j * BANK:(j + 1) * BANK])
            with sync.Fori(1, turns) as i:
                for j in range(per):
                    sync.wait_ge(s.summed, i * per + (j - SLOTS + 2))
                    sync.dma_start(ring.slots[:, j % SLOTS], w[:, :, ds((i * per + j) * BANK, BANK)])\
                        .then_inc(ring.loaded[j % SLOTS], 16)
            for j in range(SLOTS):
                ring.count[j] += 32 * (turns - 1)
            if following is not None:
                ring.ahead = SLOTS
                for j in range(SLOTS):
                    sync.wait_ge(s.summed, chunks - SLOTS + j + 2)
                    ring.load(sync, j, by_chunk(following)[:, :, j * BANK:(j + 1) * BANK])
            sync.wait_ge(s.added, chunks + 1)
            sync.dma_start(rows_dram, b.row[:]).then_inc(s.stored, 16)
            sync.wait_ge(s.stored, 16)

        @block.scalar
        def _(act):
            act.wait_ge(s.c_loaded, 32)
            act.activation(b.act[:], b.cin[:], ACT.Silu).then_inc(s.c_ready, 1)
            act.wait_ge(s.c_ready, 1)
            act.copy(b.high[:], b.act[:]).then_inc(s.c_high, 1)
            with act.Fori(0, turns) as i:
                for j in range(per):
                    act.wait_ge(ring.loaded[j % SLOTS], i * 32 + (base[j % SLOTS] + 16 * (j // SLOTS + 1)))
                    act.wait_ge(s.summed, i * per + max(j - SLOTS + 2, 1))
                    act.copy(b.w_high[:, j % SLOTS], ring.slots[:, j % SLOTS, WHOLE:, :]).then_inc(s.high_made, 1)

        @block.tensor
        def _(pe):
            pe.wait_ge(s.c_ready, 1)
            pe.wait_ge(s.c_high, 1)
            pe.wait_ge(s.c_split, 1)
            with pe.Fori(0, turns) as i:
                for j in range(per):
                    out = psum[0:2, j % 2, :]
                    pe.wait_ge(ring.loaded[j % SLOTS], i * 32 + (base[j % SLOTS] + 16 * (j // SLOTS + 1)))
                    pe.wait_ge(s.added, i * per + max(j, 1))
                    for kc in range(WHOLE):
                        pe.matmul(out, b.act[:, :, kc], ring.slots[:, j % SLOTS, kc, :], start=kc == 0, stop=False)
                    pe.wait_ge(s.high_made, i * per + (j + 2))
                    for kc in range(SK):
                        for part in (b.high, b.low):
                            pe.matmul(out, part[:, :, WHOLE + kc], b.w_high[:, j % SLOTS, kc, :],
                                      start=False, stop=False)
                    pe.wait_ge(s.low_made, i * per + (j + 2))
                    for kc in range(SK):
                        mm = pe.matmul(out, b.high[:, :, WHOLE + kc], b.w_low[:, j % SLOTS, kc, :],
                                       start=False, stop=kc == SK - 1)
                    mm.then_inc(s.summed, 1)
            pe.wait_ge(s.added, chunks + 1)
            for m in range(n // P):
                mm = pe.transpose(psum[:, 2, 2 * m:2 * m + 2], b.row[:, m * P:(m + 1) * P], k.ident[0:2, 0:2])
            mm.then_inc(s.turned, 1)

        @block.vector
        def _(dve):
            dve.wait_ge(s.c_high, 1)
            dve.tensor_tensor(b.low[:], b.act[:], b.high[:].bitcast(F32), ALU.subtract).then_inc(s.c_split, 1)
            dve.wait_ge(s.b_loaded, 16)
            with dve.Fori(0, turns) as i:
                for j in range(per):
                    dve.wait_ge(s.high_made, i * per + (j + 2))
                    dve.tensor_tensor(b.w_low[:, j % SLOTS], ring.slots[:, j % SLOTS, WHOLE:, :],
                                      b.w_high[:, j % SLOTS].bitcast(F32), ALU.subtract).then_inc(s.low_made, 1)
                    dve.wait_ge(s.summed, i * per + (j + 2))
                    at = ds((i * per + j) * BANK, BANK)
                    dve.tensor_tensor(b.row[:, at], psum[0:2, j % 2, :], b.brow[:, at], ALU.add).then_inc(s.added, 1)
            dve.wait_ge(s.turned, 1)
            dve.tensor_copy(columns[:], psum[:, 2, 0:2 * (n // P)].rearrange("p (m c) -> p m c", c=2))\
                .then_inc(s.kept, 1)
            dve.wait_ge(s.kept, 1)


def scale_columns(core, k, name, pairs):
    with ExitStack() as stack:
        gains = [None if p[1] is None else stack.enter_context(
            core.nc.sbuf_tensor(f"gain_{core.nc.next_id()}", [P, DC], F32)) for p in pairs]
        with stage(core, name, "gains_loaded", "vector_step") as (block, s):
            @block.sync
            def _(sync):
                for gain, p in zip(gains, pairs):
                    if gain is not None:
                        sync.dma_start(gain[:], by_column(p[1]), allow_slow_non_contiguous=True).then_inc(s.gains_loaded, 16)

            @block.vector
            def _(dve):
                step = Steps(dve, s.vector_step)
                n = sum(g is not None for g in gains)
                if n:
                    dve.wait_ge(s.gains_loaded, 16 * n)
                for gain, (out, _, column) in zip(gains, pairs):
                    if gain is None:
                        step(dve.tensor_scalar(out, column, 1.0, None, ALU.add))
                    else:
                        step(dve.scalar_tensor_tensor(out=out, in0=column, scalar=1.0, in1=gain[:], op0=ALU.add,
                                                      op1=ALU.mult))


def norm_rows(core, k, name, sources, scratch):
    n = len(sources)
    with buffers(core, sums=[P, n], roots=[P, n], rates=[P, n]) as b, \
            stage(core, name, "scalar_step", "rooted", "vector_step") as (block, s):
        @block.scalar
        def _(act):
            step = Steps(act, s.scalar_step)
            for t, (src, _) in enumerate(sources):
                step(act.activation(scratch, src, ACT.Square, accum_out=b.sums[:, t:t + 1]))
            act.activation(b.roots[:], b.sums[:], ACT.Sqrt, scale=1.0 / D, bias=k.eps[:, 0:1]).then_inc(s.rooted, 1)

        @block.vector
        def _(dve):
            step = Steps(dve, s.vector_step)
            dve.wait_ge(s.rooted, 1)
            step(dve.reciprocal(b.rates[:], b.roots[:]))
            for t, (src, out) in enumerate(sources):
                step(dve.tensor_scalar(out, src, b.rates[:, t:t + 1], None, ALU.mult))


def to_features(core, k, name, groups, prefetch=None):
    nc, psum = core.nc, core.psum
    everything = [(tiles, m, out, scale, bias) for tiles, chunks, out, scale, bias in groups for m in range(chunks)]
    whole = [w for w in everything if not isinstance(w[2](w[1]), tuple)]
    split = [w for w in everything if isinstance(w[2](w[1]), tuple)]
    assert not split or len(split) == len(whole)
    work = [w for both in zip(whole, split) for w in both] if split else whole
    with buffers(core, turned=[P, 2, L]) as b, \
            stage(core, name, "turned", "kept_by_scalar", "kept_by_vector", "high_made", "low_made") as (block, s):
        if prefetch:
            @block.sync
            def _(sync):
                prefetch(sync)

        @block.tensor
        def _(pe):
            for w, (tiles, m, *_) in enumerate(work):
                if w >= 8:
                    pe.wait_ge(s.kept_by_vector if w % 2 else s.kept_by_scalar, (w - 8) // 2 + 1)
                for t, tile in enumerate(tiles):
                    mm = pe.transpose(psum[:, w % 8, t * P:(t + 1) * P], tile(m), k.ident[:])
                mm.then_inc(s.turned, 1)

        def keep(engine, w, vector, into=None):
            tiles, m, out, scale, bias = work[w]
            engine.wait_ge(s.turned, w + 1)
            src = psum[:, w % 8, 0:len(tiles) * P]
            target = out(m) if into is None else into
            if vector and bias is not None:
                ins = engine.tensor_scalar(target, src, scale(m), bias(m), ALU.mult, ALU.add)
            elif vector and scale is not None:
                ins = engine.tensor_scalar(target, src, scale(m), None, ALU.mult)
            elif vector:
                ins = engine.tensor_copy(target, src)
            elif scale is not None:
                ins = engine.activation(target, src, ACT.Identity, scale=scale(m),
                                        **({} if bias is None else {"bias": bias(m)}))
            else:
                ins = engine.copy(target, src)
            ins.then_inc(s.kept_by_vector if vector else s.kept_by_scalar, 1)

        def part(i):
            tiles, m, out, *_ = split[i]
            return b.turned[:, i % 2, 0:len(tiles) * P], out(m)

        @block.scalar
        def _(act):
            for w in range(0, len(work), 2):
                keep(act, w, False)
                if split:
                    src, (high, _) = part(w // 2)
                    act.wait_ge(s.kept_by_vector, w // 2 + 1)
                    act.copy(high, src).then_inc(s.high_made, 1)
            act.wait_ge(s.kept_by_scalar, (len(work) + 1) // 2)

        @block.vector
        def _(dve):
            def make_low(i):
                src, (high, low) = part(i)
                dve.wait_ge(s.high_made, i + 1)
                dve.tensor_tensor(low, src, high.bitcast(F32), ALU.subtract).then_inc(s.low_made, 1)

            for w in range(1, len(work), 2):
                i = w // 2
                if split and i >= 2:
                    dve.wait_ge(s.low_made, i - 1)
                keep(dve, w, True, part(i)[0] if split else None)
                if split and i:
                    make_low(i - 1)
            if split:
                make_low(len(split) - 1)
                dve.wait_ge(s.low_made, len(split))
            elif len(work) > 1:
                dve.wait_ge(s.kept_by_vector, len(work) // 2)


def features(b, m, lo, hi):
    q, i = divmod(m, DC)
    if i < SK:
        return b.whole[:, q * SK + i, lo:hi]
    return b.high[:, q * SK + i - SK, lo:hi], b.low[:, q * SK + i - SK, lo:hi]


def load_first(core, chunks):
    core.ring.ahead = min(SLOTS, len(chunks))

    def go(engine):
        for j in range(core.ring.ahead):
            core.ring.load(engine, j, chunks[j].source)
    return go


def project(core, k, name, chunks, evacuate, extra=(), vector_only=False, loads=None):
    nc, ring, psum = core.nc, core.ring, core.psum
    ahead, ring.ahead = ring.ahead, 0
    passes = [(j, p) for j, c in enumerate(chunks) for p in c.passes]
    last_group = max(p.group for _, p in passes)
    sharers = 1 if vector_only else 2
    start = list(ring.count)
    for j in range(ahead):
        start[j] -= 16
    done, n = [], 0
    for c in chunks:
        n += len(c.passes)
        done.append(n)
    finish = {p.group: i + 1 for i, (_, p) in enumerate(passes) if p.last}
    in_chunk = {p.group: j for j, p in passes if p.last}
    splitting = len(chunks[0].x) == 3
    with ExitStack() as stack:
        if splitting:
            w = stack.enter_context(buffers(core, high=[P, SK, BANK, F32R], low=[P, SK, BANK, F32R]))
        block, s = stack.enter_context(stage(core, name, "summed", "out_by_scalar", "out_by_vector", "high_made",
                                             "low_made", "scalar_step", "vector_step", *extra))

        @block.sync
        def _(sync):
            if loads:
                loads(sync, s)
            for j in range(ahead, len(chunks)):
                if j >= SLOTS:
                    sync.wait_ge(s.summed, done[j - SLOTS])
                ring.load(sync, j % SLOTS, chunks[j].source)

        @block.tensor
        def _(pe):
            for j, c in enumerate(chunks):
                slot = ring.slots[:, j % SLOTS]
                pe.wait_ge(ring.loaded[j % SLOTS], start[j % SLOTS] + 16 * (j // SLOTS + 1))
                ks = SK if splitting else c.source.shape[1]
                for p in c.passes:
                    if p.first and p.group >= 8:
                        by_vector = vector_only or p.group % 2
                        pe.wait_ge(s.out_by_vector if by_vector else s.out_by_scalar, (p.group - 8) // sharers + 1)
                    for kc in range(ks):
                        mm = pe.matmul(psum[:, p.group % 8, 0:p.width], *p.operands(c.x[0], slot, kc),
                                       start=p.first and kc == 0, stop=not splitting and p.last and kc == ks - 1)
                    if not splitting:
                        mm.then_inc(s.summed, 1)
                if splitting:
                    pe.wait_ge(s.high_made, j + 1)
                    pe.wait_ge(s.low_made, j + 1)
                    _, x_high, x_low = c.x
                    for p in c.passes:
                        for kc in range(SK):
                            for x, weights in ((x_high, w.high), (x_low, w.high), (x_high, w.low)):
                                mm = pe.matmul(psum[:, p.group % 8, 0:p.width], *p.operands(x, weights, kc),
                                               start=False, stop=p.last and kc == SK - 1 and weights is w.low)
                        mm.then_inc(s.summed, 1)

        def out(engine, which, finished, step):
            for j, c in enumerate(chunks):
                width = c.source.shape[2]
                slot = ring.slots[:, j % SLOTS, SK:, 0:width]
                if splitting and engine.engine == mybir.EngineType.Activation:
                    engine.wait_ge(ring.loaded[j % SLOTS], start[j % SLOTS] + 16 * (j // SLOTS + 1))
                    if j:
                        engine.wait_ge(s.summed, done[j - 1])
                    engine.copy(w.high[:, :, 0:width], slot).then_inc(s.high_made, 1)
                elif splitting:
                    engine.wait_ge(s.high_made, j + 1)
                    engine.tensor_tensor(w.low[:, :, 0:width], slot, w.high[:, :, 0:width].bitcast(F32),
                                         ALU.subtract).then_inc(s.low_made, 1)
                if which is None:
                    continue
                for group in range(which, last_group + 1, sharers):
                    if in_chunk[group] == j:
                        engine.wait_ge(s.summed, finish[group])
                        step.reach(evacuate(engine, s, group, psum[:, group % 8, :], step), finished,
                                   group // sharers + 1)

        if splitting or not vector_only:
            @block.scalar
            def _(act):
                out(act, None if vector_only else 0, s.out_by_scalar, Steps(act, s.scalar_step))

        @block.vector
        def _(dve):
            out(dve, 0 if vector_only else 1, s.out_by_vector, Steps(dve, s.vector_step))


def token_chunk(source, x, tiles, first_group, first=True, last=True):
    width = source.shape[2]
    return record(source=source, x=x, passes=[
        record(group=first_group + i, width=width, first=first, last=last,
               operands=lambda x, w, kc, t=t, width=width: (x[:, kc, t * P:(t + 1) * P], w[:, kc, 0:width]))
        for i, t in enumerate(tiles)])


def copy_out(engine, out, bank):
    if engine.engine == mybir.EngineType.Activation:
        return engine.copy(out, bank)
    return engine.tensor_copy(out, bank)


def rotate(step, dve, x, cos, sin, turned, sums, halves):
    for i in range(2):
        step(dve.tensor_tensor(halves(turned, i), halves(x, 1 - i), halves(sin, i), ALU.mult))
    step(dve.tensor_tensor(sums, x, cos, ALU.mult))
    step(dve.tensor_tensor(x, sums, turned, ALU.add))


def blocked_halves(width):
    q = width // 4

    def halves(view, i):
        return view.rearrange("p h (a b) -> p h a b", a=2)[:, :, :, i * q:(i + 1) * q]
    return halves


def pair_halves(view, i):
    return view.rearrange("p h (m b) -> p h m b", b=2)[:, :, :, i]


def latent_norms(core, k, px, pc):
    with buffers(core, sums=[P, TX + TK], roots=[P, TX + TK], rates=[P, TX + TK], junk=[P, QL]) as b, \
            stage(core, "latents", "scalar_step", "rooted", "vector_step") as (block, s):
        q = [px[:, t, 0:QL] for t in range(TX)]
        kv = [px[:, t, O_KV:O_PE] for t in range(TX)] + [pc[:, t, 0:KVL] for t in range(TC)]

        @block.scalar
        def _(act):
            step = Steps(act, s.scalar_step)
            for i, src in enumerate(q + kv):
                step(act.activation(b.junk[:, 0:src.shape[1]], src, ACT.Square, accum_out=b.sums[:, i:i + 1]))
            act.activation(b.roots[:, 0:TX], b.sums[:, 0:TX], ACT.Sqrt, scale=1.0 / QL,
                           bias=k.eps[:, 0:1]).then_inc(s.rooted, 1)
            act.activation(b.roots[:, TX:], b.sums[:, TX:], ACT.Sqrt, scale=1.0 / KVL,
                           bias=k.eps[:, 0:1]).then_inc(s.rooted, 1)

        @block.vector
        def _(dve):
            step = Steps(dve, s.vector_step)
            dve.wait_ge(s.rooted, 2)
            step(dve.reciprocal(b.rates[:], b.roots[:]))
            for i, src in enumerate(q + kv):
                step(dve.tensor_scalar(src, src, b.rates[:, i:i + 1], None, ALU.mult))


def head_norms(core, k, name, jobs, width, rope, loads):
    off, rw, halves = rope
    most = max(x.shape[1] for x, *_ in jobs)
    base, n = [], 0
    for x, *_ in jobs:
        base.append(n)
        n += x.shape[1]
    with buffers(core, squares=[P, 2, most * width], sums=[P, n], roots=[P, n], rates=[P, n],
                 turned=[P, most, rw], products=[P, most, rw]) as b, \
            stage(core, name, "tables_loaded", "squared", "reduced", "rooted", "vector_step") as (block, s):
        @block.sync
        def _(sync):
            for out, src in loads:
                sync.dma_start(out, src).then_inc(s.tables_loaded, 16)

        def sq(i):
            h = jobs[i][0].shape[1]
            return b.squares[:, i % 2, 0:h * width].rearrange("p (h w) -> p h w", w=width)

        @block.scalar
        def _(act):
            for i, (x, *_) in enumerate(jobs):
                if i >= 2:
                    act.wait_ge(s.reduced, i - 1)
                act.activation(sq(i), x, ACT.Square).then_inc(s.squared, 1)
            act.wait_ge(s.reduced, len(jobs))
            act.activation(b.roots[:], b.sums[:], ACT.Sqrt, scale=1.0 / width,
                           bias=k.eps[:, 0:1]).then_inc(s.rooted, 1)

        @block.vector
        def _(dve):
            step = Steps(dve, s.vector_step)
            for i, (x, *_) in enumerate(jobs):
                dve.wait_ge(s.squared, i + 1)
                dve.tensor_reduce(b.sums[:, base[i]:base[i] + x.shape[1]], sq(i), AX, ALU.add).then_inc(s.reduced, 1)
            dve.wait_ge(s.rooted, 1)
            step(dve.reciprocal(b.rates[:], b.roots[:]))
            dve.wait_ge(s.tables_loaded, 16 * len(loads))
            for i, (x, gain, table) in enumerate(jobs):
                h = x.shape[1]
                step(dve.tensor_tensor(x, x, spread(b.rates[:, base[i]:base[i] + h], 2, width), ALU.mult))
                step(dve.tensor_tensor(x, x, spread(gain, 1, h), ALU.mult))
                if table is not None:
                    cos, sin = (spread(v, 1, h) for v in table)
                    rotate(step, dve, x[:, :, off:off + rw], cos, sin, b.turned[:, 0:h], b.products[:, 0:h], halves)


def attention(core, k, name, q, kv_groups, rep, dim, keys, values, out, vdim):
    nc, psum = core.nc, core.psum
    n_keys = TK * P
    groups = 4 if rep == 1 else 2
    per = groups * rep
    loops = kv_groups // groups
    scale = float(dim) ** -0.5
    flat = psum[:, :, :].rearrange("p b n -> p (b n)")
    rows_ps = [flat[:, 0:n_keys], flat[:, 2 * BANK:2 * BANK + n_keys]]
    keys_ps = [psum[:, 4, :], psum[:, 5, :]]
    turn_ps = psum[:, 6, :]
    o_ps = psum[:, 7, 0:TX * (vdim + 1)].rearrange("p (t w) -> p t w", t=TX)
    probs = core.ring.slots[:, 0].rearrange("p k n -> p (k n)")[:, 0:TK * L].rearrange("p (j n) -> p j n", j=TK)
    signals = ("q_staged", "k_staged", "v_staged", "exped", "q_turned", "k_turned", "scored", "shifted_turned", "key_scored",
               "weighted", "q_kept", "k_kept", "peaked", "shifted", "shifted_high_kept", "shifted_low_kept", "put")
    with buffers(core, q_head=[P, 2, TX, dim + 1], k_head=[P, TK, dim], v_head=[P, 2, TK, vdim + 1],
                 q_high=[dim, L, F32R], q_low=[dim, L, F32R], shifted_high=[dim + 1, L, F32R],
                 shifted_low=[dim + 1, L, F32R], k_high=[dim + 1, 2, n_keys, F32R], k_low=[dim + 1, 2, n_keys, F32R], peaks=[P, TX], shares=[P, TX]) as b, \
            stage(core, name, *signals, "ones_set", "vector_step", "begun", from_one=signals) as (block, s):
        def next_head(n):
            n1 = (n + 1) % per
            return n1, n1 % rep == 0

        @block.gpsimd
        def _(pool):
            for copy, fill in ((b.k_high, k.ones[:]), (b.k_low, k.zeros[:, 0:P])):
                row = copy[dim:dim + 1].rearrange("p c (t n) -> p (c t) n", n=P)
                pool.tensor_copy(row, spread(fill[dim:dim + 1], 1, 2 * TK)).then_inc(s.ones_set, 1)
                pool.wait_ge(s.ones_set, 1 if copy is b.k_high else 2)
            pool.memset(b.v_head[:, :, :, vdim:], 1.0).then_inc(s.ones_set, 1)
            pool.wait_ge(s.ones_set, 3)

            def stage_values(group, copy):
                pool.tensor_copy(b.v_head[:, copy, :, 0:vdim], values(group)).then_inc(s.v_staged, 1)

            stage_values(0, 0)
            pool.wait_ge(s.v_staged, 2)
            stage_values(1, 1)
            with pool.Fori(0, kv_groups // 2 - 1) as i:
                for copy in range(2):
                    pool.wait_ge(s.weighted, i * (2 * rep) + ((copy + 1) * rep + 1))
                    pool.wait_ge(s.v_staged, i * 2 + (copy + 3))
                    stage_values(i * 2 + (copy + 2), copy)
            pool.wait_ge(s.v_staged, kv_groups + 1)

        @block.tensor
        def _(pe):
            def turn_queries(head, n):
                pe.wait_ge(s.q_staged, head + 2)
                pe.wait_ge(s.shifted_low_kept, head if not isinstance(head, int) else max(head, 1))
                pe.sem_inc(s.begun, 1)
                for t in range(TX):
                    mm = pe.transpose(turn_ps[0:dim, t * P:(t + 1) * P], b.q_head[:, n % 2, t, 0:dim], k.ident[:])
                mm.then_inc(s.q_turned, 1)

            def turn_keys(head, group):
                pe.wait_ge(s.k_staged, group + 2)
                pe.wait_ge(s.peaked, head * TX if not isinstance(head, int) else max(head * TX, 1))
                pe.sem_inc(s.begun, 1)
                for t in range(TK):
                    mm = pe.transpose(rows_ps[0][0:dim, t * P:(t + 1) * P], b.k_head[:, t, :], k.ident[:])
                mm.then_inc(s.k_turned, 1)

            def row_scores(head, group, n, t):
                if t == 0:
                    pe.wait_ge(s.q_kept, head + 2)
                    pe.wait_ge(s.k_kept, group + 2)
                pe.wait_ge(s.peaked, head * TX + max(t, 1))
                for c in range(0, n_keys, BANK):
                    e = min(c + BANK, n_keys)
                    for part, (query, key) in enumerate(((b.q_high, b.k_high), (b.q_high, b.k_low),
                                                         (b.q_low, b.k_high))):
                        mm = pe.matmul(rows_ps[t % 2][:, c:e], query[:, t * P:(t + 1) * P],
                                       key[0:dim, n // rep % 2, c:e], start=part == 0, stop=part == 2)
                mm.then_inc(s.scored, 1)

            def turn_shifted(head, n, queries_turned):
                pe.wait_ge(s.shifted, head + 2)
                pe.wait_ge(s.q_kept, head + queries_turned)
                pe.sem_inc(s.begun, 1)
                for t in range(TX):
                    mm = pe.transpose(turn_ps[0:dim + 1, t * P:(t + 1) * P], b.q_head[:, n % 2, t, :], k.ident[:])
                mm.then_inc(s.shifted_turned, 1)

            def shifted_scores(head, n, j):
                if j == 0:
                    pe.wait_ge(s.shifted_high_kept, head + 2)
                    pe.wait_ge(s.shifted_low_kept, head + 2)
                pe.wait_ge(s.exped, head * TK + max(j, 1))
                for part, (key, query) in enumerate(((b.k_high, b.shifted_high), (b.k_high, b.shifted_low),
                                                     (b.k_low, b.shifted_high))):
                    mm = pe.matmul(keys_ps[j % 2], key[:, n // rep % 2, j * P:(j + 1) * P], query[:],
                                   start=part == 0, stop=part == 2)
                mm.then_inc(s.key_scored, 1)

            def weigh(head, group, n, tiles):
                if n % rep == 0:
                    pe.wait_ge(s.v_staged, group + 2)
                pe.wait_ge(s.exped, head * TK + TK + 1)
                pe.wait_ge(s.put, head + 1)
                for t in tiles:
                    for j in range(TK):
                        mm = pe.matmul(o_ps[:, t, :], probs[:, j, t * P:(t + 1) * P], b.v_head[:, n // rep % 2, j, :],
                                       start=j == 0, stop=j == TK - 1)
                if t == TX - 1:
                    mm.then_inc(s.weighted, 1)

            def body(i, last):
                for n in range(per):
                    head = i * per + n
                    n1, opens = next_head(n)
                    group1 = i * groups + (n + 1) // rep
                    more, more2 = not (last and n + 1 >= per), not (last and n + 2 >= per)
                    n2, group2 = (n + 2) % per, i * groups + (n + 2) // rep
                    shifted_scores(head, n, 0)
                    shifted_scores(head, n, 1)
                    for t in range(TX):
                        if t + 2 < TK:
                            shifted_scores(head, n, t + 2)
                        if more:
                            row_scores(head + 1, group1, n1, t)
                    if more2:
                        turn_queries(head + 2, n2)
                        if n2 % rep == 0:
                            turn_keys(head + 2, group2)
                    weigh(head, i * groups + n // rep, n, range(TX - 1))
                    if more:
                        turn_shifted(head + 1, n1, 3 if more2 else 2)
                    weigh(head, i * groups + n // rep, n, [TX - 1])

            turn_queries(0, 0)
            turn_keys(0, 0)
            for t in range(TX):
                row_scores(0, 0, 0, t)
            turn_queries(1, 1)
            if rep == 1:
                turn_keys(1, 1)
            pe.wait_ge(s.ones_set, 3)
            turn_shifted(0, 0, 3)
            with pe.Fori(0, loops - 1) as i:
                body(i, False)
            body(loops - 1, True)

        @block.scalar
        def _(act):
            def stage_queries(head, n):
                if not isinstance(head, int) or head > 1:
                    act.wait_ge(s.shifted_turned, head)
                act.copy(b.q_head[:, n % 2, :, 0:dim], q[:, :, ds(head * dim, dim)]).then_inc(s.q_staged, 1)

            def stage_keys(group):
                act.wait_ge(s.k_turned, group + 1)
                act.copy(b.k_head[:], keys[:, :, ds(group * dim, dim)]).then_inc(s.k_staged, 1)

            def keep_shifted(head):
                act.wait_ge(s.shifted_turned, head + 2)
                act.copy(b.shifted_high[:], turn_ps[0:dim + 1, :]).then_inc(s.shifted_high_kept, 1)

            def body(i, last):
                for n in range(per):
                    head = i * per + n
                    n2, group2 = (n + 2) % per, i * groups + (n + 2) // rep
                    staging = not (last and n + 2 >= per)
                    for j in range(TK):
                        act.wait_ge(s.key_scored, head * TK + (j + 2))
                        act.activation(probs[:, j], keys_ps[j % 2], ACT.Exp, scale=scale).then_inc(s.exped, 1)
                        if staging and j == 1:
                            stage_queries(head + 2, n2)
                        if staging and n2 % rep == 0 and j == 2:
                            stage_keys(group2)
                    if not (last and n == per - 1):
                        keep_shifted(head + 1)

            stage_queries(0, 0)
            stage_keys(0)
            stage_queries(1, 1)
            if rep == 1:
                stage_keys(1)
            keep_shifted(0)
            with act.Fori(0, loops - 1) as i:
                body(i, False)
            body(loops - 1, True)
            act.wait_ge(s.exped, kv_groups * rep * TK + 1)

        @block.vector
        def _(dve):
            step = Steps(dve, s.vector_step)

            def keep_queries(head, group, n):
                dve.wait_ge(s.q_turned, head + 2)
                dve.wait_ge(s.scored, head * TX + 1)
                step(dve.tensor_copy(b.q_high[:], turn_ps[0:dim, :]))
                dve.tensor_tensor(b.q_low[:], turn_ps[0:dim, :], b.q_high[:].bitcast(F32), ALU.subtract)\
                    .then_inc(s.q_kept, 1)
                if n % rep == 0:
                    dve.wait_ge(s.k_turned, group + 2)
                    step(dve.tensor_copy(b.k_high[0:dim, n // rep % 2], rows_ps[0][0:dim, :]))
                    dve.tensor_tensor(b.k_low[0:dim, n // rep % 2], rows_ps[0][0:dim, :],
                                      b.k_high[0:dim, n // rep % 2].bitcast(F32), ALU.subtract).then_inc(s.k_kept, 1)

            def shift(head, n):
                for t in range(TX):
                    dve.wait_ge(s.scored, head * TX + (t + 2))
                    step.reach(dve.tensor_reduce(b.peaks[:, t:t + 1], rows_ps[t % 2], AX, ALU.max), s.peaked,
                               head * TX + (t + 2))
                dve.tensor_scalar(b.q_head[:, n % 2, :, dim], b.peaks[:], -1.0, None, ALU.mult)\
                    .then_inc(s.shifted, 1)

            def keep_shifted_low(head):
                dve.wait_ge(s.shifted_high_kept, head + 2)
                dve.tensor_tensor(b.shifted_low[:], turn_ps[0:dim + 1, :], b.shifted_high[:].bitcast(F32),
                                  ALU.subtract).then_inc(s.shifted_low_kept, 1)

            def body(i, last):
                for n in range(per):
                    head = i * per + n
                    n1, opens = next_head(n)
                    more, more2 = not (last and n + 1 >= per), not (last and n + 2 >= per)
                    if more:
                        shift(head + 1, n1)
                    if more2:
                        keep_queries(head + 2, i * groups + (n + 2) // rep, (n + 2) % per)
                    if more:
                        keep_shifted_low(head + 1)
                    dve.wait_ge(s.weighted, head + 2)
                    step(dve.reciprocal(b.shares[:], o_ps[:, :, vdim]))
                    dve.tensor_tensor(out(head), o_ps[:, :, 0:vdim], spread(b.shares[:], 2, vdim), ALU.mult)\
                        .then_inc(s.put, 1)

            keep_queries(0, 0, 0)
            shift(0, 0)
            keep_queries(1, 2 // (2 * rep), 1)
            keep_shifted_low(0)
            with dve.Fori(0, loops - 1) as i:
                step.restart()
                body(i, False)
            step.restart()
            body(loops - 1, True)
            dve.wait_ge(s.put, kv_groups * rep + 1)


def retention(core, k, px, pc, mix, decay):
    nc, psum = core.nc, core.psum
    W, WC = 2 * L - P, L + P
    flat = psum[:, :, :].rearrange("p b n -> p (b n)")
    k_ps, q_ps, o_ps = flat[:, 4 * BANK:4 * BANK + TK * P], psum[:, 7, :], psum[:, 6, :]
    with ExitStack() as inner:
        b = inner.enter_context(buffers(
            core, lg_in=[P, 2 * RH], lg=[P, 2 * RH], t0=[P, 2 * RH], gap=[P, W], dist=[P, W], fwd=[P, W], bwd=[P, W],
            gap_cf=[P, WC], gap_cb=[P, WC], pw=[P, 2, W], pwc=[P, 2, WC], both=[P, W], both_c=[P, WC],
            q_head=[P, TX, RDK], k_head=[P, TK, RDK], q_turned=[RDK, L], k_turned=[RDK, TK * P], weights=[P, TK, L],
            cos=[P, TX, RDK], sin=[P, TX, RDK], turned=[P, 2 * RH, RDK], products=[P, 2 * RH, RDK]))
        with stage(core, "ret_prep", "loaded", "patterned", "logs", "vector_step", "scalar_step") as (block, s):
            @block.sync
            def _(sync):
                sync.dma_start(b.lg_in[:], on_all(decay.rearrange("a d h -> a (d h)"))).then_inc(s.loaded, 16)
                sync.dma_start(b.cos[:], k.args.cos_ret.rearrange("(t p) w -> p t w", p=P)).then_inc(s.loaded, 16)
                sync.dma_start(b.sin[:], k.args.sin_ret.rearrange("(t p) w -> p t w", p=P)).then_inc(s.loaded, 16)

            @block.gpsimd
            def _(pool):
                pool.iota(b.gap[:], [[1, W]], base=-(L - P), channel_multiplier=-1,
                          allow_small_or_imprecise_dtypes=True).then_inc(s.patterned, 1)
                pool.iota(b.gap_cf[:], [[1, WC]], base=LC - P, channel_multiplier=-1,
                          allow_small_or_imprecise_dtypes=True).then_inc(s.patterned, 1)
                pool.iota(b.gap_cb[:], [[-1, WC]], base=L + P, channel_multiplier=1,
                          allow_small_or_imprecise_dtypes=True).then_inc(s.patterned, 1)

            @block.scalar
            def _(act):
                step = Steps(act, s.scalar_step)
                act.wait_ge(s.loaded, 48)
                step(act.activation(b.t0[:], b.lg_in[:], ACT.Abs))
                step(act.activation(b.t0[:], b.t0[:], ACT.Exp, scale=-1.0))
                act.activation(b.t0[:], b.t0[:], ACT.Ln, bias=k.one[:, 0:1]).then_inc(s.logs, 1)

            @block.vector
            def _(dve):
                step = Steps(dve, s.vector_step)
                dve.wait_ge(s.patterned, 3)
                step(dve.scalar_tensor_tensor(out=b.dist[:], in0=b.gap[:], scalar=-1.0, in1=b.gap[:], op0=ALU.mult,
                                              op1=ALU.max))
                step(dve.tensor_scalar(b.fwd[:], b.gap[:], 0.0, None, ALU.is_ge))
                step(dve.tensor_scalar(b.bwd[:], b.gap[:], 0.0, None, ALU.is_le))
                dve.wait_ge(s.logs, 1)
                step(dve.scalar_tensor_tensor(out=b.lg[:], in0=b.lg_in[:], scalar=0.0, in1=b.t0[:], op0=ALU.min,
                                              op1=ALU.subtract))
                halves = blocked_halves(RDK)
                for t in range(TX):
                    x = px[:, t, O_RQ:O_RV].rearrange("p (h w) -> p h w", w=RDK)
                    cos, sin = spread(b.cos[:, t], 1, 2 * RH), spread(b.sin[:, t], 1, 2 * RH)
                    rotate(step, dve, x, cos, sin, b.turned[:], b.products[:], halves)

        rk_c = O_PE + ROPE - O_KV
        with stage(core, "retention", "staged", "powered", "mixed", "k_turned", "k_kept", "q_turned", "q_kept",
                   "scored", "weighed", "summed", "put", "vector_step", "begun",
                  from_one=("staged", "powered", "mixed", "k_turned", "k_kept", "q_turned", "q_kept", "scored", "weighed", "summed", "put")) as (block, s):
            @block.sync
            def _(sync):
                clear_slots(k)(sync)

            @block.scalar
            def _(act):
                with act.Fori(0, RH) as h:
                    act.wait_ge(s.k_turned, h + 1)
                    act.wait_ge(s.q_turned, h + 1)
                    act.copy(b.k_head[:, 0:TX], px[:, :, ds(h * RDK + O_RK, RDK)]).then_inc(s.staged, 1)
                    act.copy(b.k_head[:, TX:], pc[:, :, ds(h * RDK + rk_c, RDK)]).then_inc(s.staged, 1)
                    act.copy(b.q_head[:], px[:, :, ds(h * RDK + O_RQ, RDK)]).then_inc(s.staged, 1)
                    act.wait_ge(s.mixed, h + 1)
                    for d in range(2):
                        lg = b.lg[:, ds(h + d * RH, 1)]
                        act.activation(b.pw[:, d], b.dist[:], ACT.Exp, scale=lg).then_inc(s.powered, 1)
                        act.activation(b.pwc[:, d], b.gap_cb[:] if d else b.gap_cf[:], ACT.Exp, scale=lg)\
                            .then_inc(s.powered, 1)
                    act.wait_ge(s.scored, h * TK + 1)
                    act.wait_ge(s.q_turned, h + 2)
                    act.copy(b.q_turned[:], q_ps[0:RDK, :]).then_inc(s.q_kept, 1)
                    act.wait_ge(s.summed, h + 2)
                    act.copy(mix[:, :, ds(h * RDV + H1 * VD, RDV)], o_ps.rearrange("p (t w) -> p t w", t=TX))\
                        .then_inc(s.put, 1)
                act.wait_ge(s.put, RH + 1)

            @block.tensor
            def _(pe):
                with pe.Fori(0, RH) as h:
                    pe.wait_ge(s.staged, h * 3 + 4)
                    pe.wait_ge(s.k_kept, h + 1)
                    pe.sem_inc(s.begun, 1)
                    for t in range(TK):
                        mm = pe.transpose(k_ps[0:RDK, t * P:(t + 1) * P], b.k_head[:, t, :], k.ident[:])
                    mm.then_inc(s.k_turned, 1)
                    pe.wait_ge(s.q_kept, h + 1)
                    pe.sem_inc(s.begun, 1)
                    for t in range(TX):
                        mm = pe.transpose(q_ps[0:RDK, t * P:(t + 1) * P], b.q_head[:, t, :], k.ident[:])
                    mm.then_inc(s.q_turned, 1)
                    pe.wait_ge(s.k_kept, h + 2)
                    pe.wait_ge(s.q_kept, h + 2)
                    for t in range(TK):
                        pe.wait_ge(s.weighed, h * TK + max(t - 1, 0) + 1)
                        pe.matmul(psum[:, t % 2, :], b.k_turned[:, t * P:(t + 1) * P], b.q_turned[:],
                                  start=True, stop=True).then_inc(s.scored, 1)
                    pe.wait_ge(s.weighed, h * TK + TK + 1)
                    pe.wait_ge(s.put, h + 1)
                    for t in range(TX):
                        for j in range(TK):
                            src = px[:, j, ds(h * RDV + O_RV, RDV)] if j < TX else \
                                pc[:, j - TX, ds(h * RDV + rk_c + RH * RDK, RDV)]
                            mm = pe.matmul(o_ps[:, t * P:(t + 1) * P], b.weights[:, j, t * P:(t + 1) * P], src,
                                           start=j == 0, stop=j == TK - 1)
                    mm.then_inc(s.summed, 1)

            @block.vector
            def _(dve):
                step = Steps(dve, s.vector_step)
                with dve.Fori(0, RH) as h:
                    step.restart()
                    dve.wait_ge(s.powered, h * 4 + 5)
                    step(dve.tensor_tensor(b.pw[:, 0], b.pw[:, 0], b.fwd[:], ALU.mult))
                    step(dve.tensor_tensor(b.pw[:, 1], b.pw[:, 1], b.bwd[:], ALU.mult))
                    step(dve.tensor_tensor(b.both[:], b.pw[:, 0], b.pw[:, 1], ALU.add))
                    step.reach(dve.tensor_tensor(b.both_c[:], b.pwc[:, 0], b.pwc[:, 1], ALU.add), s.mixed, h + 2)
                    dve.wait_ge(s.k_turned, h + 2)
                    dve.wait_ge(s.scored, h * TK + 1)
                    dve.tensor_copy(b.k_turned[:], k_ps[0:RDK, :]).then_inc(s.k_kept, 1)
                    dve.wait_ge(s.summed, h + 1)
                    for t in range(TK):
                        dve.wait_ge(s.scored, h * TK + (t + 2))
                        m = b.both[:, L - P - t * P:2 * L - P - t * P] if t < TX else \
                            b.both_c[:, P - (t - TX) * P:P - (t - TX) * P + L]
                        dve.scalar_tensor_tensor(out=b.weights[:, t], in0=psum[:, t % 2, :], scalar=RDK ** -0.5,
                                                 in1=m, op0=ALU.mult, op1=ALU.mult).then_inc(s.weighed, 1)
                dve.wait_ge(s.weighed, RH * TK + 1)

    with buffers(core, squares=[P, TX, RH * RDV], sums=[P, TX * RH], roots=[P, TX * RH], rates=[P, TX * RH],
                 gain=[P, RH * RDV], gate=[P, TX, RH * RDV]) as b, \
            stage(core, "ret_out", "loaded", "squared", "reduced", "rooted", "gated", "vector_step") as (block, s):
        o = mix[:, :, H1 * VD:]
        by_head = [v.rearrange("p t (h w) -> p t h w", w=RDV) for v in (o, b.squares[:])]
        sums, rates = (v[:].rearrange("p (t h) -> p t h", t=TX) for v in (b.sums, b.rates))

        @block.sync
        def _(sync):
            sync.dma_start(b.gain[:], on_all(k.args.g_ret_out)).then_inc(s.loaded, 16)

        @block.scalar
        def _(act):
            act.activation(b.squares[:], o, ACT.Square).then_inc(s.squared, 1)
            act.activation(b.gate[:], px[:, :, O_RG:], ACT.Silu).then_inc(s.gated, 1)
            act.wait_ge(s.reduced, 1)
            act.activation(b.roots[:], b.sums[:], ACT.Sqrt, scale=1.0 / RDV, bias=k.eps[:, 0:1]).then_inc(s.rooted, 1)

        @block.vector
        def _(dve):
            step = Steps(dve, s.vector_step)
            dve.wait_ge(s.squared, 1)
            dve.tensor_reduce(sums, by_head[1], AX, ALU.add).then_inc(s.reduced, 1)
            dve.wait_ge(s.rooted, 1)
            step(dve.reciprocal(b.rates[:], b.roots[:]))
            step(dve.tensor_tensor(by_head[0], by_head[0], spread(rates, 3, RDV), ALU.mult))
            dve.wait_ge(s.loaded, 16)
            step(dve.tensor_tensor(o, o, spread(b.gain[:], 1, TX), ALU.mult))
            dve.wait_ge(s.gated, 1)
            step(dve.tensor_tensor(o, o, b.gate[:], ALU.mult))


def first_mixer(core, k, args):
    nc = core.nc
    w_in = args.w_in[0].rearrange("(k p) n -> p k n", p=P)
    with buffers(core, mix=[P, TX, MIX1], px=[P, TX, DIN1], pc=[P, TC, O_PE + ROPE - O_KV + O_RG - O_RK]) as m:
        with buffers(core, whole=[P, SK, TK * P], high=[P, SK, TK * P, F32R], low=[P, SK, TK * P, F32R]) as h:
            with buffers(core, ctx=[P, TC, D], xn=[P, TX, D], junk=[P, D]) as b:
                with stage(core, "load_ctx", "loaded") as (block, s):
                    @block.sync
                    def _(sync):
                        sync.dma_start(b.ctx[:], args.ctx[0].rearrange("(t p) d -> p t d", p=P)).then_inc(s.loaded, 16)
                        sync.wait_ge(s.loaded, 16)
                norm_rows(core, k, "norm1", [(k.x[:, t], b.xn[:, t]) for t in range(TX)] +
                          [(b.ctx[:, t], b.ctx[:, t]) for t in range(TC)], b.junk[:])
                cols = [(0, QL, False), (O_KV, O_PE + ROPE, True), (O_RQ, O_RK, False),
                        (O_RK, O_RK + BANK, True), (O_RK + BANK, O_RG, True), (O_RG, DIN1, False)]
                chunks, outs, g = [], [], 0
                for lo, hi, ctx_too in cols:
                    tiles = range(TK if ctx_too else TX)
                    chunks.append(token_chunk(w_in[:, :, lo:hi], (h.whole, h.high, h.low), tiles, g))
                    at = lo - O_KV if lo < O_RQ else lo - O_KV - RH * RDK
                    outs += [m.px[:, t, lo:hi] if t < TX else m.pc[:, t - TX, at:at + hi - lo] for t in tiles]
                    g += len(tiles)
                to_features(core, k, "turn1", [
                    ([lambda i, t=t: b.xn[:, t, i * P:(i + 1) * P] for t in range(TX)], DC,
                     lambda i: features(h, i, 0, L), lambda i: k.scale1[:, i:i + 1],
                     lambda i: k.cols1[:, i, 0:1]),
                    ([lambda i, t=t: b.ctx[:, t, i * P:(i + 1) * P] for t in range(TC)], DC,
                     lambda i: features(h, i, L, L + LC), lambda i: k.scale1c[:, i:i + 1],
                     lambda i: k.cols1[:, i, 1:2])], prefetch=load_first(core, chunks))
            project(core, k, "in1", chunks,
                    lambda e, s, g, bank, step: copy_out(e, outs[g], bank[:, 0:outs[g].shape[1]]))
        retention(core, k, m.px[:], m.pc[:], m.mix[:], args.ret_decay_logit)
        with buffers(core, q=[P, TX, H1 * QK], kv=[P, TK, H1 * (NOPE + VD)], keys=[P, TK, H1 * QK]) as a:
            with buffers(core, cq=[P, QL // P, L], ckv=[P, 1, TK * P], gq=[P, 2], gkv=[P, 1]) as b:
                latent_norms(core, k, m.px[:], m.pc[:])
                with stage(core, "lora_gain", "loaded") as (block, s):
                    @block.sync
                    def _(sync):
                        sync.dma_start(b.gq[:], by_column(args.g_q_lora[0]), allow_slow_non_contiguous=True)\
                            .then_inc(s.loaded, 16)
                        sync.dma_start(b.gkv[:], by_column(args.g_kv_lora[0]), allow_slow_non_contiguous=True)\
                            .then_inc(s.loaded, 16)
                        sync.wait_ge(s.loaded, 32)
                wq = args.w_q_up[0].rearrange("(k p) n -> p k n", p=P)
                wkv = args.w_kv_up[0].rearrange("(k p) n -> p k n", p=P)
                chunks, outs, g = [], [], 0
                for w, lo, hi, src, tiles, out in (
                        (wq, 0, BANK, b.cq, TX, a.q), (wq, BANK, H1 * QK, b.cq, TX, a.q),
                        (wkv, 0, BANK, b.ckv, TK, a.kv), (wkv, BANK, 2 * BANK, b.ckv, TK, a.kv)):
                    chunks.append(token_chunk(w[:, :, lo:hi], (src,), range(tiles), g))
                    outs += [out[:, t, lo:hi] for t in range(tiles)]
                    g += tiles
                to_features(core, k, "turn_latents", [
                    ([lambda i, t=t: m.px[:, t, i * P:(i + 1) * P] for t in range(TX)], QL // P,
                     lambda i: b.cq[:, i, :], lambda i: b.gq[:, i:i + 1], None),
                    ([lambda i, t=t: m.px[:, t, O_KV:O_PE] for t in range(TX)], 1,
                     lambda i: b.ckv[:, 0, 0:L], lambda i: b.gkv[:, 0:1], None),
                    ([lambda i, t=t: m.pc[:, t, 0:KVL] for t in range(TC)], 1,
                     lambda i: b.ckv[:, 0, L:], lambda i: b.gkv[:, 0:1], None)],
                    prefetch=load_first(core, chunks))
                project(core, k, "up1", chunks,
                        lambda e, s, g, bank, step: copy_out(e, outs[g], bank[:, 0:outs[g].shape[1]]))
            with stage(core, "join_keys", "joined") as (block, s):
                @block.gpsimd
                def _(pool):
                    for t in range(TK):
                        pe_src = m.px[:, t, O_PE:O_RQ] if t < TX else m.pc[:, t - TX, KVL:KVL + ROPE]
                        pool.tensor_copy(a.keys[:, t].rearrange("p (h w) -> p h w", w=QK)[:, :, NOPE:],
                                         spread(pe_src, 1, H1)).then_inc(s.joined, 1)
                    pool.wait_ge(s.joined, TK)

                @block.scalar
                def _(act):
                    for t in range(TK):
                        act.copy(a.keys[:, t].rearrange("p (h w) -> p h w", w=QK)[:, :, 0:NOPE],
                                 a.kv[:, t].rearrange("p (h w) -> p h w", w=NOPE + VD)[:, :, 0:NOPE])
            with buffers(core, cos=[P, TX, ROPE], sin=[P, TX, ROPE], gq=[P, QK], gk=[P, QK]) as b:
                table = [(b.cos[:, t], b.sin[:, t]) for t in range(TX)] + [None] * TC
                view = lambda x, t: x[:, t].rearrange("p (h w) -> p h w", w=QK)
                head_norms(core, k, "heads1",
                           [(view(a.q, t), b.gq[:], table[t]) for t in range(TX)] +
                           [(view(a.keys, t), b.gk[:], table[t]) for t in range(TK)],
                           QK, (NOPE, ROPE, blocked_halves(ROPE)),
                           [(b.cos[:], k.args.cos_mla.rearrange("(t p) w -> p t w", p=P)),
                            (b.sin[:], k.args.sin_mla.rearrange("(t p) w -> p t w", p=P)),
                            (b.gq[:], on_all(args.g_q_head)), (b.gk[:], on_all(args.g_k_head))])
            attention(core, k, "attn1", a.q[:], H1, 1, QK, a.keys[:],
                      lambda g: a.kv[:, :, ds(g * (NOPE + VD) + NOPE, VD)],
                      lambda h: m.mix[:, :, ds(h * VD, VD)], VD)
        project_out(core, k, "out1", lambda t, i: m.mix[:, t, i * P:(i + 1) * P], MIX1, args.w_out[0], k.rows1, 1.0)


def project_out(core, k, name, mix, width, w_out, rows, alpha):
    kc = width // P
    parts = kc // DC
    w = w_out.rearrange("(q k p) n -> p q k n", p=P, k=DC)
    with buffers(core, whole=[P, kc // 2, L], high=[P, kc // 2, L, F32R], low=[P, kc // 2, L, F32R], gate=[P, D]) as b:
        chunks = []
        for n in range(2):
            for q in range(parts):
                x = tuple(v[:, q * SK:(q + 1) * SK] for v in (b.whole, b.high, b.low))
                chunks.append(token_chunk(w[:, q, :, n * BANK:(n + 1) * BANK], x, range(TX), n * TX,
                                          first=q == 0, last=q == parts - 1))
        to_features(core, k, name + "_turn", [
            ([lambda i, t=t: mix(t, i) for t in range(TX)], kc,
             lambda i: features(b, i, 0, L), None, None)], prefetch=load_first(core, chunks))

        def add(dve, s, g, bank, step):
            n, t = divmod(g, TX)
            cols = slice(n * BANK, (n + 1) * BANK)
            if g == 0:
                dve.wait_ge(s.gate_loaded, 16)
            step(dve.tensor_tensor(bank, bank, b.gate[:, cols], ALU.mult))
            return dve.scalar_tensor_tensor(out=k.x[:, t, cols], in0=k.x[:, t, cols], scalar=alpha, in1=bank,
                                            op0=ALU.mult, op1=ALU.add)

        project(core, k, name, chunks, add, extra=("gate_loaded",), vector_only=True,
                loads=lambda sync, s: sync.dma_start(b.gate[:], on_all(rows[0:1, 2 * D:3 * D]))
                .then_inc(s.gate_loaded, 16))




def places(core, k, name, r, oneh, mask, experts, top, n_blocks):
    nc, psum = core.nc, core.psum
    with buffers(core, pos=[P, TX, experts], full=[experts, 4], wide=[experts, P], count=[experts, 1],
                 ends=[experts, 1], passed=[experts, n_blocks], prod=[P, TX, experts], dest=[P, TX, top],
                 zeros=[P, n_blocks + 1, I32], ids=[P, TX, I32]) as b, \
            stage(core, name, "counted", "rounded", "summed", "compared", "listed", "placed", "ids_made", "cleared",
                  "vector_step", pool_dma=("scattered",)) as (block, s):
        ps_pos, ps_count, ps_start, ps_end, ps_total, ps_blocks = (psum[:, i, :] for i in range(6))

        @block.tensor
        def _(pe):
            for t in range(TX):
                for u in range(t + 1):
                    pe.matmul(ps_pos[:, t * experts:(t + 1) * experts], k.before[:] if u == t else k.ones[:],
                              mask[:, u, :], start=u == 0, stop=u == t)
            for t in range(TX):
                mm = pe.matmul(ps_count[0:experts, 0:1], mask[:, t, :], k.ones[:, 0:1], start=t == 0, stop=t == TX - 1)
            mm.then_inc(s.counted, 1)
            pe.wait_ge(s.rounded, 2)
            pe.matmul(ps_start[:, 0:experts], b.wide[:], k.before[0:experts, 0:experts], start=True, stop=True)
            pe.matmul(ps_end[0:experts, 0:1], k.upto[0:experts, 0:experts], b.count[:], start=True, stop=True)
            pe.matmul(ps_total[0:1, 0:1], b.count[:], k.ones[0:experts, 0:1], start=True, stop=True)\
                .then_inc(s.summed, 1)
            pe.wait_ge(s.compared, 1)
            pe.matmul(ps_blocks[0:1, 0:n_blocks], k.ones[0:experts, 0:1], b.passed[:], start=True, stop=True)\
                .then_inc(s.listed, 1)

        @block.vector
        def _(dve):
            step = Steps(dve, s.vector_step)
            step(dve.memset(b.zeros[:], 0))
            dve.engine_nop().then_inc(s.cleared, 1)
            dve.wait_ge(s.counted, 1)
            step(dve.tensor_copy(b.pos[:], ps_pos[:, 0:TX * experts].rearrange("p (t e) -> p t e", t=TX)))
            for i in range(4):
                step(dve.tensor_scalar(b.full[:, i:i + 1], ps_count[0:experts, 0:1], float(P * i), None, ALU.is_gt))
            dve.tensor_reduce(b.count[:], b.full[:], AX, ALU.add).then_inc(s.rounded, 1)
            dve.wait_ge(s.rounded, 1)
            dve.tensor_scalar(b.wide[:], k.ones[0:experts, :], b.count[:, 0:1], None, ALU.mult).then_inc(s.rounded, 1)
            dve.wait_ge(s.summed, 1)
            step(dve.tensor_copy(b.ends[:], ps_end[0:experts, 0:1]))
            dve.tensor_scalar(b.passed[:], k.numbers[0:experts, 0:n_blocks], b.ends[:, 0:1], None, ALU.is_ge)\
                .then_inc(s.compared, 1)
            step(dve.tensor_copy(r.blocks[0:1, n_blocks:n_blocks + 1], ps_total[0:1, 0:1]))
            for t in range(TX):
                step(dve.scalar_tensor_tensor(out=b.pos[:, t], in0=ps_start[:, 0:experts], scalar=float(P),
                                              in1=b.pos[:, t], op0=ALU.mult, op1=ALU.add))
            for j in range(top):
                step(dve.tensor_tensor(b.prod[:], oneh[:, j], b.pos[:], ALU.mult))
                step(dve.tensor_reduce(b.dest[:, :, j], b.prod[:], AX, ALU.add))
            dve.tensor_copy(r.dest[:], b.dest[:].rearrange("p t j -> p (t j)")).then_inc(s.placed, 1)
            dve.wait_ge(s.listed, 1)
            step(dve.tensor_scalar(r.blocks[0:1, 0:n_blocks], ps_blocks[0:1, 0:n_blocks], float(experts - 1), None,
                                   ALU.min))

        @block.gpsimd
        def _(pool):
            pool.iota(b.ids[:], [[P, TX]], base=0, channel_multiplier=1).then_inc(s.ids_made, 1)
            pool.wait_ge(s.ids_made, 1)
            pool.wait_ge(s.cleared, 1)
            pool.dma_start(r.slot_token.rearrange("(p b) o -> p (b o)", p=P), b.zeros[:]).then_inc(s.scattered, 16)
            pool.wait_ge(s.scattered, 16)
            pool.wait_ge(s.placed, 1)
            for t in range(TX):
                for j in range(top):
                    i = t * top + j
                    pool.indirect_dma_start(r.slot_token, bass.IndirectOffsetOnAxis(ap=r.dest[:, i:i + 1], axis=0),
                                            b.ids[:, t:t + 1], None).then_inc(s.scattered, 16)
            pool.wait_ge(s.scattered, 16 * (1 + TX * top))


def logits_of(core, k, name, turned, r, weights, biases, width):
    psum = core.psum
    with buffers(core, w=[P, DC, width], bias=[P, width]) as b, \
            stage(core, name, "loaded", "summed", "vector_step", "stored") as (block, s):
        @block.sync
        def _(sync):
            at = 0
            for w, bias in zip(weights, biases):
                n = w.shape[1]
                sync.dma_start(b.w[:, :, at:at + n], w.rearrange("(k p) n -> p k n", p=P)).then_inc(s.loaded, 16)
                sync.dma_start(b.bias[:, at:at + n], on_all(bias)).then_inc(s.loaded, 16)
                at += n

        @block.tensor
        def _(pe):
            pe.wait_ge(s.loaded, 32 * len(weights))
            for t in range(TX):
                for kc in range(DC):
                    mm = pe.matmul(psum[:, 0, t * width:(t + 1) * width], turned[:, kc, t * P:(t + 1) * P],
                                   b.w[:, kc, :], start=kc == 0, stop=kc == DC - 1)
            mm.then_inc(s.summed, 1)

        @block.vector
        def _(dve):
            step = Steps(dve, s.vector_step)
            dve.wait_ge(s.summed, 1)
            dve.wait_ge(s.loaded, 32 * len(weights))
            step(dve.tensor_tensor(r.logits[:], psum[:, 0, 0:TX * width].rearrange("p (t e) -> p t e", t=TX),
                                   spread(b.bias[:], 1, TX), ALU.add))


def choose_first(core, k, r, oneh, mask):
    with buffers(core, top=[P, TX, 8], index=[P, TX, 8, U32], indexf=[P, TX, 8], less=[P, TX, K1], sums=[P, TX],
                 e=[P, TX, K1]) as b, \
            stage(core, "choose1", "shifted", "exped", "vector_step") as (block, s):
        @block.scalar
        def _(act):
            act.wait_ge(s.shifted, 1)
            act.activation(b.e[:], b.less[:], ACT.Exp).then_inc(s.exped, 1)

        @block.vector
        def _(dve):
            step = Steps(dve, s.vector_step)
            for t in range(TX):
                step(dve.max(b.top[:, t], r.logits[:, t]))
                step(dve.max_index(b.index[:, t], b.top[:, t], r.logits[:, t]))
            dve.tensor_tensor(b.less[:], b.top[:, :, 0:K1], b.top[:, :, 0:1].to_broadcast([P, TX, K1]),
                              ALU.subtract).then_inc(s.shifted, 1)
            step(dve.tensor_copy(b.indexf[:], b.index[:]))
            one_hot(step, dve, k, oneh, mask, b.indexf, E1, K1)
            dve.wait_ge(s.exped, 1)
            step(dve.tensor_reduce(b.sums[:], b.e[:], AX, ALU.add))
            step(dve.reciprocal(b.sums[:], b.sums[:]))
            step(dve.tensor_tensor(r.gates[:], b.e[:], spread(b.sums[:], 2, K1), ALU.mult))


def one_hot(step, dve, k, oneh, mask, index, experts, top):
    for j in range(top):
        step(dve.tensor_tensor(oneh[:, j], spread(k.numbers[:, 0:experts], 1, TX),
                               index[:, :, j:j + 1].to_broadcast([P, TX, experts]), ALU.is_equal))
        if j == 1:
            step(dve.tensor_tensor(mask[:], oneh[:, 0], oneh[:, 1], ALU.add))
        elif j > 1:
            step(dve.tensor_tensor(mask[:], mask[:], oneh[:, j], ALU.add))


def choose_second(core, k, r, oneh, mask):
    with buffers(core, padded=[P, TX, 8], top=[P, TX, 8], index=[P, TX, 8, U32], indexf=[P, TX, 8],
                 less=[P, TX, MG], e=[P, TX, MG], sums=[P, TX], group=[P, TX, MG], penalty=[P, TX, MG],
                 inside=[P, TX, E2], gap=[P, TX], ratio=[P, TX], share=[P, TX]) as b, \
            stage(core, "choose2", "shifted", "exped", "vector_step") as (block, s):
        @block.scalar
        def _(act):
            act.wait_ge(s.shifted, 1)
            act.activation(b.e[:], b.less[:], ACT.Exp).then_inc(s.exped, 1)
            act.wait_ge(s.shifted, 2)
            act.activation(b.ratio[:], b.gap[:], ACT.Exp).then_inc(s.exped, 1)

        @block.vector
        def _(dve):
            step = Steps(dve, s.vector_step)
            step(dve.memset(b.padded[:], -BIG))
            step(dve.tensor_copy(b.padded[:, :, 0:MG], r.logits[:, :, 0:MG]))
            for t in range(TX):
                step(dve.max(b.top[:, t], b.padded[:, t]))
                step(dve.max_index(b.index[:, t], b.top[:, t], b.padded[:, t]))
            dve.tensor_tensor(b.less[:], r.logits[:, :, 0:MG], b.top[:, :, 0:1].to_broadcast([P, TX, MG]),
                              ALU.subtract).then_inc(s.shifted, 1)
            step(dve.tensor_copy(b.indexf[:], b.index[:]))
            step(dve.tensor_tensor(b.group[:], spread(k.numbers[:, 0:MG], 1, TX),
                                   b.indexf[:, :, 0:1].to_broadcast([P, TX, MG]), ALU.is_equal))
            step(dve.tensor_scalar(b.penalty[:], b.group[:], -1.0, BIG, ALU.add, ALU.mult))
            for t in range(TX):
                inside = b.inside[:, t].rearrange("p (g e) -> p g e", e=ME)
                step(dve.tensor_tensor(inside, r.logits[:, t, MG:].rearrange("p (g e) -> p g e", e=ME),
                                       spread(b.group[:, t], 2, ME), ALU.mult))
                step(dve.tensor_tensor(inside, inside, spread(b.penalty[:, t], 2, ME), ALU.add))
                step(dve.max(b.top[:, t], b.inside[:, t]))
                step(dve.max_index(b.index[:, t], b.top[:, t], b.inside[:, t]))
            dve.tensor_tensor(b.gap[:], b.top[:, :, 1], b.top[:, :, 0], ALU.subtract).then_inc(s.shifted, 1)
            step(dve.tensor_copy(b.indexf[:], b.index[:]))
            one_hot(step, dve, k, oneh, mask, b.indexf, E2, K2)
            dve.wait_ge(s.exped, 2)
            step(dve.tensor_reduce(b.sums[:], b.e[:], AX, ALU.add))
            step(dve.scalar_tensor_tensor(out=b.share[:], in0=b.ratio[:], scalar=1.0, in1=b.sums[:], op0=ALU.add,
                                          op1=ALU.mult))
            step(dve.reciprocal(r.gates[:, :, 0], b.share[:]))
            step(dve.tensor_tensor(r.gates[:, :, 1], r.gates[:, :, 0], b.ratio[:], ALU.mult))


def store_rows(core, name, rows, dram, cleared):
    with stage(core, name, "stored") as (block, s):
        @block.sync
        def _(sync):
            sync.dma_start(dram.rearrange("(t p) d -> p t d", p=P), rows).then_inc(s.stored, 16)
            sync.wait_ge(s.stored, 16)
            sync.wait_ge(cleared, 16)


def gather_tokens(pool, s, b, r, rows, block_no, value):
    pool.dma_start(b.slot_ids[:], r.slot_token[ds(block_no * P, P), :] if not isinstance(block_no, int) else
                   r.slot_token[block_no * P:(block_no + 1) * P, :]).then_inc(s.gathered, 16)
    pool.wait_ge(s.gathered, value + 16)
    pool.sem_inc(s.taken, 1)
    pool.indirect_dma_start(b.rows[:], None, rows, bass.IndirectOffsetOnAxis(ap=b.slot_ids[:, 0:1], axis=0))\
        .then_inc(s.gathered, 16)


def block_count(engine, r, n_blocks):
    return engine.value_load(r.blocks[0:1, n_blocks:n_blocks + 1], min_val=1, max_val=n_blocks)


def first_expert_blocks(core, k, r, rows, y_rows, args, n_blocks):
    nc, psum, ring = core.nc, core.psum, core.ring
    UC, YC = 2 * FF1 // BANK, D // BANK
    per = UC + YC
    half = BANK // 2
    y_bank = 2
    with buffers(core, more=[P, per - SLOTS, DC, BANK], slot_ids=[P, 1, I32], rows=[P, D], turned=[P, DC, P],
                 bias_row=[1, 2 * FF1 + D], bias=[P, 2 * FF1 + D], u=[P, BANK], glu=[P, half], lin=[P, half],
                 sig=[P, half], act=[P, FF1], act_turned=[P, SK, P], y=[P, D], w_high=[P, 2, SK, BANK, F32R],
                 w_low=[P, 2, SK, BANK, F32R],
                 x_high=[P, SK, P, F32R], x_low=[P, SK, P, F32R], act_high=[P, SK, P, F32R],
                 act_low=[P, SK, P, F32R]) as b, \
            stage(core, "experts1", *[f"chunk{c}_loaded" for c in range(per)], "chunk_done", "bias_loaded",
                  "bias_spread", "x_turned", "x_kept", "clipped", "squashed", "activated",
                  "high_made", "low_made", "x_made", "lows_made", "act_turned", "act_kept", "y_added", "y_stored", "vector_step", "taken", pool_dma=("gathered",),
                  from_one=("high_made", "low_made", "x_made", "lows_made", "chunk_done", "bias_spread", "x_turned", "x_kept", "clipped", "squashed", "activated", "act_turned", "act_kept", "y_added", "y_stored")) as (block, s):
        slots = [ring.slots[:, i] for i in range(SLOTS)] + [b.more[:, i] for i in range(per - SLOTS)]
        loaded = [s.chunk0_loaded, s.chunk1_loaded, s.chunk2_loaded, s.chunk3_loaded, s.chunk4_loaded,
                  s.chunk5_loaded]


        @block.sync
        def _(sync):
            n = block_count(sync, r, n_blocks)

            def load_block(i):
                e = sync.value_load(r.blocks[0:1, ds(i, 1)] if not isinstance(i, int) else r.blocks[0:1, i:i + 1],
                                    min_val=0, max_val=E1 - 1)
                sync.wait_ge(s.bias_spread, i * 2 + 1)
                sync.dma_start(b.bias_row[:, 0:2 * FF1], args.b_mlp1[0][ds(e, 1), :]).then_inc(s.bias_loaded, 16)
                sync.dma_start(b.bias_row[:, 2 * FF1:], args.b_mlp2[0][ds(e, 1), :]).then_inc(s.bias_loaded, 16)
                for c in range(per):
                    sync.wait_ge(s.chunk_done, i * per + c + 1)
                    w, at = (args.w_mlp1, c) if c < UC else (args.w_mlp2, c - UC)
                    src = w[0][ds(e, 1)].rearrange("a (k p) n -> p (a k) n", p=P)
                    sync.dma_start(slots[c], src[:, :, at * BANK:(at + 1) * BANK]).then_inc(loaded[c], 16)

            def store_block(i):
                sync.wait_ge(s.y_added, i * 2 + 3)
                sync.dma_start(y_rows[ds(i * P, P), :], b.y[:]).then_inc(s.y_stored, 16)

            load_block(0)
            with sync.Fori(0, n - 1) as i:
                load_block(i + 1)
                store_block(i)
            store_block(n - 1)
            sync.wait_ge(s.y_stored, n * 16 + 1)
            sync.sem_inc(s.taken, 1)

        @block.gpsimd
        def _(pool):
            n = block_count(pool, r, n_blocks)
            gather_tokens(pool, s, b, r, rows, 0, 0)
            with pool.Fori(0, n) as i:
                pool.wait_ge(s.bias_loaded, i * 32 + 32)
                pool.wait_ge(s.activated, i * UC + 1)
                pool.sem_inc(s.taken, 1)
                pool.partition_broadcast(b.bias[:, 0:2 * FF1], b.bias_row[:, 0:2 * FF1]).then_inc(s.bias_spread, 1)
                pool.wait_ge(s.y_added, i * 2 + 1)
                pool.sem_inc(s.taken, 1)
                pool.partition_broadcast(b.bias[:, 2 * FF1:], b.bias_row[:, 2 * FF1:]).then_inc(s.bias_spread, 1)
                pool.wait_ge(s.x_turned, i + 2)
                pool.wait_ge(s.gathered, i * 32 + 32)
                gather_tokens(pool, s, b, r, rows, i + 1, i * 32 + 32)
            pool.wait_ge(s.gathered, n * 32 + 32)

        @block.tensor
        def _(pe):
            n = block_count(pe, r, n_blocks)

            def turn_rows():
                for m in range(DC):
                    mm = pe.transpose(psum[:, 4 + m // 4, (m % 4) * P:(m % 4 + 1) * P], b.rows[:, m * P:(m + 1) * P],
                                      k.ident[:])
                mm.then_inc(s.x_turned, 1)

            pe.sem_inc(s.chunk_done, per - 1)
            pe.wait_ge(s.gathered, 32)
            turn_rows()
            with pe.Fori(0, n) as i:
                def turn_activations(c):
                    pe.wait_ge(s.activated, i * UC + (c + 2))
                    for m in range(2 * c, 2 * c + 2):
                        mm = pe.transpose(psum[:, 6 + m // 4, (m % 4) * P:(m % 4 + 1) * P],
                                          b.act[:, m * P:(m + 1) * P], k.ident[:])
                    if c % 2:
                        mm.then_inc(s.act_turned, 1)

                def whole_half(bank, x, c):
                    for kc in range(SK):
                        pe.matmul(psum[:, bank, :], x[:, kc, :], slots[c][:, kc, :], start=kc == 0, stop=False)

                def split_half(bank, high, low, c):
                    pe.wait_ge(s.high_made, i * per + (c + 2))
                    for kc in range(SK):
                        w = b.w_high[:, c % 2, kc, :]
                        pe.matmul(psum[:, bank, :], high[:, kc, :], w, start=False, stop=False)
                        pe.matmul(psum[:, bank, :], low[:, kc, :], w, start=False, stop=False)
                    pe.wait_ge(s.low_made, i * per + (c + 2))
                    for kc in range(SK):
                        mm = pe.matmul(psum[:, bank, :], high[:, kc, :], b.w_low[:, c % 2, kc, :], start=False,
                                       stop=kc == SK - 1)
                    mm.then_inc(s.chunk_done, 1)

                pe.wait_ge(s.x_kept, i + 2)
                for c in range(UC):
                    pe.wait_ge(loaded[c], i * 16 + 16)
                    if c == y_bank:
                        pe.wait_ge(s.y_added, i * 2 + 1)
                    whole_half(c, b.turned, c)
                    if c == 0:
                        pe.wait_ge(s.lows_made, i * 2 + 2)
                    split_half(c, b.x_high, b.x_low, c)
                    if c:
                        turn_activations(c - 1)
                pe.wait_ge(s.gathered, i * 32 + 64)
                turn_rows()
                pe.wait_ge(s.act_kept, i * 2 + 2)
                pe.wait_ge(loaded[UC], i * 16 + 16)
                pe.wait_ge(s.activated, i * UC + (y_bank + 2))
                whole_half(y_bank, b.act_turned, UC)
                turn_activations(UC - 1)
                pe.wait_ge(loaded[UC + 1], i * 16 + 16)
                whole_half(y_bank + 1, b.act_turned, UC + 1)
                pe.wait_ge(s.act_kept, i * 2 + 3)
                pe.wait_ge(s.lows_made, i * 2 + 4)
                split_half(y_bank, b.act_high, b.act_low, UC)
                split_half(y_bank + 1, b.act_high, b.act_low, UC + 1)

        @block.scalar
        def _(act):
            n = block_count(act, r, n_blocks)

            def keep_rows(value):
                act.wait_ge(s.x_turned, value + 1)
                for m in range(DC):
                    ins = act.activation(b.turned[:, m, :], psum[:, 4 + m // 4, (m % 4) * P:(m % 4 + 1) * P],
                                         ACT.Identity, scale=k.scale1f[:, m:m + 1],
                                         bias=k.cols1[:, 3 * DC + m, 0:1])
                ins.then_inc(s.x_made, 1)
                act.wait_ge(s.x_made, value + 1)
                act.copy(b.x_high[:], b.turned[:, SK:, :]).then_inc(s.x_kept, 1)

            keep_rows(1)
            with act.Fori(0, n) as i:
                def keep_activations(c):
                    act.wait_ge(s.act_turned, i * 2 + (c + 2))
                    act.copy(b.act_high[:] if c else b.act_turned[:], psum[:, 6 + c, :].rearrange(
                        "p (m q) -> p m q", q=P)).then_inc(s.act_kept, 1)

                def make_high(c):
                    act.wait_ge(loaded[c], i * 16 + 16)
                    act.wait_ge(s.chunk_done, i * per + (c - 2 + per + 1))
                    act.copy(b.w_high[:, c % 2], slots[c][:, SK:, :]).then_inc(s.high_made, 1)

                make_high(0)
                make_high(1)
                for c in range(UC):
                    act.wait_ge(s.clipped, i * UC + (c + 2))
                    act.activation(b.sig[:], b.glu[:], ACT.Sigmoid, scale=ALPHA).then_inc(s.squashed, 1)
                    if c == UC - 2:
                        keep_activations(0)
                    make_high(c + 2)
                keep_rows(i + 2)
                keep_activations(1)

        @block.vector
        def _(dve):
            n = block_count(dve, r, n_blocks)
            step = Steps(dve, s.vector_step)
            def make_x_low(value):
                dve.wait_ge(s.x_kept, value + 1)
                dve.tensor_tensor(b.x_low[:], b.turned[:, SK:, :], b.x_high[:].bitcast(F32), ALU.subtract)\
                    .then_inc(s.lows_made, 1)

            make_x_low(1)
            with dve.Fori(0, n) as i:
                step.restart()

                def make_low(c):
                    dve.wait_ge(s.high_made, i * per + (c + 2))
                    dve.tensor_tensor(b.w_low[:, c % 2], slots[c][:, SK:, :], b.w_high[:, c % 2].bitcast(F32),
                                      ALU.subtract).then_inc(s.low_made, 1)

                make_low(0)
                make_low(1)
                dve.wait_ge(s.act_turned, i * 2 + 1)
                dve.wait_ge(s.bias_spread, i * 2 + 3)
                for c in range(UC):
                    dve.wait_ge(s.chunk_done, i * per + (c + per + 1))
                    step(dve.tensor_tensor(b.u[:], psum[:, c, :], b.bias[:, c * BANK:(c + 1) * BANK], ALU.add))
                    step.reach(dve.tensor_scalar(b.glu[:], b.u[:, 0::2], LIMIT, None, ALU.min), s.clipped,
                                i * UC + (c + 2))
                    step(dve.tensor_scalar(b.lin[:], b.u[:, 1::2], LIMIT, -LIMIT, ALU.min, ALU.max))
                    step(dve.scalar_tensor_tensor(out=b.lin[:], in0=b.lin[:], scalar=1.0, in1=b.glu[:], op0=ALU.add,
                                                  op1=ALU.mult))
                    dve.wait_ge(s.squashed, i * UC + (c + 2))
                    step.reach(dve.tensor_tensor(b.act[:, c * half:(c + 1) * half], b.lin[:], b.sig[:], ALU.mult),
                                s.activated, i * UC + (c + 2))
                    make_low(c + 2)
                make_x_low(i + 2)
                dve.wait_ge(s.act_kept, i * 2 + 3)
                dve.tensor_tensor(b.act_low[:], psum[:, 7, :].rearrange("p (m q) -> p m q", q=P),
                                  b.act_high[:].bitcast(F32), ALU.subtract).then_inc(s.lows_made, 1)
                dve.wait_ge(s.y_stored, i * 16 + 1)
                for c in range(YC):
                    dve.wait_ge(s.chunk_done, i * per + (UC + c + per + 1))
                    dve.tensor_tensor(b.y[:, c * BANK:(c + 1) * BANK], psum[:, y_bank + c, :],
                                      b.bias[:, 2 * FF1 + c * BANK:2 * FF1 + (c + 1) * BANK], ALU.add)\
                        .then_inc(s.y_added, 1)


def second_expert_blocks(core, k, r, rows, y_rows, args, n_blocks):
    nc, psum, ring = core.nc, core.psum, core.ring
    hk = DC // 2
    fk = FF2 // P
    per = 3
    down = ring.slots[:, 2].rearrange("p k n -> p (k n)")[:, 0:fk * D].rearrange("p (k n) -> p k n", k=fk)
    with buffers(core, slot_ids=[P, 1, I32], rows=[P, D], turned=[P, DC, P], sil=[P, FF2], act=[P, FF2],
                 act_turned=[P, fk, P], y=[P, D]) as b, \
            stage(core, "experts2", "first_loaded", "second_loaded", "down_loaded", "chunk_done", "x_turned", "x_kept", "silued", "activated", "act_turned", "act_kept", "y_copied", "y_stored", "taken",
                  pool_dma=("gathered",),
                  from_one=("chunk_done", "x_turned", "x_kept", "silued", "activated", "act_turned", "act_kept", "y_copied", "y_stored")) \
            as (block, s):
        @block.sync
        def _(sync):
            n = block_count(sync, r, n_blocks)
            with sync.Fori(0, n) as i:
                e = sync.value_load(r.blocks[0:1, ds(i, 1)], min_val=0, max_val=E2 - 1)
                for c, loaded in enumerate((s.first_loaded, s.second_loaded)):
                    sync.wait_ge(s.chunk_done, i * per + c + 1)
                    for at, w in enumerate((args.w_gate_2, args.w_up_2)):
                        src = w[0][ds(e, 1)].rearrange("a (k p) n -> p (a k) n", p=P)
                        sync.dma_start(ring.slots[:, c, 0:hk, at * FF2:(at + 1) * FF2],
                                       src[:, c * hk:(c + 1) * hk, :]).then_inc(loaded, 16)
                sync.wait_ge(s.chunk_done, i * per + 3)
                sync.dma_start(down, args.w_down_2[0][ds(e, 1)].rearrange("a (k p) n -> p (a k) n", p=P))\
                    .then_inc(s.down_loaded, 16)

        @block.gpsimd
        def _(pool):
            n = block_count(pool, r, n_blocks)
            gather_tokens(pool, s, b, r, rows, 0, 0)
            with pool.Fori(0, n) as i:
                pool.wait_ge(s.x_turned, i + 2)
                pool.wait_ge(s.gathered, i * 32 + 32)
                gather_tokens(pool, s, b, r, rows, i + 1, i * 32 + 32)
            pool.wait_ge(s.gathered, n * 32 + 32)

        @block.tensor
        def _(pe):
            n = block_count(pe, r, n_blocks)

            def turn_rows():
                for m in range(DC):
                    mm = pe.transpose(psum[:, 4 + m // 4, (m % 4) * P:(m % 4 + 1) * P], b.rows[:, m * P:(m + 1) * P],
                                      k.ident[:])
                mm.then_inc(s.x_turned, 1)

            pe.sem_inc(s.chunk_done, per - 1)
            pe.wait_ge(s.gathered, 32)
            turn_rows()
            with pe.Fori(0, n) as i:
                pe.wait_ge(s.x_kept, i * 2 + 3)
                pe.wait_ge(s.activated, i + 1)
                for c, loaded in enumerate((s.first_loaded, s.second_loaded)):
                    pe.wait_ge(loaded, i * 32 + 32)
                    for kc in range(hk):
                        mm = pe.matmul(psum[:, 0, :], b.turned[:, c * hk + kc, :], ring.slots[:, c, kc, :],
                                       start=c == 0 and kc == 0, stop=c == 1 and kc == hk - 1)
                    mm.then_inc(s.chunk_done, 1)
                pe.wait_ge(s.gathered, i * 32 + 64)
                turn_rows()
                pe.wait_ge(s.activated, i + 2)
                for m in range(fk):
                    mm = pe.transpose(psum[:, 6, m * P:(m + 1) * P], b.act[:, m * P:(m + 1) * P], k.ident[:])
                mm.then_inc(s.act_turned, 1)
                pe.wait_ge(s.down_loaded, i * 16 + 16)
                pe.wait_ge(s.act_kept, i + 2)
                pe.wait_ge(s.y_copied, i * 2 + 1)
                for c in range(D // BANK):
                    for kc in range(fk):
                        mm = pe.matmul(psum[:, 1 + c, :], b.act_turned[:, kc, :],
                                       down[:, kc, c * BANK:(c + 1) * BANK], start=kc == 0, stop=kc == fk - 1)
                mm.then_inc(s.chunk_done, 1)

        @block.scalar
        def _(act):
            n = block_count(act, r, n_blocks)

            def keep_rows(value):
                act.wait_ge(s.x_turned, value + 1)
                for m in range(DC):
                    ins = act.activation(b.turned[:, m, :], psum[:, 4 + m // 4, (m % 4) * P:(m % 4 + 1) * P],
                                         ACT.Identity, scale=k.scale2f[:, m:m + 1],
                                         bias=k.cols2[:, 3 * DC + m, 0:1])
                    if m >= DC - 2:
                        ins.then_inc(s.x_kept, 1)

            keep_rows(1)
            with act.Fori(0, n) as i:
                act.wait_ge(s.chunk_done, i * per + 5)
                act.activation(b.sil[:], psum[:, 0, 0:FF2], ACT.Silu).then_inc(s.silued, 1)
                keep_rows(i + 2)
                act.wait_ge(s.y_copied, i * 2 + 3)
                act.dma_start(y_rows[ds(i * P, P), :], b.y[:]).then_inc(s.y_stored, 16)
            act.wait_ge(s.y_stored, n * 16 + 1)
            act.sem_inc(s.taken, 1)

        @block.vector
        def _(dve):
            n = block_count(dve, r, n_blocks)
            with dve.Fori(0, n) as i:
                dve.wait_ge(s.silued, i + 2)
                dve.wait_ge(s.act_turned, i + 1)
                dve.tensor_tensor(b.act[:], b.sil[:], psum[:, 0, FF2:2 * FF2], ALU.mult).then_inc(s.activated, 1)
                dve.wait_ge(s.act_turned, i + 2)
                dve.tensor_copy(b.act_turned[:], psum[:, 6, 0:FF2].rearrange("p (m q) -> p m q", q=P))\
                    .then_inc(s.act_kept, 1)
                dve.wait_ge(s.chunk_done, i * per + 6)
                dve.wait_ge(s.y_stored, i * 16 + 1)
                for c in range(D // BANK):
                    dve.tensor_copy(b.y[:, c * BANK:(c + 1) * BANK], psum[:, 1 + c, :]).then_inc(s.y_copied, 1)


def combine(core, k, name, r, y_rows, rows, top, alpha):
    ahead = 4
    with buffers(core, got=[P, ahead, D], total=[P, D], gate=[P, D]) as b, \
            stage(core, name, "gate_loaded", "added", "vector_step", pool_dma=("got0", "got1", "got2", "got3")) as (block, s):
        got = [s.got0, s.got1, s.got2, s.got3]
        work = [(t, j) for t in range(TX) for j in range(top)]

        @block.sync
        def _(sync):
            sync.dma_start(b.gate[:], on_all(rows[0:1, 5 * D:6 * D])).then_inc(s.gate_loaded, 16)

        @block.gpsimd
        def _(pool):
            for i, (t, j) in enumerate(work):
                if i >= ahead:
                    pool.wait_ge(s.added, i - ahead + 1)
                pool.indirect_dma_start(b.got[:, i % ahead], None, y_rows,
                                        bass.IndirectOffsetOnAxis(ap=r.dest[:, i:i + 1], axis=0))\
                    .then_inc(got[i % ahead], 16)

        @block.vector
        def _(dve):
            step = Steps(dve, s.vector_step)
            dve.wait_ge(s.gate_loaded, 16)
            for i, (t, j) in enumerate(work):
                dve.wait_ge(got[i % ahead], 16 * (i // ahead + 1))
                share = r.gates[:, t, j:j + 1]
                if j == 0:
                    ins = dve.tensor_scalar(b.total[:], b.got[:, i % ahead], share, None, ALU.mult)
                else:
                    ins = dve.scalar_tensor_tensor(out=b.total[:], in0=b.got[:, i % ahead], scalar=share,
                                                   in1=b.total[:], op0=ALU.mult, op1=ALU.add)
                step.reach(ins, s.added, i + 1)
                if j == top - 1:
                    step(dve.tensor_tensor(b.total[:], b.total[:], b.gate[:], ALU.mult))
                    step(dve.scalar_tensor_tensor(out=k.x[:, t], in0=k.x[:, t], scalar=alpha, in1=b.total[:],
                                                  op0=ALU.mult, op1=ALU.add))


def expert_layer(core, k, args, which):
    nc = core.nc
    first = which == 1
    experts, top = (E1, K1) if first else (E2, K2)
    width = E1 if first else MG + E2
    n_blocks = most_blocks(L, top, experts)
    rows = nc.dram_tensor(f"token_rows{which}", [L, D], F32).ap()
    y_rows = k.slot_rows
    slot_token = nc.dram_tensor(f"slot_token{which}", [(n_blocks + 1) * P, 1], I32).ap()
    scale, cols = (k.scale1f, k.cols1) if first else (k.scale2f, k.cols2)
    with buffers(core, logits=[P, TX, width], gates=[P, TX, top], dest=[P, TX * top, I32],
                 blocks=[1, n_blocks + 1, I32], others={"slot_token": slot_token}) as r:
        with buffers(core, turned=[P, DC, L], xn=[P, TX, D], junk=[P, D]) as b:
            src = k.x
            if first:
                norm_rows(core, k, "norm_ffn", [(k.x[:, t], b.xn[:, t]) for t in range(TX)], b.junk[:])
                src = b.xn
            store_rows(core, f"store_rows{which}", src[:], rows, k.slots_cleared)
            to_features(core, k, f"turn_ffn{which}", [
                ([lambda i, t=t: src[:, t, i * P:(i + 1) * P] for t in range(TX)], DC,
                 lambda i: b.turned[:, i, :], lambda i: scale[:, i:i + 1], lambda i: cols[:, 3 * DC + i, 0:1])])
            if first:
                logits_of(core, k, "logits1", b.turned, r, [args.w_router[0]], [args.b_router], width)
            else:
                logits_of(core, k, "logits2", b.turned, r, [args.w_rg_2[0], args.w_re_2[0]],
                          [args.b_rg_2, args.b_re_2], width)
        with buffers(core, oneh=[P, top, TX, experts], mask=[P, TX, experts]) as b:
            (choose_first if first else choose_second)(core, k, r, b.oneh, b.mask)
            places(core, k, f"places{which}", r, b.oneh, b.mask, experts, top, n_blocks)
        (first_expert_blocks if first else second_expert_blocks)(core, k, r, rows, y_rows, args, n_blocks)
        combine(core, k, f"combine{which}", r, y_rows, k.rows1 if first else k.rows2, top, 1.0 if first else ALPHA2)


def first_experts(core, k, args):
    expert_layer(core, k, args, 1)


def second_experts(core, k, args):
    expert_layer(core, k, args, 2)
    layer_norm(core, k, "ln2", args.ln2_g_2, args.ln2_b_2)




CTX_AT, X_AT = 2, LC + 6
WIDE = LC + L + 8


def layer_norm(core, k, name, gain, bias):
    with buffers(core, sums=[P, TX], squares=[P, TX], roots=[P, TX], rates=[P, TX], eps=[P, 1], junk=[P, D],
                 gain=[P, D], bias=[P, D]) as b, \
            stage(core, name, "loaded", "summed", "centred", "rooted", "scalar_step", "vector_step", "eps_set") \
            as (block, s):
        @block.sync
        def _(sync):
            sync.dma_start(b.gain[:], on_all(gain)).then_inc(s.loaded, 16)
            sync.dma_start(b.bias[:], on_all(bias)).then_inc(s.loaded, 16)

        @block.gpsimd
        def _(pool):
            pool.memset(b.eps[:], 1e-5).then_inc(s.eps_set, 1)

        @block.scalar
        def _(act):
            step = Steps(act, s.scalar_step)
            for t in range(TX):
                step.reach(act.activation(b.junk[:], k.x[:, t], ACT.Copy, accum_out=b.sums[:, t:t + 1]),
                            s.summed, t + 1)
            for t in range(TX):
                act.wait_ge(s.centred, t + 1)
                step(act.activation(b.junk[:], k.x[:, t], ACT.Square, accum_out=b.squares[:, t:t + 1]))
            act.wait_ge(s.eps_set, 1)
            act.activation(b.roots[:], b.squares[:], ACT.Sqrt, scale=1.0 / D, bias=b.eps[:, 0:1])\
                .then_inc(s.rooted, 1)

        @block.vector
        def _(dve):
            step = Steps(dve, s.vector_step)
            for t in range(TX):
                dve.wait_ge(s.summed, t + 1)
                step(dve.tensor_scalar(b.sums[:, t:t + 1], b.sums[:, t:t + 1], 1.0 / D, None, ALU.mult))
                step.reach(dve.tensor_scalar(k.x[:, t], k.x[:, t], b.sums[:, t:t + 1], None, ALU.subtract),
                            s.centred, t + 1)
            dve.wait_ge(s.rooted, 1)
            step(dve.reciprocal(b.rates[:], b.roots[:]))
            dve.wait_ge(s.loaded, 32)
            for t in range(TX):
                step(dve.scalar_tensor_tensor(out=k.x[:, t], in0=k.x[:, t], scalar=b.rates[:, t:t + 1],
                                              in1=b.gain[:], op0=ALU.mult, op1=ALU.mult))
                step(dve.tensor_tensor(k.x[:, t], k.x[:, t], b.bias[:], ALU.add))


def convolve(core, k, raw, xs, b_rows, conv_w, conv_b):
    nc, psum = core.nc, core.psum
    chunks = DXBC // P
    n_xs = DS // P
    n_turned = n_xs + SG
    span = WIDE - TAPS + 1
    flat = psum[:, :, :].rearrange("p b n -> p (b n)")
    with buffers(core, taps=[P, chunks, TAPS], bias=[P, chunks], acc=[P, 2, span], sil=[P, 2, span]) as b, \
            stage(core, "convolve", "loaded", "first_tap", "last_tap", "silued", "turned", "kept", "vector_step") \
            as (block, s):
        @block.sync
        def _(sync):
            for j in range(TAPS):
                sync.dma_start(b.taps[:, :, j], by_column(conv_w[0, j]), allow_slow_non_contiguous=True)\
                    .then_inc(s.loaded, 16)
            sync.dma_start(b.bias[:], by_column(conv_b[0]), allow_slow_non_contiguous=True).then_inc(s.loaded, 16)

        @block.scalar
        def _(act):
            act.wait_ge(s.loaded, 16 * (TAPS + 1))

            def first(c):
                if c >= 2:
                    act.wait_ge(s.silued, c - 1)
                act.activation(b.acc[:, c % 2], raw[:, c, 0:span], ACT.Identity,
                               scale=b.taps[:, c, 0:1]).then_inc(s.first_tap, 1)

            first(0)
            for c in range(chunks):
                if c + 1 < chunks:
                    first(c + 1)
                act.wait_ge(s.last_tap, c + 1)
                if 2 <= c < n_turned:
                    act.wait_ge(s.turned, c - 1)
                out = b.sil[:, c % 2] if c < n_xs else raw[:, c, 0:span]
                act.activation(out, b.acc[:, c % 2], ACT.Silu, bias=b.bias[:, c:c + 1]).then_inc(s.silued, 1)
                if c < n_turned:
                    act.wait_ge(s.turned, c + 1)
                    dst = xs[:, :, c * P:(c + 1) * P] if c < n_xs else b_rows[:, :, c - n_xs]
                    act.copy(dst, flat[:, (c % 2) * 2 * BANK:(c % 2) * 2 * BANK + TK * P]
                             .rearrange("p (t n) -> p t n", t=TK)).then_inc(s.kept, 1)
            act.wait_ge(s.kept, n_turned)

        @block.vector
        def _(dve):
            step = Steps(dve, s.vector_step)
            for c in range(chunks):
                dve.wait_ge(s.first_tap, c + 1)
                for j in range(1, TAPS):
                    ins = dve.scalar_tensor_tensor(out=b.acc[:, c % 2], in0=raw[:, c, j:j + span],
                                                   scalar=b.taps[:, c, j:j + 1], in1=b.acc[:, c % 2],
                                                   op0=ALU.mult, op1=ALU.add)
                    if j < TAPS - 1:
                        step(ins)
                    else:
                        step.reach(ins, s.last_tap, c + 1)

        @block.tensor
        def _(pe):
            for c in range(n_turned):
                pe.wait_ge(s.silued, c + 1)
                if c >= 2:
                    pe.wait_ge(s.kept, c - 1)
                src = b.sil[:, c % 2] if c < n_xs else raw[:, c]
                for t in range(TK):
                    at = X_AT - CTX_AT + t * P if t < TX else (t - TX) * P
                    mm = pe.transpose(flat[:, (c % 2) * 2 * BANK + t * P:(c % 2) * 2 * BANK + (t + 1) * P],
                                      src[:, at:at + P], k.ident[:])
                mm.then_inc(s.turned, 1)


def step_sizes(core, k, w, args):
    nc, psum = core.nc, core.psum
    n = 2 * SH
    with buffers(core, bias=[P, n], a_row=[P, n], a_neg=[P, n], t0=[P, TK, n], t1=[P, TK, n], left=[P, TK, n]) as b, \
            stage(core, "step_sizes", "loaded", "a_exped", "biased", "logs", "scaled", "summed", "differed",
                  "exped", "scalar_step", "vector_step") as (block, s):
        @block.sync
        def _(sync):
            sync.dma_start(b.bias[:], on_all(args.dt_bias_2.rearrange("o d h -> o (d h)"))).then_inc(s.loaded, 16)
            sync.dma_start(b.a_row[:], on_all(args.a_log_2.rearrange("o d h -> o (d h)"))).then_inc(s.loaded, 16)

        @block.scalar
        def _(act):
            step = Steps(act, s.scalar_step)
            act.wait_ge(s.loaded, 32)
            act.activation(b.a_neg[:], b.a_row[:], ACT.Exp).then_inc(s.a_exped, 1)
            act.wait_ge(s.biased, 1)
            step(act.activation(b.t1[:], b.t0[:], ACT.Abs))
            step(act.activation(b.t1[:], b.t1[:], ACT.Exp, scale=-1.0))
            act.activation(b.t1[:], b.t1[:], ACT.Ln, bias=k.one[:, 0:1]).then_inc(s.logs, 1)
            act.wait_ge(s.differed, 1)
            step(act.activation(w.to_end[:], b.left[:], ACT.Exp))
            step(act.activation(w.whole[:], w.total[:], ACT.Exp))
            act.activation(w.grown[:], w.running[:, 0:TX], ACT.Exp).then_inc(s.exped, 1)

        @block.tensor
        def _(pe):
            pe.wait_ge(s.scaled, 1)
            half = lambda bank, d: psum[:, bank, 0:TK * SH].rearrange("p (t h) -> p t h", t=TK)
            pe.matmul(half(0, 0), k.upto[:], w.a[:, :, 0:SH], start=True, stop=True)
            pe.matmul(half(1, 1), k.after[:], w.a[:, :, SH:n], start=True, stop=True)
            pe.matmul(psum[:, 2, 0:TK * n].rearrange("p (t h) -> p t h", t=TK), k.ones[:], w.a[:],
                      start=True, stop=True).then_inc(s.summed, 1)

        @block.vector
        def _(dve):
            step = Steps(dve, s.vector_step)
            dve.wait_ge(s.loaded, 32)
            dve.tensor_tensor(b.t0[:], w.raw_dt[:], spread(b.bias[:], 1, TK), ALU.add).then_inc(s.biased, 1)
            dve.wait_ge(s.logs, 1)
            step(dve.scalar_tensor_tensor(out=w.dt[:], in0=b.t0[:], scalar=0.0, in1=b.t1[:], op0=ALU.max, op1=ALU.add))
            dve.wait_ge(s.a_exped, 1)
            dve.scalar_tensor_tensor(out=w.a[:], in0=w.dt[:], scalar=-1.0, in1=spread(b.a_neg[:], 1, TK),
                                     op0=ALU.mult, op1=ALU.mult).then_inc(s.scaled, 1)
            dve.wait_ge(s.summed, 1)
            for d in range(2):
                step(dve.tensor_copy(w.running[:, :, d * SH:(d + 1) * SH],
                                     psum[:, d, 0:TK * SH].rearrange("p (t h) -> p t h", t=TK)))
            step(dve.tensor_copy(w.total[:], psum[:, 2, 0:TK * n].rearrange("p (t h) -> p t h", t=TK)))
            step(dve.tensor_scalar(w.fallen[:], w.running[:], -1.0, None, ALU.mult))
            dve.tensor_tensor(b.left[:], w.total[:], w.running[:], ALU.subtract).then_inc(s.differed, 1)
            dve.wait_ge(s.exped, 1)
            step(dve.tensor_tensor(w.to_end[:], w.to_end[:], w.dt[:], ALU.mult))


def carry_states(core, k, w, raw, xs, b_rows, y):
    nc, psum = core.nc, core.psum
    work = [(d, i, t) for d, tiles in enumerate(([4, 5, 0, 1, 2, 3], [5, 4, 3, 2, 1, 0])) for i, t in enumerate(tiles)]
    states = [(d, i, t) for d, i, t in work if i < TK - 1]
    gw = SR * SP_
    with buffers(core, weighted=[P, 2, DS], h=[P, SG, gw], read=[P, gw]) as b, \
            stage(core, "carry", "weighted", "state_summed", "read_summed", "read_out", "updated", "vector_step") \
            as (block, s):
        per_head = lambda v, t, d, g: spread(v[:, t, d * SH + g * SR:d * SH + (g + 1) * SR], 2, SP_)
        heads = lambda v: v.rearrange("p (r e) -> p r e", e=SP_)

        @block.gpsimd
        def _(pool):
            for n, (d, i, t) in enumerate(states):
                if n >= 2:
                    pool.wait_ge(s.state_summed, n - 1)
                pool.tensor_tensor(heads(b.weighted[:, n % 2]), heads(xs[:, t]),
                                   spread(w.to_end[:, t, d * SH:(d + 1) * SH], 2, SP_), ALU.mult)\
                    .then_inc(s.weighted, 1)

        @block.tensor
        def _(pe):
            n = reads = 0
            for d, i, t in work:
                if t < TX:
                    pe.wait_ge(s.updated, n)
                    pe.wait_ge(s.read_out, reads)
                    for g in range(SG):
                        mm = pe.matmul(psum[:, 4 + g, :], raw[:, DS // P + SG + g, X_AT - CTX_AT + t * P:
                                                              X_AT - CTX_AT + (t + 1) * P], b.h[:, g, :],
                                       start=True, stop=True)
                    mm.then_inc(s.read_summed, 1)
                    reads += 1
                if i < TK - 1:
                    pe.wait_ge(s.weighted, n + 1)
                    if n >= 2:
                        pe.wait_ge(s.updated, n - 1)
                    for g in range(SG):
                        mm = pe.matmul(psum[:, 2 * (n % 2) + g, :], b_rows[:, t, g], b.weighted[:, n % 2,
                                       g * gw:(g + 1) * gw], start=True, stop=True)
                    mm.then_inc(s.state_summed, 1)
                    n += 1

        @block.vector
        def _(dve):
            step = Steps(dve, s.vector_step)
            n = reads = 0
            for d, i, t in work:
                if t < TX:
                    reads += 1
                    dve.wait_ge(s.read_summed, reads)
                    for g in range(SG):
                        into = y[:, t, g * gw:(g + 1) * gw] if d == 0 else b.read[:]
                        step(dve.tensor_tensor(heads(into), heads(psum[:, 4 + g, :]), per_head(w.grown, t, d, g),
                                               ALU.mult))
                        if d == 1:
                            out = y[:, t, g * gw:(g + 1) * gw]
                            step(dve.tensor_tensor(out, out, b.read[:], ALU.add))
                    dve.sem_inc(s.read_out, 1)
                if i < TK - 1:
                    dve.wait_ge(s.state_summed, n + 1)
                    for g in range(SG):
                        bank = psum[:, 2 * (n % 2) + g, :]
                        if i == 0:
                            ins = dve.tensor_copy(b.h[:, g], bank)
                        else:
                            step(dve.tensor_tensor(heads(b.h[:, g]), heads(b.h[:, g]), per_head(w.whole, t, d, g),
                                                   ALU.mult))
                            ins = dve.tensor_tensor(b.h[:, g], b.h[:, g], bank, ALU.add)
                        if g < SG - 1:
                            step(ins)
                        else:
                            step.reach(ins, s.updated, n + 1)
                    n += 1


def within_chunks(core, k, w, raw, xs, y):
    nc, psum = core.nc, core.psum
    flat = psum[:, :, :].rearrange("p b n -> p (b n)")
    work = [(t, g, d) for t in range(TX) for g in range(SG) for d in range(2)]
    gw = SR * SP_
    with buffers(core, decay=[P, 2, SR * P], xdt=[P, 2, DS], cb=[P, P], never=[P, 2, P]) as b, \
            stage(core, "within", "xdt_made", "never_made", "cb_summed", "cb_kept", "spread_out", "exped", "joined",
                  "summed", "added", "vector_step") as (block, s):
        @block.gpsimd
        def _(pool):
            for t in range(TX):
                for d in range(2):
                    if t:
                        pool.wait_ge(s.summed, 4 * t)
                    pool.tensor_tensor(b.xdt[:, d].rearrange("p (h e) -> p h e", e=SP_),
                                       xs[:, t].rearrange("p (h e) -> p h e", e=SP_),
                                       spread(w.dt[:, t, d * SH:(d + 1) * SH], 2, SP_), ALU.mult)\
                        .then_inc(s.xdt_made, 1)

        @block.tensor
        def _(pe):
            pe.wait_ge(s.never_made, 2)

            def decays(n):
                t, g, d = work[n]
                at = X_AT - CTX_AT + t * P
                if d == 0:
                    pe.wait_ge(s.cb_kept, n // 2)
                    pe.matmul(psum[:, 6, 0:P], raw[:, DS // P + g, at:at + P],
                              raw[:, DS // P + SG + g, at:at + P], start=True, stop=True).then_inc(s.cb_summed, 1)
                if n >= 2:
                    pe.wait_ge(s.exped, n - 1)
                for r in range(SR):
                    c = d * SH + g * SR + r
                    out = flat[:, (n % 2) * 2 * BANK + r * P:(n % 2) * 2 * BANK + (r + 1) * P]
                    pe.matmul(out, w.a[:, t, c:c + 1].to_broadcast([P, P]), k.after[:] if d else k.upto[:],
                              start=True, stop=False)
                    mm = pe.matmul(out, k.ident[:], b.never[:, d], start=False, stop=True)
                mm.then_inc(s.spread_out, 1)

            decays(0)
            for n, (t, g, d) in enumerate(work):
                if n + 1 < len(work):
                    decays(n + 1)
                pe.wait_ge(s.joined, n + 1)
                pe.wait_ge(s.xdt_made, 2 * t + 2)
                if n >= 2:
                    pe.wait_ge(s.added, n - 1)
                for r in range(SR):
                    mm = pe.matmul(psum[:, 4 + n % 2, r * SP_:(r + 1) * SP_], b.decay[:, n % 2, r * P:(r + 1) * P],
                                   b.xdt[:, d, (g * SR + r) * SP_:(g * SR + r + 1) * SP_], start=True, stop=True)
                mm.then_inc(s.summed, 1)

        @block.scalar
        def _(act):
            for n, (t, g, d) in enumerate(work):
                act.wait_ge(s.spread_out, n + 1)
                if n >= 2:
                    act.wait_ge(s.summed, n - 1)
                for r in range(SR):
                    c = d * SH + g * SR + r
                    ins = act.activation(b.decay[:, n % 2, r * P:(r + 1) * P],
                                         flat[:, (n % 2) * 2 * BANK + r * P:(n % 2) * 2 * BANK + (r + 1) * P],
                                         ACT.Exp, bias=w.fallen[:, t, c:c + 1])
                ins.then_inc(s.exped, 1)

        @block.vector
        def _(dve):
            step = Steps(dve, s.vector_step)
            for d in range(2):
                dve.tensor_scalar(b.never[:, d], k.after[:] if d else k.upto[:], -1.0, 1e30, ALU.add, ALU.mult)\
                    .then_inc(s.never_made, 1)

            def add(n):
                t, g, _ = work[n]
                out = y[:, t, g * gw:(g + 1) * gw]
                dve.wait_ge(s.summed, n + 1)
                step.reach(dve.tensor_tensor(out, out, psum[:, 4 + n % 2, :], ALU.add), s.added, n + 1)

            for n, (t, g, d) in enumerate(work):
                if d == 0:
                    dve.wait_ge(s.cb_summed, n // 2 + 1)
                    step.reach(dve.tensor_copy(b.cb[:], psum[:, 6, 0:P]), s.cb_kept, n // 2 + 1)
                dve.wait_ge(s.exped, n + 1)
                v = b.decay[:, n % 2].rearrange("p (r q) -> p r q", q=P)
                step.reach(dve.tensor_tensor(v, v, spread(b.cb[:], 1, SR), ALU.mult), s.joined, n + 1)
                if n >= 1:
                    add(n - 1)
            add(len(work) - 1)


def state_output(core, k, xs, y, z, args):
    gw = DS // SG
    with buffers(core, skip=[P, SH], gain=[P, DS], skipped=[P, DS], junk=[P, gw], sums=[P, TX * SG],
                 roots=[P, TX * SG], rates=[P, TX * SG]) as b, \
            stage(core, "state_out", "loaded", "gated", "multiplied", "rooted", "scalar_step", "vector_step") \
            as (block, s):
        @block.sync
        def _(sync):
            sync.dma_start(b.skip[:], on_all(args.d_skip_2)).then_inc(s.loaded, 16)
            sync.dma_start(b.gain[:], on_all(args.ssd_norm_g_2)).then_inc(s.loaded, 16)

        @block.scalar
        def _(act):
            step = Steps(act, s.scalar_step)
            act.activation(z, z, ACT.Silu).then_inc(s.gated, 1)
            for t in range(TX):
                act.wait_ge(s.multiplied, t + 1)
                for g in range(SG):
                    step(act.activation(b.junk[:], y[:, t, g * gw:(g + 1) * gw], ACT.Square,
                                        accum_out=b.sums[:, t * SG + g:t * SG + g + 1]))
            act.activation(b.roots[:], b.sums[:], ACT.Sqrt, scale=1.0 / gw, bias=k.eps[:, 0:1]).then_inc(s.rooted, 1)

        @block.vector
        def _(dve):
            step = Steps(dve, s.vector_step)
            dve.wait_ge(s.loaded, 32)
            heads = lambda v: v.rearrange("p (h e) -> p h e", e=SP_)
            for t in range(TX):
                step(dve.tensor_tensor(heads(b.skipped[:]), heads(xs[:, t]), spread(b.skip[:], 2, SP_), ALU.mult))
                step(dve.tensor_tensor(y[:, t], y[:, t], b.skipped[:], ALU.add))
                dve.wait_ge(s.gated, 1)
                step.reach(dve.tensor_tensor(y[:, t], y[:, t], z[:, t], ALU.mult), s.multiplied, t + 1)
            dve.wait_ge(s.rooted, 1)
            step(dve.reciprocal(b.rates[:], b.roots[:]))
            for t in range(TX):
                for g in range(SG):
                    v = y[:, t, g * gw:(g + 1) * gw]
                    step(dve.scalar_tensor_tensor(out=v, in0=v, scalar=b.rates[:, t * SG + g:t * SG + g + 1],
                                                  in1=b.gain[:, g * gw:(g + 1) * gw], op0=ALU.mult, op1=ALU.mult))


def second_mixer(core, k, args):
    w_in = args.w_in_2[0].rearrange("(k p) n -> p k n", p=P)
    with buffers(core, z=[P, TX, DS], q=[P, TX, AH * AD], raw=[P, DXBC // P, WIDE], raw_dt=[P, TK, 2 * SH]) as m:
        with buffers(core, keys=[P, TK, AKV * AD], values=[P, TK, AKV * AD]) as a:
            with buffers(core, whole=[P, SK, TK * P], high=[P, SK, TK * P, F32R], low=[P, SK, TK * P, F32R]) as h:
                chunks, outs = [], []
                x = (h.whole, h.high, h.low)

                def rows(lo, hi, tiles, out):
                    chunks.append(token_chunk(w_in[:, :, lo:hi], x, tiles, len(outs)))
                    outs.extend((hi - lo, out(t)) for t in tiles)

                for i in range(2):
                    rows(i * BANK, (i + 1) * BANK, range(TX), lambda t: m.z[:, t, i * BANK:(i + 1) * BANK])
                for i in range(2):
                    rows(O_Q2 + i * BANK, O_Q2 + (i + 1) * BANK, range(TX),
                         lambda t: m.q[:, t, i * BANK:(i + 1) * BANK])
                for j in range(DXBC // BANK):
                    passes = []
                    for c in range(BANK // P):
                        ch = j * (BANK // P) + c
                        for lo, n, at in ((0, L, X_AT), (L, LC, CTX_AT)):
                            if lo and ch >= (DS + SG * SN) // P:
                                continue
                            passes.append(record(
                                group=len(outs), width=n, first=True, last=True,
                                operands=lambda x, w, kc, c=c, lo=lo, n=n: (w[:, kc, c * P:(c + 1) * P],
                                                                            x[:, kc, lo:lo + n])))
                            outs.append((n, m.raw[:, ch, at:at + n]))
                    chunks.append(record(
                        x=x, source=w_in[:, :, O_XBC + j * BANK:O_XBC + (j + 1) * BANK], passes=passes))
                rows(O_DT, O_K2, range(TK), lambda t: m.raw_dt[:, t])
                rows(O_K2, O_V2, range(TK), lambda t: a.keys[:, t])
                rows(O_V2, DIN2, range(TK), lambda t: a.values[:, t])
                with buffers(core, ctx=[P, TC, D]) as b:
                    with stage(core, "load_ctx2", "loaded", "padded") as (block, s):
                        @block.sync
                        def _(sync):
                            sync.dma_start(b.ctx[:], args.ctx_2[0].rearrange("(t p) d -> p t d", p=P))\
                                .then_inc(s.loaded, 16)
                            sync.wait_ge(s.loaded, 16)

                        @block.gpsimd
                        def _(pool):
                            pool.memset(m.raw[:, :, 0:CTX_AT], 0.0).then_inc(s.padded, 1)
                            pool.memset(m.raw[:, :, CTX_AT + LC:X_AT], 0.0).then_inc(s.padded, 1)
                            pool.memset(m.raw[:, :, X_AT + L:WIDE], 0.0).then_inc(s.padded, 1)
                            pool.memset(m.raw[:, (DS + SG * SN) // P:, CTX_AT:CTX_AT + LC], 0.0)\
                                .then_inc(s.padded, 1)
                            pool.wait_ge(s.padded, 4)
                    to_features(core, k, "turn2", [
                        ([lambda i, t=t: k.x[:, t, i * P:(i + 1) * P] for t in range(TX)], DC,
                         lambda i: features(h, i, 0, L), lambda i: k.scale2[:, i:i + 1],
                         lambda i: k.cols2[:, i, 0:1]),
                        ([lambda i, t=t: b.ctx[:, t, i * P:(i + 1) * P] for t in range(TC)], DC,
                         lambda i: features(h, i, L, L + LC), lambda i: k.scale2c[:, i:i + 1],
                         lambda i: k.cols2[:, i, 1:2])], prefetch=load_first(core, chunks))
                project(core, k, "in2", chunks,
                        lambda e, s, g, bank, step: copy_out(e, outs[g][1], bank[:, 0:outs[g][0]]))
            with buffers(core, cos=[P, TX, AD], sin=[P, TX, AD], gq=[P, AD], gk=[P, AD]) as b:
                table = [(b.cos[:, t], b.sin[:, t]) for t in range(TX)] + [None] * TC
                view = lambda x, t: x[:, t].rearrange("p (h w) -> p h w", w=AD)
                head_norms(core, k, "heads2",
                           [(view(m.q, t), b.gq[:], table[t]) for t in range(TX)] +
                           [(view(a.keys, t), b.gk[:], table[t]) for t in range(TK)],
                           AD, (0, AD, pair_halves),
                           [(b.cos[:], args.cos_gqa.rearrange("(t p) w -> p t w", p=P)),
                            (b.sin[:], args.sin_gqa.rearrange("(t p) w -> p t w", p=P)),
                            (b.gq[:], on_all(args.q_norm_g_2)), (b.gk[:], on_all(args.k_norm_g_2))])
            attention(core, k, "attn2", m.q[:], AKV, AH // AKV, AD, a.keys[:],
                      lambda g: a.values[:, :, ds(g * AD, AD)], lambda h: m.q[:, :, ds(h * AD, AD)], AD)
        y = m.raw[:].rearrange("p c n -> p (c n)")[:, 0:TX * DS].rearrange("p (t n) -> p t n", t=TX)
        with buffers(core, xs=[P, TK, DS]) as c:
            n = 2 * SH
            with buffers(core, a=[P, TK, n], dt=[P, TK, n], running=[P, TK, n], fallen=[P, TK, n], total=[P, TK, n],
                         to_end=[P, TK, n], whole=[P, TK, n], grown=[P, TX, n],
                         others={"raw_dt": m.raw_dt}) as w:
                with buffers(core, b_rows=[P, TK, SG, SN]) as e:
                    convolve(core, k, m.raw[:], c.xs[:], e.b_rows[:], args.conv_w_2, args.conv_b_2)
                    step_sizes(core, k, w, args)
                    carry_states(core, k, w, m.raw[:], c.xs[:], e.b_rows[:], y)
                within_chunks(core, k, w, m.raw[:], c.xs[:], y)
            state_output(core, k, c.xs[:], y, m.z[:], args)
        project_out(core, k, "out2", lambda t, i: y[:, t, i * P:(i + 1) * P] if i < DS // P else
                    m.q[:, t, i * P - DS:(i + 1) * P - DS], MIX2, args.w_out_2[0], k.rows2, ALPHA2)
    layer_norm(core, k, "ln1", args.ln1_g_2, args.ln1_b_2)


def build(nc, **tensors):
    args = record(**tensors)
    with ExitStack() as stack:
        core = core_state(nc, stack)
        others = {
            "args": args,
            "slot_rows": nc.dram_tensor("slot_rows", [max(most_blocks(L, K1, E1), most_blocks(L, K2, E2)) * P, D],
                                        F32).ap(),
            "slots_cleared": stack.enter_context(nc.semaphore("slots_cleared")),
            "rows1": nc.dram_tensor("rows1", [2, 6 * D], F32).ap(),
            "rows2": nc.dram_tensor("rows2", [2, 6 * D], F32).ap(),
        }
        k = stack.enter_context(buffers(
            core, others=others, x=[P, TX, D], ident=[P, P], ones=[P, P], upto=[P, P], after=[P, P], before=[P, P],
            zeros=[P, D // 4], eps=[P, 1], one=[P, 1], numbers=[P, 64], cols1=[P, 6 * DC, 2], cols2=[P, 6 * DC, 2],
            scale1=[P, DC], scale1c=[P, DC], scale1f=[P, DC], scale2=[P, DC], scale2c=[P, DC], scale2f=[P, DC]))
        setup(core, k, args)
        modulation(core, k, "mod1", args.c, args.c_ctx, args.w_ada[0], args.b_ada[0], k.cols1, k.rows1,
                   following=args.w_mod_2[0])
        modulation(core, k, "mod2", args.c_2, args.c_ctx_2, args.w_mod_2[0], args.b_mod_2[0], k.cols2, k.rows2)
        part = lambda cols, i, which: cols[:, i * DC:(i + 1) * DC, which]
        scale_columns(core, k, "scales", [
            (k.scale1[:], args.g_attn[0], part(k.cols1, 1, 0)), (k.scale1c[:], args.g_attn[0], part(k.cols1, 1, 1)),
            (k.scale1f[:], args.g_ffn[0], part(k.cols1, 4, 0)), (k.scale2[:], None, part(k.cols2, 1, 0)),
            (k.scale2c[:], None, part(k.cols2, 1, 1)), (k.scale2f[:], None, part(k.cols2, 4, 0))])
        first_mixer(core, k, args)
        first_experts(core, k, args)
        second_mixer(core, k, args)
        second_experts(core, k, args)
        finish(core, k, args)


def finish(core, k, args):
    with stage(core, "store", "stored") as (block, s):
        @block.sync
        def _(sync):
            sync.dma_start(args.out[0].rearrange("(t p) d -> p t d", p=P), k.x[:]).then_inc(s.stored, 16)
            sync.wait_ge(s.stored, 16)


def rotary_tables(width, paired):
    n = width // 4
    inv = np.power(np.float32(10000.0), -np.arange(n, dtype=np.float32) / np.float32(n)).astype(np.float32)
    at = np.arange(L)
    row = (at // GRID_W).astype(np.float32)[:, None] * inv
    col = (at % GRID_W).astype(np.float32)[:, None] * inv
    if paired:
        angle = np.repeat(np.concatenate([row, col], -1), 2, axis=-1)
        sign = np.tile(np.array([-1.0, 1.0]), width // 2)
    else:
        angle = np.concatenate([row, row, col, col], -1)
        sign = np.tile(np.repeat(np.array([-1.0, 1.0]), n), 2)
    return np.cos(angle).astype(np.float32), (np.sin(angle) * sign).astype(np.float32)


INPUTS = """x c ctx c_ctx g_attn g_ffn w_ada b_ada w_in g_q_lora w_q_up g_q_head g_kv_lora w_kv_up g_k_head
ret_decay_logit g_ret_out w_out w_router b_router w_mlp1 b_mlp1 w_mlp2 b_mlp2 c_2 ctx_2 c_ctx_2 w_mod_2 b_mod_2 w_in_2
conv_w_2 conv_b_2 dt_bias_2 a_log_2 d_skip_2 ssd_norm_g_2 q_norm_g_2 k_norm_g_2 w_out_2 ln1_g_2 ln1_b_2 w_rg_2 b_rg_2
w_re_2 b_re_2 w_gate_2 w_up_2 w_down_2 ln2_g_2 ln2_b_2""".split()


def kernel(**inputs):
    import concourse.bacc as bacc
    from concourse.bass_utils import run_bass_kernel_spmd

    nc = bacc.Bacc("TRN2", target_bir_lowering=False, num_devices=1)
    arrays = {name: np.ascontiguousarray(inputs[name]) for name in INPUTS}
    for name, width, paired in (("mla", ROPE, False), ("ret", RDK, False), ("gqa", AD, True)):
        arrays["cos_" + name], arrays["sin_" + name] = rotary_tables(width, paired)
    tensors = {name: nc.dram_tensor("in_" + name, a.shape, mybir.dt.from_np(a.dtype), kind="ExternalInput").ap()
               for name, a in arrays.items()}
    out = nc.dram_tensor("out_x", (1, L, D), F32, kind="ExternalOutput").ap()
    build(nc, out=out, **tensors)
    result = run_bass_kernel_spmd(nc, [{"in_" + name: a for name, a in arrays.items()}], core_ids=[0])
    return result.results[0]["out_x"]
```
